# Optimizing a Trainium2 kernel written in Bass

```python
import math
import jax, jax.numpy as jnp
from jax import lax
import numpy as np

D_MODEL = 1024
BATCH = 1
SEQ = 512
DEPTH = 2

HEAD_DIM = 64
N_HEADS = D_MODEL // HEAD_DIM
D_FF = 4 * D_MODEL
DECAY_LORA = 64
AAA_LORA = 64
GATE_LORA = 160
N_SHIFT_MIX = 6
BLOCK_Q = 128
N_A_LAYERS = DEPTH // 2
N_B_LAYERS = DEPTH - N_A_LAYERS
NORM_EPS = 1e-6
GN_EPS = 64e-5


def rmsnorm(x, g, eps=NORM_EPS):
    xf = x.astype(jnp.float32)
    y = xf * lax.rsqrt(jnp.mean(xf * xf, axis=-1, keepdims=True) + eps)
    return (y * g.astype(jnp.float32)).astype(x.dtype)

def to_heads(t):
    b, s, _ = t.shape
    return t.reshape(b, s, N_HEADS, HEAD_DIM)

def rwkv7_time_mix(h, mu, w_rkv, w0, w1, w2, a0, a1, a2, g1, g2,
                   k_k, k_a, r_k, lnx_w, lnx_b, w_o):
    B, T, D = h.shape
    f32 = jnp.float32
    x_prev = jnp.pad(h[:, :-1], ((0, 0), (1, 0), (0, 0)))
    xx = x_prev - h
    xs = h[None] + xx[None] * mu[:, None, None, :]
    x_r, x_w, x_k, x_v, x_a, x_g = xs[0], xs[1], xs[2], xs[3], xs[4], xs[5]
    rkv = jnp.einsum('pbtd,pde->pbte', jnp.stack([x_r, x_k, x_v]), w_rkv)
    r, k, v = rkv[0], rkv[1], rkv[2]
    w = -jax.nn.softplus(-(w0 + jnp.tanh(x_w @ w1) @ w2)) - 0.5
    decay = jnp.exp(-jnp.exp(w.astype(f32)))
    a = jax.nn.sigmoid(a0 + (x_a @ a1) @ a2)
    g = jax.nn.sigmoid(x_g @ g1) @ g2
    kk = to_heads((k * k_k).astype(f32))
    kk = kk / jnp.maximum(jnp.linalg.norm(kk, axis=-1, keepdims=True), 1e-12)
    k = k * (1.0 + (a - 1.0) * k_a)

    r_h = to_heads(r).astype(f32)
    k_h = to_heads(k).astype(f32)
    v_h = to_heads(v).astype(f32)
    a_h = to_heads(a).astype(f32)
    w_h = to_heads(decay)
    b_h = kk * a_h

    def step(S, inp):
        r_t, w_t, k_t, v_t, kk_t, b_t = inp
        sa = jnp.einsum('bhvk,bhk->bhv', S, -kk_t)
        S = (S * w_t[:, :, None, :] + sa[..., None] * b_t[:, :, None, :]
             + v_t[..., None] * k_t[:, :, None, :])
        y_t = jnp.einsum('bhvk,bhk->bhv', S, r_t)
        return S, y_t

    tm = lambda t: jnp.moveaxis(t, 1, 0)
    S0 = jnp.zeros((B, N_HEADS, HEAD_DIM, HEAD_DIM), f32)
    _, y = lax.scan(step, S0, (tm(r_h), tm(w_h), tm(k_h), tm(v_h), tm(kk), tm(b_h)))
    y = jnp.moveaxis(y, 0, 1)

    mean = jnp.mean(y, axis=-1, keepdims=True)
    var = jnp.mean(jnp.square(y - mean), axis=-1, keepdims=True)
    y = (y - mean) * lax.rsqrt(var + GN_EPS)
    y = y.reshape(B, T, D) * lnx_w.astype(f32) + lnx_b.astype(f32)
    bonus = jnp.sum(r_h * k_h * r_k.astype(f32), axis=-1, keepdims=True) * v_h
    y = (y + bonus.reshape(B, T, D)).astype(h.dtype) * g
    return y @ w_o

def shared_kv(x, kv_norm_g, kv_w, kv_f_bias, k_norm_g):
    D = x.shape[-1]
    h = rmsnorm(x, kv_norm_g)
    proj = h @ kv_w
    k = to_heads(proj[..., :D])
    v = to_heads(proj[..., D:2 * D])
    f_logit = (proj[..., 2 * D:] + kv_f_bias).astype(jnp.float32)
    k = rmsnorm(k, k_norm_g)
    log_f = jax.nn.log_sigmoid(f_logit)
    c = jnp.cumsum(jnp.transpose(log_f, (0, 2, 1)), axis=-1)
    return jnp.transpose(k, (0, 2, 1, 3)), jnp.transpose(v, (0, 2, 1, 3)), c

def forgetting_attention(q, k, v, c):
    T = q.shape[2]
    scale = 1.0 / math.sqrt(HEAD_DIM)
    outs = []
    for s in range(0, T, BLOCK_Q):
        e = s + BLOCK_Q
        logits = jnp.einsum('bhqd,bhkd->bhqk', q[:, :, s:e], k[:, :, :e]).astype(jnp.float32) * scale
        logits = logits + (c[:, :, s:e, None] - c[:, :, None, :e])
        causal = jnp.arange(s, e)[:, None] >= jnp.arange(e)[None, :]
        logits = jnp.where(causal, logits, -jnp.inf)
        p = jax.nn.softmax(logits, axis=-1).astype(v.dtype)
        outs.append(jnp.einsum('bhqk,bhkd->bhqd', p, v[:, :, :e]))
    return jnp.concatenate(outs, axis=2)

def fox_layer(h, w_q, q_norm_g, w_o, k_sh, v_sh, c_sh):
    B, T, D = h.shape
    q = rmsnorm(to_heads(h @ w_q), q_norm_g)
    q = jnp.transpose(q, (0, 2, 1, 3))
    o = forgetting_attention(q, k_sh, v_sh, c_sh)
    o = jnp.transpose(o, (0, 2, 1, 3)).reshape(B, T, D)
    return o @ w_o

def sq_relu_mlp(h, w_in, w_out):
    return jnp.square(jax.nn.relu(h @ w_in)) @ w_out

def first_inputs(seed: int = 0) -> dict:
    key = jax.random.key(seed)
    ks = iter(jax.random.split(key, 40))
    D, H, N, F = D_MODEL, N_HEADS, HEAD_DIM, D_FF
    nA, nB = N_A_LAYERS, N_B_LAYERS
    nrm = lambda shape, s: s * jax.random.normal(next(ks), shape, jnp.float32)
    gain = lambda shape: 1.0 + nrm(shape, 0.05)
    decay_base = jnp.linspace(-6.5, -1.5, D, dtype=jnp.float32)
    inp = {}
    inp["x"] = jax.random.normal(next(ks), (BATCH, SEQ, D), jnp.float32)
    inp["rwkv_norm_g"] = gain((nA, D))
    inp["rwkv_mu"] = jax.random.uniform(next(ks), (nA, N_SHIFT_MIX, D), jnp.float32)
    inp["rwkv_w_rkv"] = nrm((nA, 3, D, D), D ** -0.5)
    inp["rwkv_w0"] = decay_base[None] + nrm((nA, D), 0.1)
    inp["rwkv_w1"] = nrm((nA, D, DECAY_LORA), D ** -0.5)
    inp["rwkv_w2"] = nrm((nA, DECAY_LORA, D), 0.1 * DECAY_LORA ** -0.5)
    inp["rwkv_a0"] = nrm((nA, D), 0.1)
    inp["rwkv_a1"] = nrm((nA, D, AAA_LORA), D ** -0.5)
    inp["rwkv_a2"] = nrm((nA, AAA_LORA, D), 0.1 * AAA_LORA ** -0.5)
    inp["rwkv_g1"] = nrm((nA, D, GATE_LORA), D ** -0.5)
    inp["rwkv_g2"] = nrm((nA, GATE_LORA, D), GATE_LORA ** -0.5)
    inp["rwkv_k_k"] = 0.85 + nrm((nA, D), 0.05)
    inp["rwkv_k_a"] = 1.0 + nrm((nA, D), 0.05)
    inp["rwkv_r_k"] = nrm((nA, H, N), 0.1)
    inp["rwkv_lnx_w"] = gain((nA, D))
    inp["rwkv_lnx_b"] = nrm((nA, D), 0.02)
    inp["rwkv_w_o"] = nrm((nA, D, D), 0.5 * D ** -0.5)
    inp["kv_norm_g"] = gain((D,))
    inp["kv_w"] = nrm((D, 2 * D + H), D ** -0.5)
    inp["kv_f_bias"] = jax.random.uniform(next(ks), (H,), jnp.float32, 0.5, 3.0)
    inp["k_norm_g"] = gain((H, N))
    inp["attn_norm_g"] = gain((nB, D))
    inp["attn_w_q"] = nrm((nB, D, D), D ** -0.5)
    inp["q_norm_g"] = gain((nB, H, N))
    inp["attn_w_o"] = nrm((nB, D, D), 0.5 * D ** -0.5)
    inp["mlp_norm_g"] = gain((DEPTH, D))
    inp["mlp_w_in"] = nrm((DEPTH, D, F), D ** -0.5)
    inp["mlp_w_out"] = nrm((DEPTH, F, D), 0.5 * F ** -0.5)
    return inp

def first_block(x, rwkv_norm_g, rwkv_mu, rwkv_w_rkv, rwkv_w0, rwkv_w1, rwkv_w2,
              rwkv_a0, rwkv_a1, rwkv_a2, rwkv_g1, rwkv_g2, rwkv_k_k, rwkv_k_a,
              rwkv_r_k, rwkv_lnx_w, rwkv_lnx_b, rwkv_w_o,
              kv_norm_g, kv_w, kv_f_bias, k_norm_g,
              attn_norm_g, attn_w_q, q_norm_g, attn_w_o,
              mlp_norm_g, mlp_w_in, mlp_w_out):
    k_sh = v_sh = c_sh = None
    for layer in range(DEPTH):
        if layer < N_A_LAYERS:
            i = layer
            h = rmsnorm(x, rwkv_norm_g[i])
            x = x + rwkv7_time_mix(h, rwkv_mu[i], rwkv_w_rkv[i], rwkv_w0[i], rwkv_w1[i],
                                   rwkv_w2[i], rwkv_a0[i], rwkv_a1[i], rwkv_a2[i],
                                   rwkv_g1[i], rwkv_g2[i], rwkv_k_k[i], rwkv_k_a[i],
                                   rwkv_r_k[i], rwkv_lnx_w[i], rwkv_lnx_b[i], rwkv_w_o[i])
        else:
            j = layer - N_A_LAYERS
            h = rmsnorm(x, attn_norm_g[j])
            x = x + fox_layer(h, attn_w_q[j], q_norm_g[j], attn_w_o[j], k_sh, v_sh, c_sh)
        x = x + sq_relu_mlp(rmsnorm(x, mlp_norm_g[layer]), mlp_w_in[layer], mlp_w_out[layer])
        if layer == N_A_LAYERS - 1:
            k_sh, v_sh, c_sh = shared_kv(x, kv_norm_g, kv_w, kv_f_bias, k_norm_g)
    return x


DEPTH_2 = 1

M_HEADS = 4
M_HEAD_DIM = 128
M_WIDTH = M_HEADS * M_HEAD_DIM
M_CHUNK = 128
CONV_WIDTH = 4
N_HEADS_2 = 8
N_KV_GROUPS = 2
N_REP = N_HEADS_2 // N_KV_GROUPS
N_HEAD_DIM = 64
N_WIDTH = N_HEADS_2 * N_HEAD_DIM
N_KV_WIDTH = N_KV_GROUPS * N_HEAD_DIM
CMP_BLOCK = 32
CMP_STRIDE = 16
CMP_HIDDEN = 2 * N_HEAD_DIM
SEL_BLOCK = 64
SEL_TOPK = 16
WINDOW = 512
NSA_Q_BLOCK = 64
REL_BUCKETS = 32
REL_MAX_DIST = 1024
N_BRANCH = 2
BRANCH_WIDTH = 512
D_FF_2 = -(-8 * D_MODEL // (3 * 256)) * 256
RMS_EPS = 1e-6
BIG = 1e9

IN_SIZES = (M_WIDTH, M_WIDTH, M_WIDTH, M_WIDTH, M_HEADS, M_HEADS,
            N_WIDTH, 6 * N_KV_WIDTH, 3 * N_HEADS_2, N_BRANCH * D_MODEL)
D_IN_TOTAL = sum(IN_SIZES)


def rms_norm(x, g):
    x32 = x.astype(jnp.float32)
    y = x32 * lax.rsqrt(jnp.mean(x32 * x32, axis=-1, keepdims=True) + RMS_EPS)
    return (y * g.astype(jnp.float32)).astype(x.dtype)

def split_columns(p, sizes):
    out = []
    start = 0
    for s in sizes:
        out.append(p[..., start:start + s])
        start += s
    return out

def causal_depthwise_conv(x, w):
    T = x.shape[1]
    xp = jnp.pad(x, ((0, 0), (CONV_WIDTH - 1, 0), (0, 0)))
    return sum(w[j] * xp[:, j:j + T] for j in range(CONV_WIDTH))

def rel_bucket(dist):
    n = jnp.maximum(dist, 0)
    max_exact = REL_BUCKETS // 2
    nf = jnp.maximum(n, 1).astype(jnp.float32)
    large = max_exact + (jnp.log(nf / max_exact) / math.log(REL_MAX_DIST / max_exact)
                         * (REL_BUCKETS - max_exact)).astype(jnp.int32)
    large = jnp.minimum(large, REL_BUCKETS - 1)
    return jnp.where(n < max_exact, n, large)

def masked_softmax(logits, mask):
    logits = logits.astype(jnp.float32)
    z = jnp.where(mask, logits, -1e30)
    z = z - jnp.max(z, axis=-1, keepdims=True)
    e = jnp.where(mask, jnp.exp(z), 0.0)
    return e / jnp.maximum(jnp.sum(e, axis=-1, keepdims=True), 1e-30)

def mlstm_chunkwise(q, k, v, i_pre, f_pre):
    B, H, T, dk = q.shape
    dv = v.shape[-1]
    L = M_CHUNK
    nc = T // L
    qc = q.reshape(B, H, nc, L, dk)
    kc = k.reshape(B, H, nc, L, dk)
    vc = v.reshape(B, H, nc, L, dv)
    ic = i_pre.reshape(B, H, nc, L)
    bc = jnp.cumsum(jax.nn.log_sigmoid(f_pre).reshape(B, H, nc, L), axis=-1)
    b_last = bc[..., -1]
    a = b_last[..., None] - bc + ic

    def step(carry, inp):
        C, n, m = carry
        k_j, v_j, a_j, bl = inp
        m_new = jnp.maximum(bl + m, jnp.max(a_j, axis=-1))
        decay = jnp.exp(bl + m - m_new)
        w = jnp.exp(a_j - m_new[..., None])
        C_new = decay[..., None, None] * C + jnp.einsum('bhl,bhlk,bhlv->bhkv', w, k_j, v_j)
        n_new = decay[..., None] * n + jnp.einsum('bhl,bhlk->bhk', w, k_j)
        return (C_new, n_new, m_new), (C, n, m)

    init = (jnp.zeros((B, H, dk, dv), jnp.float32), jnp.zeros((B, H, dk), jnp.float32),
            jnp.zeros((B, H), jnp.float32))
    xs = (jnp.moveaxis(kc, 2, 0), jnp.moveaxis(vc, 2, 0), jnp.moveaxis(a, 2, 0), jnp.moveaxis(b_last, 2, 0))
    _, (C_prev, n_prev, m_prev) = lax.scan(step, init, xs)
    C_prev = jnp.moveaxis(C_prev, 0, 2)
    n_prev = jnp.moveaxis(n_prev, 0, 2)
    m_prev = jnp.moveaxis(m_prev, 0, 2)

    causal = jnp.tril(jnp.ones((L, L), dtype=bool))
    log_d = jnp.where(causal, bc[..., :, None] - bc[..., None, :] + ic[..., None, :], -jnp.inf)
    log_inter = bc + m_prev[..., None]
    m_i = jnp.maximum(jnp.max(log_d, axis=-1), log_inter)
    P = jnp.exp(log_d - m_i[..., None]) * jnp.einsum('bhcid,bhcjd->bhcij', qc, kc)
    s_inter = jnp.exp(log_inter - m_i)
    num = (jnp.einsum('bhcij,bhcjv->bhciv', P, vc)
           + s_inter[..., None] * jnp.einsum('bhcid,bhcdv->bhciv', qc, C_prev))
    den = jnp.sum(P, axis=-1) + s_inter * jnp.einsum('bhcid,bhcd->bhci', qc, n_prev)
    h = num / jnp.maximum(jnp.abs(den), jnp.exp(-m_i))[..., None]
    return h.reshape(B, H, T, dv)

def mlstm_mixer(q_pre, k_pre, v, o_pre, i_pre, f_pre, b_fgate, conv_w, g_head):
    B, T, _ = q_pre.shape
    qk = jax.nn.silu(causal_depthwise_conv(jnp.concatenate([q_pre, k_pre], axis=-1), conv_w))
    to_heads = lambda t: t.reshape(B, T, M_HEADS, M_HEAD_DIM).transpose(0, 2, 1, 3).astype(jnp.float32)
    q = to_heads(qk[..., :M_WIDTH])
    k = to_heads(qk[..., M_WIDTH:]) * (M_HEAD_DIM ** -0.5)
    vh = to_heads(v)
    ig = i_pre.astype(jnp.float32).transpose(0, 2, 1)
    fg = (f_pre.astype(jnp.float32) + b_fgate.astype(jnp.float32)).transpose(0, 2, 1)
    hh = mlstm_chunkwise(q, k, vh, ig, fg)
    hh = (hh * lax.rsqrt(jnp.mean(hh * hh, axis=-1, keepdims=True) + RMS_EPS)
          * g_head.astype(jnp.float32).reshape(M_HEADS, 1, M_HEAD_DIM))
    hh = hh.transpose(0, 2, 1, 3).reshape(B, T, M_WIDTH)
    return (jax.nn.sigmoid(o_pre.astype(jnp.float32)) * hh).astype(q_pre.dtype)

def nsa_mixer(q_in, kv_in, gate_in, pe_cmp, w_cmp1, w_cmp2, rel_bias):
    B, T, _ = q_in.shape
    G, R, dh, Q = N_KV_GROUPS, N_REP, N_HEAD_DIM, NSA_Q_BLOCK
    q = q_in.reshape(B, T, G, R, dh).transpose(0, 2, 3, 1, 4) * (dh ** -0.5)
    kv = kv_in.reshape(B, T, 6, G, dh).transpose(2, 0, 3, 1, 4)
    k_c, v_c, k_s, v_s, k_w, v_w = kv[0], kv[1], kv[2], kv[3], kv[4], kv[5]
    gates = jax.nn.sigmoid(gate_in.astype(jnp.float32).reshape(B, T, G, R, 3).transpose(0, 2, 3, 1, 4))

    n_cmp = (T - CMP_BLOCK) // CMP_STRIDE + 1
    cmp_start = jnp.arange(n_cmp) * CMP_STRIDE
    cmp_idx = cmp_start[:, None] + jnp.arange(CMP_BLOCK)[None, :]
    cmp_end = cmp_start + CMP_BLOCK - 1

    def compress(kx, j):
        blk = kx[:, :, cmp_idx] + pe_cmp[j]
        flat = blk.reshape(B, G, n_cmp, CMP_BLOCK * dh)
        return jax.nn.silu(flat @ w_cmp1[j]) @ w_cmp2[j]

    kc_ = compress(k_c, 0)
    vc_ = compress(v_c, 1)

    n_slc = T // SEL_BLOCK
    n_top = min(SEL_TOPK, n_slc)
    k_sb = k_s.reshape(B, G, n_slc, SEL_BLOCK, dh)
    v_sb = v_s.reshape(B, G, n_slc, SEL_BLOCK, dh)
    slc_start = jnp.arange(n_slc) * SEL_BLOCK
    overlap = (jnp.clip(jnp.minimum(cmp_start[:, None] + CMP_BLOCK, slc_start[None, :] + SEL_BLOCK)
                        - jnp.maximum(cmp_start[:, None], slc_start[None, :]), 0)
               / CMP_STRIDE).astype(jnp.float32)

    k_wp = jnp.pad(k_w, ((0, 0), (0, 0), (WINDOW, 0), (0, 0)))
    v_wp = jnp.pad(v_w, ((0, 0), (0, 0), (WINDOW, 0), (0, 0)))

    table = rel_bias.astype(jnp.float32).T.reshape(G, R, REL_BUCKETS)
    g_ix = jnp.arange(G)[None, :, None, None, None]
    r_ix = jnp.arange(R)[None, None, :, None, None]
    gather_blocks = jax.vmap(jax.vmap(lambda blk, ix: blk[ix]))

    def block(i):
        qs = i * Q
        t = qs + jnp.arange(Q)
        qb = lax.dynamic_slice_in_dim(q, qs, Q, axis=3)
        lc = (jnp.einsum('bgrqd,bgcd->bgrqc', qb, kc_).astype(jnp.float32)
              + table[:, :, rel_bucket(t[:, None] - cmp_end[None, :])])
        p_c = masked_softmax(lc, cmp_end[None, :] <= t[:, None])
        o_c = jnp.einsum('bgrqc,bgcd->bgrqd', p_c, vc_.astype(jnp.float32))
        imp = jnp.einsum('bgrqc,cj->bgqj', p_c, overlap)
        cur = t // SEL_BLOCK
        jb = jnp.arange(n_slc)[None, :]
        forced = (jb == 0) | (jb == cur[:, None]) | (jb == cur[:, None] - 1)
        eligible = jb * SEL_BLOCK <= t[:, None]
        score = jnp.where(eligible, jnp.where(forced, BIG, imp), -BIG)
        top_val, top_idx = lax.top_k(score, n_top)
        N = n_top * SEL_BLOCK
        k_g = gather_blocks(k_sb, top_idx).reshape(B, G, Q, N, dh)
        v_g = gather_blocks(v_sb, top_idx).reshape(B, G, Q, N, dh)
        pos_u = top_idx[..., None] * SEL_BLOCK + jnp.arange(SEL_BLOCK)
        mask_u = (top_val > -BIG / 2)[..., None] & (pos_u <= t[:, None, None])
        pos = pos_u.reshape(B, G, Q, N)
        mask_s = mask_u.reshape(B, G, Q, N)
        bias_s = table[g_ix, r_ix, rel_bucket(t[:, None] - pos)[:, :, None]]
        ls = jnp.einsum('bgrqd,bgqnd->bgrqn', qb, k_g).astype(jnp.float32) + bias_s
        p_s = masked_softmax(ls, mask_s[:, :, None])
        o_s = jnp.einsum('bgrqn,bgqnd->bgrqd', p_s, v_g.astype(jnp.float32))
        span = Q + WINDOW
        k_wb = lax.dynamic_slice_in_dim(k_wp, qs, span, axis=2)
        v_wb = lax.dynamic_slice_in_dim(v_wp, qs, span, axis=2)
        pos_w = qs - WINDOW + jnp.arange(span)
        dist = t[:, None] - pos_w[None, :]
        mask_w = (pos_w[None, :] >= 0) & (dist >= 0) & (dist < WINDOW)
        lw = jnp.einsum('bgrqd,bgkd->bgrqk', qb, k_wb).astype(jnp.float32) + table[:, :, rel_bucket(dist)]
        p_w = masked_softmax(lw, mask_w)
        o_w = jnp.einsum('bgrqk,bgkd->bgrqd', p_w, v_wb.astype(jnp.float32))
        gb = lax.dynamic_slice_in_dim(gates, qs, Q, axis=3)
        return gb[..., 0:1] * o_c + gb[..., 1:2] * o_s + gb[..., 2:3] * o_w

    out = lax.map(block, jnp.arange(T // Q))
    out = out.transpose(1, 0, 4, 2, 3, 5).reshape(B, T, N_WIDTH)
    return out.astype(q_in.dtype)

def second_inputs(seed: int = 0) -> dict:
    key = jax.random.key(seed)
    ks = jax.random.split(key, 20)
    nrm = lambda k, shape, scale: jax.random.normal(k, shape, jnp.float32) * scale
    x = nrm(ks[0], (BATCH, SEQ, D_MODEL), 1.0)
    g_norm_mix = 1.0 + nrm(ks[1], (DEPTH_2, D_MODEL), 0.02)
    w_in = nrm(ks[2], (DEPTH_2, D_MODEL, D_IN_TOTAL), D_MODEL ** -0.5)
    b_in = nrm(ks[3], (DEPTH_2, D_IN_TOTAL), 0.02)
    b_fgate = jnp.linspace(3.0, 6.0, M_HEADS, dtype=jnp.float32)[None, :] + nrm(ks[4], (DEPTH_2, M_HEADS), 0.1)
    conv_qk = nrm(ks[5], (DEPTH_2, CONV_WIDTH, 2 * M_WIDTH), CONV_WIDTH ** -0.5)
    g_mlstm_head = 1.0 + nrm(ks[6], (DEPTH_2, M_WIDTH), 0.02)
    pe_cmp = nrm(ks[7], (DEPTH_2, 2, CMP_BLOCK, N_HEAD_DIM), 0.1)
    w_cmp1 = nrm(ks[8], (DEPTH_2, 2, CMP_BLOCK * N_HEAD_DIM, CMP_HIDDEN), (CMP_BLOCK * N_HEAD_DIM) ** -0.5)
    w_cmp2 = nrm(ks[9], (DEPTH_2, 2, CMP_HIDDEN, N_HEAD_DIM), CMP_HIDDEN ** -0.5)
    rel_bias = nrm(ks[10], (REL_BUCKETS, N_HEADS_2), 0.5)
    w_branch = nrm(ks[11], (DEPTH_2, N_BRANCH, BRANCH_WIDTH, D_MODEL), BRANCH_WIDTH ** -0.5)
    w_out = nrm(ks[12], (DEPTH_2, D_MODEL, D_MODEL), D_MODEL ** -0.5)
    g_norm_ffn = 1.0 + nrm(ks[13], (DEPTH_2, D_MODEL), 0.02)
    w_gate = nrm(ks[14], (DEPTH_2, D_MODEL, D_FF_2), D_MODEL ** -0.5)
    w_up = nrm(ks[15], (DEPTH_2, D_MODEL, D_FF_2), D_MODEL ** -0.5)
    w_down = nrm(ks[16], (DEPTH_2, D_FF_2, D_MODEL), D_FF_2 ** -0.5)
    g_final = 1.0 + nrm(ks[17], (D_MODEL,), 0.02)
    return {'x': x, 'g_norm_mix': g_norm_mix, 'w_in': w_in, 'b_in': b_in, 'b_fgate': b_fgate,
            'conv_qk': conv_qk, 'g_mlstm_head': g_mlstm_head, 'pe_cmp': pe_cmp, 'w_cmp1': w_cmp1,
            'w_cmp2': w_cmp2, 'rel_bias': rel_bias, 'w_branch': w_branch, 'w_out': w_out,
            'g_norm_ffn': g_norm_ffn, 'w_gate': w_gate, 'w_up': w_up, 'w_down': w_down, 'g_final': g_final}

def second_block(x, g_norm_mix, w_in, b_in, b_fgate, conv_qk, g_mlstm_head, pe_cmp, w_cmp1, w_cmp2,
              rel_bias, w_branch, w_out, g_norm_ffn, w_gate, w_up, w_down, g_final):
    B, T, _ = x.shape
    h = x
    for l in range(DEPTH_2):
        u = rms_norm(h, g_norm_mix[l])
        proj = jnp.einsum('btd,de->bte', u, w_in[l]) + b_in[l]
        mq, mk, mv, mo, mi, mf, nq, nkv, ngate, merge = split_columns(proj, IN_SIZES)
        y_m = mlstm_mixer(mq, mk, mv, mo, mi, mf, b_fgate[l], conv_qk[l], g_mlstm_head[l])
        y_n = nsa_mixer(nq, nkv, ngate, pe_cmp[l], w_cmp1[l], w_cmp2[l], rel_bias)
        ys = jnp.stack([y_m, y_n], axis=2)
        branch = jnp.einsum('btnw,nwd->btnd', ys, w_branch[l])
        gates = jax.nn.sigmoid(merge.reshape(B, T, N_BRANCH, D_MODEL))
        mixed = jnp.sum(gates * branch, axis=2)
        h = h + mixed @ w_out[l]
        f = rms_norm(h, g_norm_ffn[l])
        h = h + (jax.nn.silu(f @ w_gate[l]) * (f @ w_up[l])) @ w_down[l]
    return rms_norm(h, g_final)


def setup_inputs(seed=0):
    out = dict(first_inputs(seed))
    for name, value in second_inputs(seed + 1).items():
        if name != "x":
            out[name + "_2"] = value
    return out


def reference(
    x, rwkv_norm_g, rwkv_mu, rwkv_w_rkv, rwkv_w0, rwkv_w1, rwkv_w2, rwkv_a0, rwkv_a1, rwkv_a2,
    rwkv_g1, rwkv_g2, rwkv_k_k, rwkv_k_a, rwkv_r_k, rwkv_lnx_w, rwkv_lnx_b, rwkv_w_o, kv_norm_g,
    kv_w, kv_f_bias, k_norm_g, attn_norm_g, attn_w_q, q_norm_g, attn_w_o, mlp_norm_g, mlp_w_in,
    mlp_w_out, g_norm_mix_2, w_in_2, b_in_2, b_fgate_2, conv_qk_2, g_mlstm_head_2, pe_cmp_2,
    w_cmp1_2, w_cmp2_2, rel_bias_2, w_branch_2, w_out_2, g_norm_ffn_2, w_gate_2, w_up_2,
    w_down_2, g_final_2,
):
    x = first_block(
        x, rwkv_norm_g, rwkv_mu, rwkv_w_rkv, rwkv_w0, rwkv_w1, rwkv_w2, rwkv_a0, rwkv_a1,
        rwkv_a2, rwkv_g1, rwkv_g2, rwkv_k_k, rwkv_k_a, rwkv_r_k, rwkv_lnx_w, rwkv_lnx_b,
        rwkv_w_o, kv_norm_g, kv_w, kv_f_bias, k_norm_g, attn_norm_g, attn_w_q, q_norm_g,
        attn_w_o, mlp_norm_g, mlp_w_in, mlp_w_out,
    )
    return second_block(
        x, g_norm_mix_2, w_in_2, b_in_2, b_fgate_2, conv_qk_2, g_mlstm_head_2, pe_cmp_2,
        w_cmp1_2, w_cmp2_2, rel_bias_2, w_branch_2, w_out_2, g_norm_ffn_2, w_gate_2, w_up_2,
        w_down_2, g_final_2,
    )


_drawn_inputs = setup_inputs


def setup_inputs(seed=0):
    import zlib

    import numpy as np

    out = dict(_drawn_inputs(seed))
    spreads = {}
    factors = {'rwkv_w1': 8.0,
     'rwkv_w2': 8.0,
     'rwkv_a0': 4.129,
     'rwkv_a1': 4.284,
     'rwkv_a2': 4.305,
     'rwkv_k_k': 4.366,
     'rwkv_k_a': 3.219,
     'rwkv_lnx_w': 3.779,
     'rwkv_lnx_b': 8.0,
     'kv_norm_g': 4.382,
     'k_norm_g': 7.987,
     'attn_norm_g': 8.0,
     'q_norm_g': 8.0,
     'g_norm_mix_2': 7.857,
     'b_in_2': 3.533,
     'g_mlstm_head_2': 33.513,
     'pe_cmp_2': 5.161,
     'g_norm_ffn_2': 13.249,
     'g_final_2': 22.945}
    for name, (base, spread) in spreads.items():
        noise = np.random.default_rng([zlib.crc32(name.encode()), seed]).standard_normal(out[name].shape)
        drawn = base * np.exp(spread * noise) if base else spread * noise
        out[name] = __import__('jax').numpy.asarray(drawn.astype(out[name].dtype))
    for name, factor in factors.items():
        out[name] = (out[name] * factor).astype(out[name].dtype)
    return out
```

```python
import math
from contextlib import ExitStack

import numpy as np
import concourse.bass as bass
from concourse import mybir
from concourse.alu_op_type import AluOpType as ALU

ACT = mybir.ActivationFunctionType
F32 = mybir.dt.float32
AX_X = mybir.AxisListType.X

P = 128
T = 512
D = 1024
KD = D // P
NT = T // P
CHUNK = 128
HD = 64
EPS = 1e-6
GN_EPS = 64e-5
FF1 = 4096
FF2 = 2816
NEG = -1e30
DECAY_UNIT = math.exp(-0.5)

MQ, MK, MV, MO, MI, MF, NQ, NKV, NG, MERGE = 0, 512, 1024, 1536, 2048, 2052, 2056, 2568, 3336, 3360
N_CMP = (T - 32) // 16 + 1
REL_N = 1023

IDENT, ONES, HALFMEAN, FLIP, CAUSAL_NEG, LATE_POS, AFTER, FROM, LEVEL = 0, 1, 2, 3, 4, 5, 6, 7, 8
SLOTS = 4


def constants():
    a = np.arange(P)
    i, j = a[:, None], a[None, :]
    mats = [
        i == j,
        np.ones((P, P)),
        (i // HD == j // HD) / HD,
        i + j == P - 1,
        np.where(j > i, NEG, 0.0),
        np.where(i > j, -NEG, 0.0),
        j > i,
        j >= i,
    ]
    for s in (1, 2, 4, 8, 16, 32, 64):
        low = (i // (2 * s) == j // (2 * s)) & ((i // s) % 2 == 1) & ((j // s) % 2 == 0)
        mats += [low, low.T]
    cmat = np.stack([np.asarray(m, np.float32) for m in mats], 1).reshape(P, -1)
    sel = np.repeat(np.eye(16, dtype=np.float32), P, axis=1)
    dist = 511 - np.arange(1024)
    n = np.maximum(dist, 0)
    nf = np.maximum(n, 1).astype(np.float32)
    large = 16 + (np.log(nf / 16) / np.float32(math.log(64)) * 16).astype(np.int32)
    bucket = np.where(n < 16, n, np.minimum(large, 31))
    onehot = np.zeros((33, 1024), np.float32)
    onehot[bucket, np.arange(1024)] = dist >= 0
    onehot[32] = dist < 0
    return {"c_mat": cmat, "c_sel": sel, "c_onehot": onehot}


def param_rows():
    spec = [("rwkv_norm_g", 8), ("rwkv_mu", 48), ("rwkv_w0", 8), ("rwkv_a0", 8), ("rwkv_k_k", 8),
            ("rwkv_k_a", 8), ("rwkv_r_k", 8), ("rwkv_lnx_w", 8), ("rwkv_lnx_b", 8),
            ("kv_norm_g", 8), ("attn_norm_g", 8),
            ("k_norm_g", 8), ("q_norm_g", 8), ("mlp_norm_g", 16), ("g_norm_mix_2", 8),
            ("b_mqk", 8), ("b_mo", 4), ("b_nq", 4), ("b_nkv", 6), ("b_merge", 16),
            ("conv_qk_2", 32), ("g_mlstm_head_2", 4), ("g_norm_ffn_2", 8), ("g_final_2", 8)]
    place, at = {}, 0
    for name, n in spec:
        if at // P != (at + n - 1) // P:
            at = (at // P + 1) * P
        place[name] = (at, n)
        at += n
    assert at <= 3 * P
    return place


N_PAR = len(param_rows()) + 1


def build(nc, a, out, scratch):
    ctx = ExitStack()
    with ctx:
        def sb(name, shape):
            return ctx.enter_context(nc.sbuf_tensor(name, shape, F32))

        def sem(name):
            return ctx.enter_context(nc.semaphore(name))

        slab = [sb(f"slab{i}", [P, KD, T]) for i in range(9)]
        ring = sb("ring", [P, SLOTS, KD, 256])
        cmat = sb("cmat", [P, 22, P])
        PK = sb("PK", [P, 3 * P])
        T1, T2, T3, T4 = (sb(f"T{i}", [P, T]) for i in (1, 2, 3, 4))
        AR = sb("AR", [P, NT, 2, P])
        BK = sb("BK", [P, 2, T])
        SS = sb("SS", [P, P])
        RT = sb("RT", [P, P])
        SA = sb("SA", [P, P])
        small = sb("small", [P, 64])
        eps6, eps6q, epsg, one1 = (small[:, i:i + 1] for i in range(4))
        omka = small[:, 4:12]
        cmid = small[:, 12:16]
        cend = small[:, 16:20]
        cexp = small[:, 20:24]
        bank = [ctx.enter_context(nc.psum_tensor(f"bank{i}", [P, T], F32)) for i in range(8)]

        rows = param_rows()

        def par(name, i=0):
            r = rows[name][0] + i
            return PK[:, r:r + 1]

        def mat(i, n=1):
            return cmat[:, i:i + n, :].rearrange("p a b -> p (a b)")

        def c4(ap):
            return ap.rearrange("p (c t) -> p c t", t=CHUNK)

        S0, S1, S2, S3, S4, S5, S6, S7, S8 = slab
        rstd = T4

        def flat(s):
            return s[:].rearrange("p k t -> p (k t)")

        stream = []
        pairs = {}
        ends = []
        pair_chunks = []
        n_pairs = [0]

        def chunk(parts, nk):
            g = len(stream)
            stream.append((g % SLOTS, [(ring[:, g % SLOTS, 0:nk, c0:c0 + src.shape[-1]], src)
                                       if len(src.shape) == 3 else (dst_of(g % SLOTS, nk, c0), src)
                                       for c0, src in parts], nk))
            return g

        def dst_of(slot, nk, c0):
            return ring[:, slot, 0:nk, c0:c0 + P].rearrange("p k (g d) -> p k g d", g=2)

        def add_pair(name, k_tiles, parts_of):
            j = n_pairs[0]
            if name in pairs and pairs[name][0] + pairs[name][1] == j:
                pairs[name] = (pairs[name][0], pairs[name][1] + 1)
            else:
                pairs[name] = (j, 1)
            mine = []
            for k0 in range(0, k_tiles, KD):
                nk = min(KD, k_tiles - k0)
                mine.append((chunk(parts_of(k0, nk), nk), k0, nk))
            pair_chunks.append(mine)
            ends.append(len(stream))
            n_pairs[0] += 1

        def cols(w, c0, n=256):
            return lambda k0, nk: [(0, w[k0 * P:(k0 + nk) * P, c0:c0 + n].rearrange("(k p) n -> p k n", p=P))]

        def gemm_plan(name, w, k_tiles, c0, n):
            for i in range(n // 256):
                add_pair(name, k_tiles, cols(w, c0 + 256 * i))

        w_rkv = a["rwkv_w_rkv"][0]
        gemm_plan("r", w_rkv[0], KD, 0, D)
        gemm_plan("k", w_rkv[1], KD, 0, D)
        gemm_plan("v", w_rkv[2], KD, 0, D)
        gemm_plan("rwkv_o", a["rwkv_w_o"][0], KD, 0, D)
        gemm_plan("mlp0_in", a["mlp_w_in"][0], KD, 0, FF1)
        gemm_plan("mlp0_out", a["mlp_w_out"][0], FF1 // P, 0, D)
        gemm_plan("fk", a["kv_w"], KD, 0, D)
        gemm_plan("fv", a["kv_w"], KD, D, D)
        gemm_plan("fq", a["attn_w_q"][0], KD, 0, D)
        gemm_plan("fox_o", a["attn_w_o"][0], KD, 0, D)
        gemm_plan("mlp1_in", a["mlp_w_in"][1], KD, 0, FF1)
        gemm_plan("mlp1_out", a["mlp_w_out"][1], FF1 // P, 0, D)
        w_in = a["w_in_2"][0]
        gemm_plan("mqk", w_in, KD, MQ, 1024)
        gemm_plan("mv", w_in, KD, MV, 512)
        gemm_plan("mo", w_in, KD, MO, 512)
        nq_src = w_in[:, NQ:NQ + 512].rearrange("(k p) (g r d) -> r p k g d", p=P, g=2, r=4)

        def two(c0, c1):
            def parts(k0, nk):
                return [(0, w_in[:, c0:c0 + P].rearrange("(k p) n -> p k n", p=P)),
                        (P, w_in[:, c1:c1 + P].rearrange("(k p) n -> p k n", p=P))]
            return parts

        def nq_tile(slot_col, r):
            return [(slot_col + 64 * g, w_in[:, NQ + 256 * g + 64 * r:NQ + 256 * g + 64 * r + 64]
                     .rearrange("(k p) n -> p k n", p=P)) for g in range(2)]

        for i in range(2):
            add_pair("nq", KD, lambda k0, nk, i=i: nq_tile(0, 2 * i) + nq_tile(P, 2 * i + 1))
        add_pair("kvc", KD, two(NKV, NKV + 128))
        add_pair("ksw", KD, two(NKV + 256, NKV + 512))
        add_pair("vsw", KD, two(NKV + 384, NKV + 640))
        w_br = a["w_branch_2"][0]

        def branch_cols(n, c0):
            if n == 0:
                return lambda k0, nk: [(0, w_br[0][:, c0:c0 + 256].rearrange("(k p) n -> p k n", p=P))]
            return lambda k0, nk: [(0, w_br[1][:, c0:c0 + 256])]

        for i in range(4):
            for n in range(2):
                add_pair(f"merge{n}_{i}", KD, cols(w_in, MERGE + D * n + 256 * i))
                add_pair(f"branch{n}_{i}", 4, branch_cols(n, 256 * i))
        gemm_plan("w_out", a["w_out_2"][0], KD, 0, D)
        for i in range(FF2 // 256):
            add_pair(f"gate_{i}", KD, cols(a["w_gate_2"][0], 256 * i))
            add_pair(f"up_{i}", KD, cols(a["w_up_2"][0], 256 * i))
        gemm_plan("down", a["w_down_2"][0], FF2 // P, 0, D)

        loads, landed, total = [], [], [0] * SLOTS
        for slot, parts, nk in stream:
            dmas = []
            for dst, src in parts:
                if len(src.shape) == 2 or src.shape[0] == 512:
                    for g in range(2):
                        dmas.append((ring[64 * g:64 * g + 64, slot, 0:4, :],
                                     src[256 * g:256 * g + 256, :].rearrange("(r d) n -> d r n", d=64)))
                else:
                    dmas.append((dst, src))
            total[slot] += 16 * len(dmas)
            loads.append(dmas)
            landed.append(total[slot])

        s_const, s_x, s_par, s_lora, s_ffw, s_small_w, s_sel, s_cmp, s_bias = (
            sem(n) for n in ("const_loaded", "x_loaded", "params_loaded", "lora_loaded", "fgate_w_loaded",
                             "small_w_loaded", "sel_loaded", "cmp_w_loaded", "bias_rows_loaded"))
        s_oh, s_relst, s_hankel, s_wz = (sem(n) for n in ("onehot_loaded", "rel_stored", "hankel_loaded",
                                                          "small_w_zeroed"))
        slot_loaded = [sem(f"slot{i}_loaded") for i in range(SLOTS)]
        chunk_done = sem("chunk_multiplied")
        evacuated = [sem(f"pair_evacuated{i}") for i in range(2)]
        pe_t, pe_tc = sem("turned"), sem("turned_copied")
        norm_sq, norm_mm, norm_root, norm_out = (sem(n) for n in ("norm_squared", "norm_summed", "norm_rooted",
                                                                  "norm_written"))
        dchain, achain = sem("vector_chain"), sem("scalar_chain")
        mix_ready, lora1, lora1_out, lora2 = (sem(n) for n in ("mix_written", "lora1_done",
                                                                         "lora1_evacuated", "lora2_done"))
        lora2_out = sem("lora2_evacuated")
        setup_done = sem("setup_done")
        (p_kk, p_sq, p_ssq, p_nrm, p_c, p_exp, p_fm, p_bon, p_bonmm, p_prod, p_prodc, p_tr, p_trc, p_x, p_xc, p_d,
         p_dc, p_r, p_rc, p_sa, p_sac, p_st, p_stc, p_y, p_yc, p_mean, p_cent, p_var, p_gn, p_out) = (
            sem("rwkv_" + n) for n in (
                "kk_raw", "kk_squared", "kk_summed", "kk_rooted", "logs", "exps", "factors", "bonus", "bonus_summed",
                "products", "products_masked", "turned", "turned_copied", "x", "x_copied", "d", "d_added",
                "r", "r_copied", "sa", "sa_copied", "state", "state_updated", "y", "y_copied", "gn_mean",
                "gn_squared", "gn_var", "gn_rooted", "out"))
        (h_sq, h_mm, h_rt, h_out) = (sem("headnorm_" + n) for n in ("squared", "summed", "rooted", "written"))
        (f_mm, f_rows, f_row2, f_cum) = (sem("fgate_" + n) for n in ("product", "rows", "row_parts", "summed"))
        (a_cb, a_cbc, a_s, a_l, a_e, a_p, a_t, a_tc, a_pv, a_o) = (
            sem("attn_" + n) for n in ("rowbias", "rowbias_copied", "scores", "logits", "exp", "probs", "turned",
                                       "turned_copied", "pv", "out_copied"))
        (m_conv, m_silu, m_rows, m_rowx, m_rowd, m_gt, m_gtc) = (
            sem("mlstm_" + n) for n in ("conv", "silu", "rows", "row_parts", "row_done", "g_turned", "g_columns"))
        (m_b, m_bd, m_e, m_kt, m_pd, m_cn, m_cnd, m_num, m_hq, m_rms, m_rt, m_y) = (
            sem("mlstm_" + n) for n in ("bcast", "exponent", "exps", "kq", "probs", "state", "state_updated", "num",
                                        "h_squared", "rms", "rooted", "y"))
        (c_mm, c_hid, c_out, c_outc, z_row, z_rowc, z_flip, z_flipc) = (
            sem(n) for n in ("cmp_hidden", "cmp_silu", "cmp_out", "cmp_copied", "rel_row", "rel_row_copied",
                             "rel_flip", "rel_bias_ready"))
        m_kscaled = sem("mlstm_keys_scaled")
        p_gn2, p_bon_done, m_rowx2, m_hq1 = (sem(n) for n in ("rwkv_gn_rooted2", "rwkv_bonus_added", "mlstm_f_row",
                                                             "mlstm_h"))
        y_done, fin_t, fin_c, s_out = (sem(n) for n in ("nsa_done", "final_turned", "final_copied", "stored"))

        BB = flat(S2)[:, 0:2048].rearrange("p (u n) -> p u n", u=8)
        KM = flat(S2)[:, 2048:4096].rearrange("p (u n) -> p u n", u=8)
        MM = flat(S3)[:, 0:2048].rearrange("p (u n) -> p u n", u=8)
        XX = flat(S3)[:, 2048:3072].rearrange("p (u n) -> p u n", u=8)
        TM = flat(S3)[:, 3072:4096].rearrange("p (w c f) -> p w c f", w=2, c=4)
        lw1 = flat(S7)[:, 0:512].rearrange("p (k n) -> p k n", k=KD)
        la1 = flat(S7)[:, 512:1024].rearrange("p (k n) -> p k n", k=KD)
        lg1 = flat(S7)[:, 1024:2304].rearrange("p (k n) -> p k n", k=KD)
        lw2 = flat(S7)[0:64, 2304:3328]
        la2 = flat(S8)[0:64, 0:1024]
        lg2 = flat(S8)[:, 1024:2048]
        lg2b = flat(S8)[0:32, 2048:3072]
        LH = AR[:].rearrange("p c w t -> p (c w t)").rearrange("p (w t) -> p w t", w=2)
        wff = flat(S6)[:, 0:128].rearrange("p (k n) -> p k n", k=KD)
        fb = small[0:16, 24:25]
        sel = flat(S8)[0:16, 0:2048]
        NC = flat(S8)[0:16, 2048:2560]
        CB = flat(S8)[:, 2560:3584].rearrange("p (b t) -> p b t", b=2)
        Pb = flat(S6)[:, 0:1536].rearrange("p (b t) -> p b t", b=3)
        PTb = flat(S6)[:, 2048:3072].rearrange("p (b t) -> p b t", b=2)
        mx = small[:, 26:29]
        rs = small[:, 29:32]
        QZ = [LH, BK[:]]
        FV = flat(S4).rearrange("p (t n) -> p t n", t=NT)
        ident = mat(IDENT)
        ones = mat(ONES)
        halfmean = mat(HALFMEAN)

        fox_units = []
        for e in range(KD):
            for hh in range(2):
                h = 2 * e + hh
                for tq in range(NT):
                    w = P * (tq + 1)
                    fox_units.append(dict(
                        q=QZ[e % 2][:, hh, tq * P:tq * P + P], k=S3[:, e, 0:w], mask=True, w=w,
                        bias=CB[:, h % 2, 0:w], gate=None, clamp=False,
                        v=[FV[:, s, h * HD:h * HD + HD] for s in range(tq + 1)],
                        out=bank[e % 2][64 * hh:64 * hh + 64, tq * P:tq * P + P], first=True, last=True,
                        rowbias=h if tq == 0 else None, e=e, ends_e=(hh == 1 and tq == NT - 1)))
        SM = flat(S6)
        YM = S6[:, 0:4, :]
        YN = S6[:, 4:8, :]
        MVT = flat(S4)[:, 0:2048].rearrange("p (t n) -> p t n", t=NT)
        OG = S4[:, 4:8, :]
        NQT = S5[:, 0:4, :]
        KVC = S5[:, 4:6, :]
        KS = S5[:, 6, :]
        KW = S5[:, 7, :]
        Z = [(S7 if h < 4 else S8)[:].rearrange("p k t -> p (k t)")[:, 1024 * (h % 4):1024 * (h % 4) + 896]
             for h in range(8)]
        VSW = BK[:].rearrange("p b t -> p (b t)").rearrange("p (t n) -> p t n", t=NT)
        GT2 = sb("GT2", [P, NT, 24])
        KC = sb("KC", [P, 32])
        VC = sb("VC", [P, 2, 64])
        GC = sb("GC", [P, NT, 4])
        DC = sb("DC", [P, NT])
        PEH = sb("PEH", [P, 2])
        late = cmat[:, LEVEL:LEVEL + 14, :].rearrange("p a b -> p (a b)")
        RSI, REM, SELM, BVS = late[0:4, 0:512], late[0:4, 512:1024], late[0:4, 1024:1536], late[:, 1536:1792]
        GR, RI, RG, RMU = S6[0:24, 0, :], S6[0:4, 1, :], S6[0:4, 2, :], S6[0:4, 3, :]
        WSM = flat(S6)[:, 2048:3072].rearrange("p (k n) -> p k n", k=KD)
        OH = flat(S6)[0:33, 3072:4096]
        CN = flat(S6)[:, 2048:3072].rearrange("p (c n) -> p c n", c=4)
        KWT, PM = S6[:, 6, :], S6[:, 7, :]
        ROW = AR[0:8].rearrange("p c w t -> p (c w t)")
        BMV, QS = T3, T4
        HID = SS[:, 0:4 * N_CMP].rearrange("p (j g c) -> p j g c", j=2, g=2)
        W2C = SA[:].rearrange("p (j d) -> p j d", j=2)
        PEC, PET = RT[0:64, 0:64], RT[0:64, 64:128]
        HK = S2[:]
        TB = small[0:33, 48:56]
        nsa_units = []
        for r in range(4):
            for g in range(2):
                h = 4 * g + r
                for tq in range(NT):
                    for b, br in enumerate(("cmp", "sel", "win")):
                        w = N_CMP if br == "cmp" else P * (tq + 1)
                        keys = {"cmp": KC[64 * g:64 * g + 64, 0:N_CMP], "sel": KS[64 * g:64 * g + 64, 0:w],
                                "win": KW[64 * g:64 * g + 64, 0:w]}[br]
                        if br == "cmp":
                            y0 = 415 - P * tq
                            bias = Z[h][:, y0:y0 + 16 * (N_CMP - 1) + 1:16]
                            v = [VC[0:N_CMP, g, :]]
                        else:
                            bias = Z[h][:, 384 - P * tq:512]
                            off = (0 if br == "sel" else 128) + 64 * g
                            v = [VSW[:, s, off:off + 64] for s in range(tq + 1)]
                        nsa_units.append(dict(
                            q=NQT[64 * g:64 * g + 64, r, tq * P:tq * P + P], k=keys, mask=False, w=w, bias=bias,
                            gate=GT2[:, tq, h * 3 + b:h * 3 + b + 1], clamp=(br == "cmp"), v=v,
                            out=bank[r % 2][64 * g:64 * g + 64, tq * P:tq * P + P],
                            first=(b == 0), last=(b == 2), rowbias=None, e=r,
                            ends_e=(g == 1 and tq == NT - 1 and b == 2)))
        NF, NN = len(fox_units), len(nsa_units)
        Pn = flat(S3)[:, 0:1536].rearrange("p (b t) -> p b t", b=3)
        PTn = flat(S3)[:, 2048:3072].rearrange("p (b t) -> p b t", b=2)

        def pair_wait(eng, name):
            first, n = pairs[name]
            for j in range(max(first, first + n - 2), first + n):
                eng.wait_ge(evacuated[j % 2], j // 2 + 1)

        NORMS = ["rwkv", "mlp0", "kv", "mlp1", "mix", "ffn", "final"]
        X_AFTER = {"rwkv": None, "mlp0": "rwkv_o", "kv": "mlp0_out", "mlp1": "fox_o", "mix": "mlp1_out",
                   "ffn": "w_out", "final": "down"}
        OUT_BEFORE = {}
        n_out = 0
        for n in NORMS:
            n_out += 16 if n == "kv" else 8
            OUT_BEFORE[n] = n_out

        block = ctx.enter_context(nc.Block())

        @block.sync
        def _(sp):
            for g, dmas in enumerate(loads):
                if g >= SLOTS:
                    sp.wait_ge(chunk_done, g - SLOTS + 1)
                for dst, src in dmas:
                    sp.dma_start(dst, src).then_inc(slot_loaded[g % SLOTS], 16)
            for t in range(NT):
                sp.wait_ge(fin_c, 2 * (t + 1))
                sp.dma_start(out[0, t * P:(t + 1) * P, :], S2[:, 2 * t:2 * t + 2, :].rearrange("p k t -> p (k t)")
                             ).then_inc(s_out, 16)
            sp.wait_ge(s_out, 16 * NT)

        @block.gpsimd
        def _(pool):
            def load(dst, src, s):
                pool.dma_start(dst, src).then_inc(s, 16)

            load(cmat[:].rearrange("p a b -> p (a b)"), a["c_mat"], s_const)
            load(flat(S3).rearrange("p (t f) -> p t f", t=NT), a["x"][0].rearrange("(t p) f -> p t f", p=P), s_x)
            b_in = a["b_in_2"][0]
            bnq = b_in[NQ:NQ + 512].rearrange("(g r d) -> g r d", g=2, r=4)
            src = {
                "b_mqk": b_in[0:1024].rearrange("(k p) -> k p", p=P),
                "b_mo": b_in[MO:MO + 512].rearrange("(k p) -> k p", p=P),
                "b_nkv": b_in[NKV:NKV + 768].rearrange("(k p) -> k p", p=P),
                "b_merge": b_in[MERGE:MERGE + 2048].rearrange("(k p) -> k p", p=P),
                "rwkv_mu": a["rwkv_mu"][0].rearrange("m (k p) -> (m k) p", p=P),
                "rwkv_r_k": a["rwkv_r_k"][0].rearrange("(k h) d -> k (h d)", h=2),
                "k_norm_g": a["k_norm_g"].rearrange("(k h) d -> k (h d)", h=2),
                "q_norm_g": a["q_norm_g"][0].rearrange("(k h) d -> k (h d)", h=2),
                "mlp_norm_g": a["mlp_norm_g"].rearrange("m (k p) -> (m k) p", p=P),
                "conv_qk_2": a["conv_qk_2"][0].rearrange("m (k p) -> (m k) p", p=P),
                "kv_norm_g": a["kv_norm_g"].rearrange("(k p) -> k p", p=P),
                "g_final_2": a["g_final_2"].rearrange("(k p) -> k p", p=P),
            }
            pool.wait_ge(setup_done, 1)
            n = 0
            for name, (r0, k) in rows.items():
                dst = S4[r0 % P:r0 % P + k, r0 // P, 0:P]
                if name == "b_nq":
                    for g in range(2):
                        load(dst[:, 64 * g:64 * g + 64], bnq[g], s_par)
                        n += 1
                    continue
                s = src[name] if name in src else a[name][0].rearrange("(k p) -> k p", p=P)
                load(dst, s, s_par)
                n += 1
            assert n == N_PAR
            load(lw1, a["rwkv_w1"][0].rearrange("(k p) n -> p k n", p=P), s_lora)
            load(lw2, a["rwkv_w2"][0], s_lora)
            load(la1, a["rwkv_a1"][0].rearrange("(k p) n -> p k n", p=P), s_lora)
            load(la2, a["rwkv_a2"][0], s_lora)
            load(lg1, a["rwkv_g1"][0].rearrange("(k p) n -> p k n", p=P), s_lora)
            load(lg2, a["rwkv_g2"][0][0:P, :], s_lora)
            load(lg2b, a["rwkv_g2"][0][P:160, :], s_lora)
            load(fb, a["kv_f_bias"].rearrange("(p n) -> p n", n=1), s_bias)
            pair_wait(pool, "mlp0_out")
            load(wff, a["kv_w"][:, 2 * D:2 * D + 16].rearrange("(k p) n -> p k n", p=P), s_ffw)
            load(sel, a["c_sel"], s_sel)
            pair_wait(pool, "mlp1_out")
            for j, s in ((0, S7), (1, S8)):
                w1 = a["w_cmp1_2"][0][j].rearrange("(p d) n -> d p n", d=64)
                for half in range(2):
                    load(s[64 * half:64 * half + 64].rearrange("d k t -> d (k t)").rearrange("d (p n) -> d p n", p=32),
                         w1, s_cmp)
            load(W2C[:, 0, :], a["w_cmp2_2"][0][0], s_cmp)
            load(W2C[:, 1, :], a["w_cmp2_2"][0][1], s_cmp)
            load(PEC, a["pe_cmp_2"][0].rearrange("j p d -> (j p) d"), s_cmp)
            pool.wait_ge(s_wz, 1)
            load(WSM[:, :, 0:4], w_in[:, MI:MI + 4].rearrange("(k p) n -> p k n", p=P), s_small_w)
            load(WSM[:, :, 32:36], w_in[:, MF:MF + 4].rearrange("(k p) n -> p k n", p=P), s_small_w)
            load(WSM[:, :, 64:88], w_in[:, NG:NG + 24].rearrange("(k p) n -> p k n", p=P), s_small_w)
            load(small[0:4, 33:34], b_in[MI:MI + 4].rearrange("(p n) -> p n", n=1), s_small_w)
            load(small[0:4, 34:35], b_in[MF:MF + 4].rearrange("(p n) -> p n", n=1), s_small_w)
            load(small[0:4, 35:36], a["b_fgate_2"].rearrange("a n -> n a"), s_small_w)
            load(small[0:24, 36:37], b_in[NG:NG + 24].rearrange("(p n) -> p n", n=1), s_small_w)
            load(BMV[:], b_in[MV:MV + 512].partition_broadcast(P), s_small_w)
            load(BVS[:, 0:128], b_in[NKV + 384:NKV + 512].partition_broadcast(P), s_small_w)
            load(BVS[:, 128:256], b_in[NKV + 640:NKV + 768].partition_broadcast(P), s_small_w)
            load(OH, a["c_onehot"], s_oh)
            load(TB[0:32, :], a["rel_bias_2"], s_oh)
            load(SELM, a["c_sel"][0:4, 0:512], s_oh)
            pool.wait_ge(z_rowc, 2)
            pool.dma_start(scratch, ROW).then_inc(s_relst, 16)
            pool.wait_ge(s_relst, 16)
            pool.wait_ge(m_silu, 8)
            hank = bass.AP(scratch.tensor, 0, [[1, P], [1024, 8], [1, 512]])
            load(HK, hank, s_hankel)

        @block.tensor
        def _(pe):
            def gemm(name, rhs, tm=False):
                first, n = pairs[name]
                for j in range(first, first + n):
                    if j >= 2:
                        pe.wait_ge(evacuated[j % 2], j // 2)
                    b = 2 * (j % 2)
                    last_k = pair_chunks[j][-1][1] + pair_chunks[j][-1][2] - 1
                    for g, k0, nk in pair_chunks[j]:
                        pe.wait_ge(slot_loaded[g % SLOTS], landed[g])
                        w = ring[:, g % SLOTS]
                        if tm:
                            for t in range(NT):
                                for k in range(nk):
                                    mm = pe.matmul(bank[b + t // 2][:, 256 * (t % 2):256 * (t % 2) + 256],
                                                   rhs(k)[:, t * P:(t + 1) * P], w[:, k, :],
                                                   start=(k == 0), stop=(k == nk - 1))
                        else:
                            for half in range(2):
                                for k in range(nk):
                                    mm = pe.matmul(bank[b + half][:], w[:, k, half * P:(half + 1) * P], rhs(k0 + k),
                                                   start=(k0 + k == 0), stop=(k0 + k == last_k))
                        mm.then_inc(chunk_done, 1)

            def norm(name):
                n = NORMS.index(name)
                for k in range(KD):
                    pe.wait_ge(norm_sq, 8 * n + k + 1)
                    pe.matmul(bank[4][:], ones, (T1, T2)[k % 2][:], start=(k == 0), stop=(k == KD - 1)
                              ).then_inc(norm_mm, 1)

            pe.wait_ge(s_const, 16)
            pe.wait_ge(s_x, 16)
            xt = flat(S3).rearrange("p (t f) -> p t f", t=NT)
            for k in range(KD):
                if k >= 2:
                    pe.wait_ge(pe_tc, k - 1)
                for t in range(NT):
                    mm = pe.transpose(bank[4 + k % 2][:, t * P:(t + 1) * P], xt[:, t, k * P:(k + 1) * P], ident)
                mm.then_inc(pe_t, 1)
            pe.wait_ge(s_par, 16 * N_PAR)
            for i in range(3):
                mm = pe.transpose(bank[6][:, i * P:(i + 1) * P], S4[:, i, 0:P], ident)
            mm.then_inc(pe_t, 1)
            norm("rwkv")

            pe.wait_ge(s_lora, 16 * 7)
            w1s = [[(lw1, 0, 64)], [(la1, 0, 64)], [(lg1, 0, 128), (lg1, 128, 32)]]
            q = 0
            nl = 0
            for i in range(3):
                pe.wait_ge(mix_ready, i + 1)
                for n, (w, c0, m) in enumerate(w1s[i]):
                    if nl >= 2:
                        pe.wait_ge(lora1_out, nl - 1)
                    for k in range(KD):
                        mm = pe.matmul(bank[4 + nl % 2][0:m, :], w[:, k, c0:c0 + m], S3[:, k, :],
                                       start=(k == 0), stop=(k == KD - 1))
                    mm.then_inc(lora1, 1)
                    nl += 1
                pe.wait_ge(lora1_out, nl)
                for e in range(KD):
                    if q >= 2:
                        pe.wait_ge(lora2_out, q - 1)
                    o = bank[6 + q % 2][:]
                    if i < 2:
                        mm = pe.matmul(o, (lw2, la2)[i][:, e * P:(e + 1) * P], LH[0:64, i, :], start=True, stop=True)
                    else:
                        pe.matmul(o, lg2[:, e * P:(e + 1) * P], LH[:, 0, :], start=True, stop=False)
                        mm = pe.matmul(o, lg2b[:, e * P:(e + 1) * P], LH[0:32, 1, :], start=False, stop=True)
                    mm.then_inc(lora2, 1)
                    q += 1
            for i, name in enumerate("rkv"):
                pe.wait_ge(mix_ready, 4 + i)
                gemm(name, lambda k: S3[:, k, :])

            def tile_front(e):
                pe.wait_ge(p_sq, e + 1)
                pe.matmul(bank[6][:], halfmean, T2[:], start=True, stop=True).then_inc(p_ssq, 1)
                pe.wait_ge(p_bon, e + 1)
                pe.matmul(bank[7][:], halfmean, T2[:], start=True, stop=True).then_inc(p_bonmm, 1)

            def products(e):
                for w in range(2):
                    if w == 1:
                        pe.wait_ge(p_prodc, 3 * e + 1)
                    elif e > 0:
                        pe.wait_ge(p_out, e)
                    for u in range(8):
                        hh, c = u // 4, u % 4
                        o = bank[u // 2][:, 256 * (u % 2):256 * (u % 2) + 256]
                        s = slice(64 * hh, 64 * hh + 64)
                        mm = pe.matmul(o, BK[s, w, c * P:(c + 1) * P], AR[s, c].rearrange("p w t -> p (w t)"),
                                       start=True, stop=True)
                    mm.then_inc(p_prod, 1)
                for u in range(8):
                    hh, c = u // 4, u % 4
                    s = slice(64 * hh, 64 * hh + 64)
                    mm = pe.matmul(bank[4 + hh][:, c * P:(c + 1) * P], AR[s, c, 0], BK[s, 0, c * P:(c + 1) * P],
                                   start=True, stop=True)
                mm.then_inc(p_prod, 1)

            def turns(e):
                pe.wait_ge(p_prodc, 3 * e + 2)
                for w, src in enumerate((BK[:, 0], BK[:, 1], S1[:, e])):
                    if w == 2:
                        pe.wait_ge(p_bon_done, e + 1)
                    for c in range(NT):
                        mm = pe.transpose(bank[w][:, c * P:(c + 1) * P], src[:, c * P:(c + 1) * P], ident)
                mm.then_inc(p_tr, 1)

            def levels(e):
                for lv in range(6):
                    for hh in range(2):
                        n = (e * 6 + lv) * 2 + hh
                        if lv == 0:
                            pe.wait_ge(p_prodc, 3 * e + 3)
                            if hh == 0:
                                pe.wait_ge(p_trc, e + 1)
                        else:
                            pe.wait_ge(p_dc, n - 1)
                        xb, db = bank[3 * hh], (bank[3 * hh + 1], bank[3 * hh + 2])
                        for c in range(NT):
                            u = 4 * hh + c
                            mm = pe.matmul(xb[:, c * P:(c + 1) * P], BB[:, u, 0:P], MM[:, u, 0:P],
                                           start=True, stop=True)
                        mm.then_inc(p_x, 1)
                    for hh in range(2):
                        n = (e * 6 + lv) * 2 + hh
                        pe.wait_ge(p_xc, n + 1)
                        db = (bank[3 * hh + 1], bank[3 * hh + 2])
                        for c in range(NT):
                            u = 4 * hh + c
                            o = db[c // 2][:, 256 * (c % 2):256 * (c % 2) + 256]
                            pe.matmul(o[:, 0:P], MM[:, u, P:2 * P], XX[:, u, :], start=True, stop=True)
                            mm = pe.matmul(o[:, P:2 * P], XX[:, u, :], MM[:, u, P:2 * P], start=True, stop=True)
                        mm.then_inc(p_d, 1)

            def scan(e):
                pe.wait_ge(p_dc, 12 * (e + 1))
                for c in range(NT):
                    n = NT * e + c
                    t = slice(c * P, (c + 1) * P)
                    if c:
                        pe.wait_ge(p_stc, n - e)
                        pe.matmul(bank[6][:, 0:P], AR[:, c, 0], SS[:], start=True, stop=False)
                    for hh in range(2):
                        u = 4 * hh + c
                        if c:
                            mm = pe.matmul(bank[6][:, 64 * hh:64 * hh + 64], KM[:, u, 0:P],
                                           S1[:, e, c * P + 64 * hh:c * P + 64 * hh + 64], start=False, stop=(hh == 1))
                        else:
                            mm = pe.matmul(bank[6][:, 64 * hh:64 * hh + 64], KM[:, u, 0:P],
                                           S1[:, e, c * P + 64 * hh:c * P + 64 * hh + 64], start=True, stop=True)
                    mm.then_inc(p_r, 1)
                    pe.wait_ge(p_rc, n + 1)
                    for hh in range(2):
                        mm = pe.matmul(bank[7][:, 64 * hh:64 * hh + 64], MM[:, 4 * hh + c, P:2 * P],
                                       RT[:, 64 * hh:64 * hh + 64], start=True, stop=True)
                    mm.then_inc(p_sa, 1)
                    pe.wait_ge(p_sac, n + 1)
                    if c < NT - 1:
                        pe.matmul(bank[2][:, 0:P], TM[:, 0, c], SA[:], start=True, stop=False)
                        pe.matmul(bank[2][:, 0:P], TM[:, 1, c], S1[:, e, t], start=False, stop=True).then_inc(p_st, 1)
                    for hh in range(2):
                        u = 4 * hh + c
                        o = bank[1][64 * hh:64 * hh + 64, t]
                        hc = slice(64 * hh, 64 * hh + 64)
                        if c:
                            pe.matmul(o, SS[:, hc], AR[:, c, 1], start=True, stop=False)
                        pe.matmul(o, SA[:, hc], BB[:, u, P:2 * P], start=(c == 0), stop=False)
                        mm = pe.matmul(o, S1[:, e, c * P + 64 * hh:c * P + 64 * hh + 64], KM[:, u, P:2 * P],
                                       start=False, stop=True)
                    mm.then_inc(p_y, 1)

            def group_norm(e):
                pe.wait_ge(p_yc, e + 1)
                pe.matmul(bank[3][:], halfmean, T1[:], start=True, stop=True).then_inc(p_mean, 1)
                pe.wait_ge(p_cent, e + 1)
                pe.matmul(bank[4][:], halfmean, T2[:], start=True, stop=True).then_inc(p_var, 1)

            for e in range(KD):
                tile_front(e)
                products(e)
                turns(e)
                levels(e)
                scan(e)
                group_norm(e)
            pe.wait_ge(p_out, KD)
            gemm("rwkv_o", lambda k: S7[:, k, :])

            def mlp(i):
                norm(f"mlp{i}")
                pe.wait_ge(norm_out, OUT_BEFORE[f"mlp{i}"])
                gemm(f"mlp{i}_in", lambda k: S1[:, k, :])
                pair_wait(pe, f"mlp{i}_in")
                gemm(f"mlp{i}_out", lambda k: slab[2 + k // KD][:, k % KD, :])

            mlp(0)

            norm("kv")
            pe.wait_ge(norm_out, OUT_BEFORE["kv"] - 8)
            gemm("fk", lambda k: S1[:, k, :])
            gemm("fv", lambda k: S1[:, k, :], tm=True)
            pe.wait_ge(s_ffw, 16)
            for k in range(KD):
                mm = pe.matmul(bank[4][0:16, :], wff[:, k, :], S1[:, k, :], start=(k == 0), stop=(k == KD - 1))
            mm.then_inc(f_mm, 1)
            pe.wait_ge(norm_out, OUT_BEFORE["kv"])
            gemm("fq", lambda k: S2[:, k, :])
            for i in range(KD):
                pe.wait_ge(h_sq, i + 1)
                pe.matmul(bank[5][:], halfmean, T2[:], start=True, stop=True).then_inc(h_mm, 1)

            def attention(units, base, Pt, PTt, o_base, tiles):
                N = len(units)
                fox = units[0]["mask"]
                for i in range(N + 2):
                    if i < N:
                        u = units[i]
                        if fox and i % 8 == 0:
                            e = u["e"]
                            pe.wait_ge(h_sq, KD + e + 1)
                            if e == 0:
                                pe.wait_ge(h_out, KD)
                            pe.matmul(bank[3][:], halfmean, T2[:], start=True, stop=True).then_inc(h_mm, 1)
                        if u["rowbias"] is not None:
                            h = u["rowbias"]
                            if h == 0:
                                pe.wait_ge(f_cum, 1)
                                pe.wait_ge(s_sel, 16)
                            if h >= 1:
                                pe.wait_ge(a_cbc, h)
                            pe.matmul(bank[2][:], sel[:, h * P:(h + 1) * P], NC, start=True, stop=True
                                      ).then_inc(a_cb, 1)
                        if fox and i % 8 == 0:
                            pe.wait_ge(h_out, KD + u["e"] + 1)
                        if i >= 2:
                            pe.wait_ge(a_l, base + i - 1)
                        s = bank[4 + i % 2]
                        mm = pe.matmul(s[:, 0:u["w"]], u["q"], u["k"], start=True, stop=not u["mask"])
                        if u["mask"]:
                            mm = pe.matmul(s[:, u["w"] - P:u["w"]], ident, mat(CAUSAL_NEG), start=False, stop=True)
                        mm.then_inc(a_s, 1)
                    if 1 <= i <= N:
                        n = i - 1
                        u = units[n]
                        pe.wait_ge(a_p, base + n + 1)
                        if n >= 2:
                            pe.wait_ge(a_tc, base + n - 1)
                        b = bank[6 + n % 2]
                        if u["w"] == N_CMP:
                            mm = pe.transpose(b[0:N_CMP, 0:P], Pt[:, n % 3, 0:N_CMP], ident)
                        else:
                            for s in range(len(u["v"])):
                                mm = pe.transpose(b[:, s * P:(s + 1) * P], Pt[:, n % 3, s * P:(s + 1) * P], ident)
                        mm.then_inc(a_t, 1)
                    if i >= 2:
                        n = i - 2
                        u = units[n]
                        pe.wait_ge(a_tc, base + n + 1)
                        if u["first"] and u["e"] >= 2:
                            pe.wait_ge(a_o, o_base + u["e"] - 1)
                        K = N_CMP if u["w"] == N_CMP else P
                        for s, v in enumerate(u["v"]):
                            mm = pe.matmul(u["out"], v, PTt[0:K, n % 2, s * P:(s + 1) * P],
                                           start=(u["first"] and s == 0), stop=(u["last"] and s == len(u["v"]) - 1))
                        mm.then_inc(a_pv, 1)

            attention(fox_units, 0, Pb, PTb, 0, KD)
            pe.wait_ge(a_o, KD)
            gemm("fox_o", lambda k: S7[:, k, :])
            mlp(1)

            norm("mix")
            pe.wait_ge(norm_out, OUT_BEFORE["mix"])
            u1 = lambda k: S1[:, k, :]
            gemm("mqk", u1)
            gemm("mv", u1, tm=True)
            gemm("mo", u1)
            gemm("nq", u1)
            gemm("kvc", u1)
            gemm("ksw", u1)
            gemm("vsw", u1, tm=True)
            pe.wait_ge(s_small_w, 16 * 10)
            for k in range(KD):
                mm = pe.matmul(bank[4][:], WSM[:, k, :], S1[:, k, :], start=(k == 0), stop=(k == KD - 1))
            mm.then_inc(m_rows, 1)
            pe.wait_ge(s_cmp, 16 * 7)
            pe.transpose(bank[5][0:64, 0:64], PEC, ident[0:64, 0:64]).then_inc(c_mm, 1)
            pe.wait_ge(c_hid, 1)
            for j, s in enumerate((S7, S8)):
                w1 = flat(s).rearrange("d (p n) -> d p n", p=32)
                for p in range(32):
                    mm = pe.matmul(bank[5][:, 128 + j:129 + j], w1[0:64, p, :], PET[:, 32 * j + p:32 * j + p + 1],
                                   start=(p == 0), stop=(p == 31))
            mm.then_inc(c_mm, 1)
            pair_wait(pe, "kvc")
            for g in range(2):
                for j, s in enumerate((S7, S8)):
                    w1 = flat(s).rearrange("d (p n) -> d p n", p=32)
                    for p in range(32):
                        mm = pe.matmul(bank[6 + g][:, 32 * j:32 * j + N_CMP], w1[64 * g:64 * g + 64, p, :],
                                       KVC[64 * g:64 * g + 64, j, p:p + 16 * (N_CMP - 1) + 1:16],
                                       start=(p == 0), stop=(p == 31))
            mm.then_inc(c_mm, 1)
            pe.wait_ge(c_hid, 3)
            for g in range(2):
                pe.matmul(bank[5][64 * g:64 * g + 64, 0:N_CMP], W2C[:, 0, :], HID[:, 0, g, :], start=True, stop=True)
                mm = pe.matmul(bank[5][0:N_CMP, 128 + 64 * g:192 + 64 * g], HID[:, 1, g, :], W2C[:, 1, :],
                               start=True, stop=True)
            mm.then_inc(c_out, 1)
            pe.wait_ge(s_oh, 48)
            pe.wait_ge(s_wz, 1)
            pe.wait_ge(z_row, 1)
            for i in range(2):
                mm = pe.matmul(bank[6 + i][0:8, :], TB, OH[:, i * 512:(i + 1) * 512], start=True, stop=True)
            mm.then_inc(z_flip, 1)

            pe.wait_ge(m_rowd, 1)
            for c in range(NT):
                mm = pe.transpose(bank[4][:, 4 * c:4 * c + 4], RG[0:4, c * P:(c + 1) * P], ident[0:4, 0:4])
            for c in range(NT):
                mm = pe.transpose(bank[4][:, 32 + 24 * c:32 + 24 * c + 24], GR[0:24, c * P:(c + 1) * P],
                                  ident[0:24, 0:24])
            mm.then_inc(m_gt, 1)
            pe.wait_ge(m_silu, 8)
            pe.wait_ge(z_rowc, 2)
            pe.wait_ge(m_gtc, 1)
            pe.wait_ge(m_rowx, 3)
            pe.wait_ge(m_kscaled, 1)
            for h in range(4):
                if h:
                    pe.wait_ge(m_y, h)
                sh = SELM[:, h * P:(h + 1) * P]
                for i, (row, b) in enumerate(((RMU, 4), (RSI, 6), (REM, 2))):
                    mm = pe.matmul(bank[b][:], sh, row, start=True, stop=True)
                mm.then_inc(m_b, 1)
                for c in range(NT):
                    t = slice(c * P, (c + 1) * P)
                    pe.matmul(bank[5][:, t], S3[:, 4 + h, t], S3[:, h, t], start=True, stop=True)
                for c in range(NT):
                    t = slice(c * P, (c + 1) * P)
                    mm = pe.transpose(bank[7][:, t], S3[:, 4 + h, t], ident)
                mm.then_inc(m_kt, 1)
                pe.wait_ge(m_pd, h + 1)
                for c in range(NT):
                    t = slice(c * P, (c + 1) * P)
                    v = MVT[:, c, h * P:(h + 1) * P]
                    if c:
                        pe.wait_ge(m_cnd, 3 * h + c)
                    pe.matmul(bank[0][:, t], v, PM[:, t], start=True, stop=(c == 0))
                    if c:
                        pe.matmul(bank[0][:, t], CN[:, c, 0:P], QS[:, t], start=False, stop=True)
                    mm = pe.matmul(bank[1][:, t], ones, PM[:, t], start=True, stop=(c == 0))
                    if c:
                        mm = pe.matmul(bank[1][:, t], CN[:, c, P:2 * P], QS[:, t], start=False, stop=True)
                    if c < NT - 1:
                        pe.matmul(bank[3][:, 0:P], KWT[:, t], v, start=True, stop=True)
                        pe.matmul(bank[3][:, P:2 * P], KWT[:, t], ones, start=True, stop=True).then_inc(m_cn, 1)
                mm.then_inc(m_num, 1)
                pe.wait_ge(m_hq, h + 1)
                pe.matmul(bank[4][:], ones, T2[:], start=True, stop=True).then_inc(m_rms, 1)
            pe.wait_ge(s_hankel, 16)
            pe.wait_ge(m_y, 4)
            for h in range(8):
                if h >= 2:
                    pe.wait_ge(z_flipc, h - 1)
                pe.matmul(bank[6 + h % 2][:], mat(FLIP), HK[:, h, :], start=True, stop=True).then_inc(z_flip, 1)
            pe.wait_ge(z_flipc, 8)
            attention(nsa_units, NF, Pn, PTn, KD, 4)
            pe.wait_ge(a_o, KD + 4)
            for i in range(4):
                for n in range(2):
                    gemm(f"merge{n}_{i}", u1)
                    gemm(f"branch{n}_{i}", lambda k, n=n: S6[:, 4 * n + k, :])
            pair_wait(pe, "branch1_3")
            gemm("w_out", lambda k: S2[:, k, :])
            norm("ffn")
            pe.wait_ge(norm_out, OUT_BEFORE["ffn"])
            for i in range(FF2 // 256):
                gemm(f"gate_{i}", u1)
                gemm(f"up_{i}", u1)
            pair_wait(pe, f"up_{FF2 // 256 - 1}")
            gemm("down", lambda k: slab[2 + k // KD][:, k % KD, :])
            norm("final")
            pe.wait_ge(norm_out, OUT_BEFORE["final"])
            for t in range(NT):
                for half in range(2):
                    n = 2 * t + half
                    if n >= 2:
                        pe.wait_ge(fin_c, n - 1)
                    for k in range(4):
                        mm = pe.transpose(bank[6 + n % 2][:, k * P:(k + 1) * P],
                                          S1[:, 4 * half + k, t * P:(t + 1) * P], ident)
                    mm.then_inc(fin_t, 1)

        @block.scalar
        def _(act):
            count = [0]
            A = nc.scalar.activation

            def link(ins):
                count[0] += 1
                ins.then_inc(achain, 1)
                act.wait_ge(achain, count[0])

            def evac(name, op):
                first, n = pairs[name]
                for i in range(n):
                    j = first + i
                    act.wait_ge(chunk_done, ends[j])
                    for half in range(2):
                        ins = op(2 * i + half, bank[2 * (j % 2) + half][:])
                    ins.then_inc(evacuated[j % 2], 1)

            def norm(name):
                n = NORMS.index(name)
                if X_AFTER[name]:
                    pair_wait(act, X_AFTER[name])
                for k in range(KD):
                    if k >= 2:
                        act.wait_ge(norm_mm, 8 * n + k - 1)
                    A((T1, T2)[k % 2][:], S0[:, k, :], ACT.Square).then_inc(norm_sq, 1)
                act.wait_ge(norm_mm, 8 * (n + 1))
                A(rstd[:], bank[4][:], ACT.Sqrt, bias=eps6, scale=1.0 / D).then_inc(norm_root, 1)

            act.wait_ge(setup_done, 2)
            act.wait_ge(pe_tc, KD)
            norm("rwkv")
            n1 = q = 0
            for i in range(3):
                for part in range(1 if i < 2 else 2):
                    act.wait_ge(lora1, n1 + 1)
                    if i == 2 and part == 0:
                        act.wait_ge(lora2, 2 * KD)
                    m = 64 if i < 2 else (128, 32)[part]
                    A(LH[0:m, i if i < 2 else part, :], bank[4 + n1 % 2][0:m, :],
                      (ACT.Tanh, ACT.Copy, ACT.Sigmoid)[i]).then_inc(lora1_out, 1)
                    n1 += 1
                for e in range(KD):
                    act.wait_ge(lora2, q + 1)
                    b = bank[6 + q % 2][:]
                    if i == 0:
                        ins = A(S4[:, e, :], b, ACT.Sigmoid, bias=par("rwkv_w0", e))
                    elif i == 1:
                        ins = A(S5[:, e, :], b, ACT.Sigmoid, bias=par("rwkv_a0", e))
                    else:
                        ins = A(S6[:, e, :], b, ACT.Copy)
                    ins.then_inc(lora2_out, 1)
                    q += 1
            evac("r", lambda e, b: A(S7[:, e, :], b, ACT.Copy))
            evac("k", lambda e, b: A(S8[:, e, :], b, ACT.Copy))
            evac("v", lambda e, b: A(S1[:, e, :], b, ACT.Copy))

            for e in range(KD):
                act.wait_ge(p_kk, e + 1)
                A(T2[:], T1[:], ACT.Square).then_inc(p_sq, 1)
                act.wait_ge(p_ssq, e + 1)
                A(T2[:], bank[6][:], ACT.Sqrt, scale=float(HD)).then_inc(p_nrm, 1)
                act.wait_ge(p_c, e + 1)
                A(S4[:, e, :], S4[:, e, :], ACT.Exp, scale=-DECAY_UNIT)
                A(T4[:], T3[:], ACT.Exp, scale=-DECAY_UNIT)
                A(cexp, cexp, ACT.Exp, scale=-DECAY_UNIT).then_inc(achain, 1)
                count[0] += 1
                act.wait_ge(achain, count[0])
                A(T3[:], T3[:], ACT.Exp, scale=DECAY_UNIT).then_inc(p_exp, 1)
                act.wait_ge(p_tr, e + 1)
                for w in range(2):
                    A(TM[:, w].rearrange("p c f -> p (c f)"), bank[w][:], ACT.Copy)
                A(S1[:, e, :], bank[2][:], ACT.Copy).then_inc(p_trc, 1)
                for lv in range(6):
                    for hh in range(2):
                        n = (e * 6 + lv) * 2 + hh
                        act.wait_ge(p_x, n + 1)
                        if lv:
                            act.wait_ge(p_d, n - 1)
                        A(XX[:, 4 * hh:4 * hh + 4, :].rearrange("p u n -> p (u n)"), bank[3 * hh][:], ACT.Copy
                          ).then_inc(p_xc, 1)
                for c in range(NT):
                    n = NT * e + c
                    act.wait_ge(p_r, n + 1)
                    A(RT[:], bank[6][:, 0:P], ACT.Copy).then_inc(p_rc, 1)
                    act.wait_ge(p_sa, n + 1)
                    if n:
                        act.wait_ge(p_y, n)
                    A(SA[:], bank[7][:, 0:P], ACT.Copy).then_inc(p_sac, 1)
                act.wait_ge(p_y, NT * (e + 1))
                A(T1[:], bank[1][:], ACT.Copy).then_inc(p_yc, 1)
                act.wait_ge(p_gn, e + 1)
                A(T2[:], T1[:], ACT.Square).then_inc(p_cent, 1)
                act.wait_ge(p_var, e + 1)
                A(T2[:], bank[4][:], ACT.Sqrt, bias=epsg).then_inc(p_gn2, 1)

            def mlp(i):
                norm(f"mlp{i}")

                def relu2(e, b):
                    h = slab[2 + e // KD][:, e % KD, :]
                    link(A(h, b, ACT.Relu))
                    return A(h, h, ACT.Square)
                evac(f"mlp{i}_in", relu2)

            mlp(0)
            norm("kv")
            evac("fk", lambda e, b: A(S3[:, e, :], b, ACT.Copy))
            first, n = pairs["fv"]
            for i in range(n):
                j = first + i
                act.wait_ge(chunk_done, ends[j])
                for half in range(2):
                    ins = A(FV[:, 2 * half:2 * half + 2, 256 * i:256 * i + 256],
                            bank[2 * (j % 2) + half][:].rearrange("p (t n) -> p t n", t=2), ACT.Copy)
                ins.then_inc(evacuated[j % 2], 1)
            evac("fq", lambda e, b: A(S5[:, e, :], b, ACT.Copy))
            act.wait_ge(f_mm, 1)
            act.wait_ge(s_bias, 16)
            link(A(T1[0:16, :], bank[4][0:16, :], ACT.Identity, bias=fb))
            link(A(T2[0:16, :], T1[0:16, :], ACT.Abs))
            link(A(T2[0:16, :], T2[0:16, :], ACT.Exp, scale=-1.0))
            A(T2[0:16, :], T2[0:16, :], ACT.Ln, bias=one1[0:16]).then_inc(f_rows, 1)
            act.wait_ge(f_cum, 1)
            for i in range(KD):
                if i:
                    act.wait_ge(h_mm, i)
                A(T2[:], S3[:, i, :], ACT.Square).then_inc(h_sq, 1)
                act.wait_ge(h_mm, i + 1)
                if i:
                    act.wait_ge(h_out, i)
                A(T3[:], bank[5][:], ACT.Sqrt, bias=eps6).then_inc(h_rt, 1)

            def attention(units, base, Pt, PTt, o_base):
                N = len(units)
                fox = units[0]["mask"]
                for i in range(N + 3):
                    if i < N:
                        u = units[i]
                        if fox and i % 8 == 0:
                            e = u["e"]
                            if e:
                                act.wait_ge(h_mm, KD + e)
                            A(T2[:], S5[:, e, :], ACT.Square).then_inc(h_sq, 1)
                            act.wait_ge(h_mm, KD + e + 1)
                            act.wait_ge(h_out, KD + e)
                            A(T3[:], bank[3][:], ACT.Sqrt, bias=eps6q, scale=64.0).then_inc(h_rt, 1)
                        if u["rowbias"] is not None:
                            h = u["rowbias"]
                            act.wait_ge(a_cb, h + 1)
                            if h >= 2:
                                act.wait_ge(a_l, base + 4 * (h - 1))
                            A(CB[:, h % 2, :], bank[2][:], ACT.Copy).then_inc(a_cbc, 1)
                        act.wait_ge(a_l, base + i + 1)
                        p = Pt[:, i % 3, 0:u["w"]]
                        A(p, p, ACT.Exp, bias=mx[:, i % 3:i % 3 + 1], accum_out=rs[:, i % 3:i % 3 + 1]
                          ).then_inc(a_e, 1)
                    if 1 <= i <= N:
                        n = i - 1
                        u = units[n]
                        act.wait_ge(a_t, base + n + 1)
                        if n >= 2:
                            act.wait_ge(a_pv, base + n - 1)
                        K = N_CMP if u["w"] == N_CMP else P
                        w = P if u["w"] == N_CMP else u["w"]
                        A(PTt[0:K, n % 2, 0:w], bank[6 + n % 2][0:K, 0:w], ACT.Copy).then_inc(a_tc, 1)
                    if 3 <= i and units[i - 3]["ends_e"]:
                        e = units[i - 3]["e"]
                        act.wait_ge(a_pv, base + i - 2)
                        dst = S7[:, e, :] if fox else YN[:, e, :]
                        A(dst, bank[e % 2][:], ACT.Copy).then_inc(a_o, 1)

            attention(fox_units, 0, Pb, PTb, 0)
            mlp(1)
            norm("mix")
            act.wait_ge(s_small_w, 16 * 10)
            evac("mqk", lambda e, b: A(S2[:, e, :], b, ACT.Identity, bias=par("b_mqk", e)))
            pair_wait(act, "mv")
            evac("mo", lambda e, b: A(OG[:, e, :], b, ACT.Sigmoid, bias=par("b_mo", e)))
            pair_wait(act, "vsw")
            act.wait_ge(m_rows, 1)
            A(RI[0:4, :], bank[4][0:4, :], ACT.Identity, bias=small[0:4, 33:34])
            A(RMU[0:4, :], bank[4][32:36, :], ACT.Copy)
            A(GR[0:24, :], bank[4][64:88, :], ACT.Copy).then_inc(m_rowx, 1)
            act.wait_ge(m_rowx2, 1)
            link(A(T2[0:4, :], RMU[0:4, :], ACT.Abs))
            link(A(T2[0:4, :], T2[0:4, :], ACT.Exp, scale=-1.0))
            A(T2[0:4, :], T2[0:4, :], ACT.Ln, bias=one1[0:4])
            A(GR[0:24, :], GR[0:24, :], ACT.Sigmoid, bias=small[0:24, 36:37]).then_inc(m_rowx, 1)
            act.wait_ge(c_mm, 1)
            A(PET[:, :], bank[5][0:64, 0:64], ACT.Copy).then_inc(c_hid, 1)
            act.wait_ge(c_mm, 2)
            link(A(PEH[:], bank[5][:, 128:130], ACT.Copy))
            act.wait_ge(c_mm, 3)
            for g in range(2):
                for j in range(2):
                    ins = A(HID[:, j, g, :], bank[6 + g][:, 32 * j:32 * j + N_CMP], ACT.Silu, bias=PEH[:, j:j + 1])
                ins.then_inc(c_hid, 1)
            act.wait_ge(c_out, 1)
            A(KC[:, 0:N_CMP], bank[5][:, 0:N_CMP], ACT.Copy)
            A(VC[0:N_CMP].rearrange("p g d -> p (g d)"), bank[5][0:N_CMP, 128:256], ACT.Copy).then_inc(z_row, 1)
            act.wait_ge(z_flip, 1)
            for i in range(2):
                A(ROW[:, i * 512:(i + 1) * 512], bank[6 + i][0:8, :], ACT.Copy).then_inc(z_rowc, 1)
            act.wait_ge(m_conv, 8)
            for k in range(8):
                A(S3[:, k, :], S3[:, k, :], ACT.Silu).then_inc(m_silu, 1)
            act.wait_ge(m_rowd, 1)
            A(RSI, RSI, ACT.Exp)
            A(REM, REM, ACT.Exp, scale=-1.0).then_inc(m_rowx, 1)
            act.wait_ge(m_gt, 1)
            A(GC[:].rearrange("p c h -> p (c h)"), bank[4][:, 0:16], ACT.Copy)
            A(GT2[:].rearrange("p c h -> p (c h)"), bank[4][:, 32:128], ACT.Copy).then_inc(m_gtc, 1)
            for h in range(4):
                act.wait_ge(m_b, h + 1)
                A(T3[:], bank[2][:], ACT.Copy)
                act.wait_ge(m_bd, h + 1)
                for c in range(NT):
                    t = slice(c * P, (c + 1) * P)
                    ins = A(T1[:, t], T1[:, t], ACT.Exp, scale=-1.0, bias=GC[:, c, h:h + 1])
                ins.then_inc(m_e, 1)
                act.wait_ge(m_hq1, h + 1)
                A(T2[:], T1[:], ACT.Square).then_inc(m_hq, 1)
                act.wait_ge(m_rms, h + 1)
                A(T2[:], bank[4][:], ACT.Sqrt, bias=eps6, scale=1.0 / P).then_inc(m_rt, 1)
            attention(nsa_units, NF, Pn, PTn, KD)

            def sigs(name, func, bufs, bias, prev):
                first, n = pairs[name]
                if prev is not None:
                    pair_wait(act, prev)
                act.wait_ge(chunk_done, ends[first])
                for half in range(2):
                    b = bank[2 * (first % 2) + half][:]
                    if bias is None:
                        ins = A(bufs[half][:], b, func)
                    else:
                        ins = A(bufs[half][:], b, func, bias=bias[half])
                ins.then_inc(evacuated[first % 2], 1)

            for i in range(4):
                for n in range(2):
                    prev = f"branch{n}_{i - 1}" if i else None
                    sigs(f"merge{n}_{i}", ACT.Sigmoid, (T1, T2) if n == 0 else (T3, T4),
                         [par("b_merge", 8 * n + 2 * i + half) for half in range(2)], prev)
            norm("ffn")
            for i in range(FF2 // 256):
                if i == 1:
                    act.wait_ge(norm_out, OUT_BEFORE["ffn"])
                sigs(f"gate_{i}", ACT.Silu, (T1, T2) if i % 2 == 0 else (T3, T4), None,
                     f"up_{i - 2}" if i >= 2 else None)
            norm("final")
            for n in range(2 * NT):
                act.wait_ge(fin_t, n + 1)
                A(S2[:, n, :], bank[6 + n % 2][:], ACT.Copy).then_inc(fin_c, 1)

        @block.vector
        def _(dve):
            V = nc.vector
            count = [0]

            def link(ins):
                count[0] += 1
                ins.then_inc(dchain, 1)
                dve.wait_ge(dchain, count[0])

            def evac(name, op):
                first, n = pairs[name]
                for i in range(n):
                    j = first + i
                    dve.wait_ge(chunk_done, ends[j])
                    for half in range(2):
                        ins = op(2 * i + half, bank[2 * (j % 2) + half][:])
                    ins.then_inc(evacuated[j % 2], 1)

            def residual(name):
                evac(name, lambda e, b: V.tensor_tensor(S0[:, e, :], b, S0[:, e, :], ALU.add))

            def norm(name, outs):
                n = NORMS.index(name)
                dve.wait_ge(norm_root, n + 1)
                link(V.reciprocal(rstd[:], rstd[:]))
                for dst, gain in outs:
                    for k in range(KD):
                        V.scalar_tensor_tensor(out=dst[:, k, :], in0=S0[:, k, :], scalar=gain(k), in1=rstd[:],
                                               op0=ALU.mult, op1=ALU.mult).then_inc(norm_out, 1)

            V.memset(S4[:, 0:3, 0:P], 0.0).then_inc(setup_done, 1)
            V.memset(eps6, EPS)
            V.memset(eps6q, EPS * 64)
            V.memset(epsg, GN_EPS)
            V.memset(one1, 1.0).then_inc(setup_done, 1)
            for k in range(KD):
                dve.wait_ge(pe_t, k + 1)
                V.tensor_copy(S0[:, k, :], bank[4 + k % 2][:]).then_inc(pe_tc, 1)
            dve.wait_ge(pe_t, KD + 1)
            link(V.tensor_copy(PK[:], bank[6][:, 0:3 * P]))
            r0 = rows["rwkv_k_a"][0]
            V.tensor_scalar(omka, PK[:, r0:r0 + 8], -1.0, 1.0, ALU.mult, ALU.add)
            norm("rwkv", [(S1, lambda k: par("rwkv_norm_g", k))])
            dve.wait_ge(norm_out, KD)
            V.tensor_scalar(S2[:, :, 0:1], S1[:, :, 0:1], -1.0, None, ALU.mult)
            link(V.tensor_tensor(S2[:, :, 1:T], S1[:, :, 0:T - 1], S1[:, :, 1:T], ALU.subtract))
            for n, m in enumerate((1, 4, 5, 0, 2, 3)):
                if n >= 1:
                    if n <= 3:
                        dve.wait_ge(lora1, (1, 2, 4)[n - 1])
                    else:
                        dve.wait_ge(chunk_done, ends[sum(pairs["rk"[n - 4]]) - 1])
                for k in range(KD):
                    ins = V.scalar_tensor_tensor(out=S3[:, k, :], in0=S2[:, k, :], scalar=par("rwkv_mu", 8 * m + k),
                                                 in1=S1[:, k, :], op0=ALU.mult, op1=ALU.add)
                ins.then_inc(mix_ready, 1)
            pair_wait(dve, "v")

            V.memset(SS[:], 0.0)

            def bc(ap, n):
                return ap.unsqueeze(2).broadcast_to([P, NT, n])

            for e in range(KD):
                if e:
                    dve.wait_ge(p_out, e)
                V.tensor_scalar(T1[:], S8[:, e, :], par("rwkv_k_k", e), None, ALU.mult).then_inc(p_kk, 1)
                for c in range(NT):
                    t = slice(c * P, (c + 1) * P)
                    ins = V.tensor_tensor_scan(T3[:, t], ones, S4[:, e, t], 0.0, ALU.mult, ALU.add)
                link(ins)
                V.tensor_copy(cmid, c4(T3[:])[:, :, P // 2 - 1])
                link(V.tensor_copy(cend, c4(T3[:])[:, :, P - 1]))
                link(V.tensor_tensor(c4(T3[:]), c4(T3[:]), bc(cmid, P), ALU.subtract))
                V.tensor_tensor(S4[:, e, :], T3[:], S4[:, e, :], ALU.subtract)
                link(V.tensor_tensor(cexp, cend, cmid, ALU.subtract))
                V.tensor_tensor(cexp[:, 0:3], cexp[:, 0:3], cmid[:, 1:4], ALU.add).then_inc(p_c, 1)
                dve.wait_ge(p_nrm, e + 1)
                link(V.tensor_scalar(T2[:], T2[:], 1e-12, None, ALU.max))
                link(V.reciprocal(T2[:], T2[:]))
                link(V.tensor_tensor(T1[:], T1[:], T2[:], ALU.mult))
                dve.wait_ge(p_exp, e + 1)
                V.scalar_tensor_tensor(out=AR[:, :, 0, :], in0=c4(T1[:]), scalar=-1.0, in1=c4(S4[:, e, :]),
                                       op0=ALU.mult, op1=ALU.mult)
                V.tensor_tensor(AR[:, :, 1, :], c4(S7[:, e, :]), c4(T4[:]), ALU.mult)
                V.tensor_scalar(T2[:], S5[:, e, :], par("rwkv_k_a", e), omka[:, e:e + 1], ALU.mult, ALU.add)
                link(V.tensor_tensor(T1[:], T1[:], S5[:, e, :], ALU.mult))
                V.tensor_tensor(BK[:, 0, :], T1[:], T3[:], ALU.mult)
                link(V.tensor_tensor(S8[:, e, :], S8[:, e, :], T2[:], ALU.mult))
                V.tensor_tensor(BK[:, 1, :], S8[:, e, :], T3[:], ALU.mult)
                V.scalar_tensor_tensor(out=T2[:], in0=S7[:, e, :], scalar=par("rwkv_r_k", e), in1=S8[:, e, :],
                                       op0=ALU.mult, op1=ALU.mult).then_inc(p_bon, 1)
                dve.wait_ge(p_bonmm, e + 1)
                V.scalar_tensor_tensor(out=S5[:, e, :], in0=bank[7][:], scalar=float(HD), in1=S1[:, e, :],
                                       op0=ALU.mult, op1=ALU.mult).then_inc(p_bon_done, 1)
                keep = mat(AFTER, 2)
                for w, dst in ((0, BB), (1, KM)):
                    dve.wait_ge(p_prod, 3 * e + w + 1)
                    for b in range(4):
                        ins = V.tensor_tensor(dst[:, 2 * b:2 * b + 2, :],
                                              bank[b][:].rearrange("p (u n) -> p u n", u=2),
                                              keep.unsqueeze(1).broadcast_to([P, 2, 256]), ALU.mult)
                    ins.then_inc(p_prodc, 1)
                dve.wait_ge(p_prod, 3 * e + 3)
                for hh in range(2):
                    V.tensor_tensor(MM[:, 4 * hh:4 * hh + 4, 0:P], c4(bank[4 + hh][:]),
                                    mat(LEVEL).unsqueeze(1).broadcast_to([P, 4, P]), ALU.mult)
                dve.wait_ge(p_prodc, 3 * e + 1)
                link(V.tensor_tensor(MM[:, :, P:2 * P], BB[:, :, 0:P],
                                     mat(LEVEL + 1).unsqueeze(1).broadcast_to([P, 8, P]), ALU.mult))
                for w in range(2):
                    ins = V.tensor_tensor(MM[:, :, w * P:(w + 1) * P], MM[:, :, w * P:(w + 1) * P],
                                          ident.unsqueeze(1).broadcast_to([P, 8, P]), ALU.add)
                ins.then_inc(p_prodc, 1)
                for lv in range(6):
                    lm = mat(LEVEL + 2 + 2 * lv, 2)
                    for hh in range(2):
                        n = (e * 6 + lv) * 2 + hh
                        dve.wait_ge(p_d, n + 1)
                        for b in range(2):
                            bb = bank[3 * hh + 1 + b][:].rearrange("p (u n) -> p u n", u=2)
                            ins = V.tensor_tensor(bb, bb, lm.unsqueeze(1).broadcast_to([P, 2, 256]), ALU.mult)
                        link(ins)
                        for b in range(2):
                            bb = bank[3 * hh + 1 + b][:].rearrange("p (u n) -> p u n", u=2)
                            mm = MM[:, 4 * hh + 2 * b:4 * hh + 2 * b + 2, :]
                            ins = V.tensor_tensor(mm, bb, mm, ALU.add)
                        ins.then_inc(p_dc, 1)
                for c in range(NT - 1):
                    n = 3 * e + c
                    dve.wait_ge(p_st, n + 1)
                    dve.wait_ge(p_y, NT * e + c + 1)
                    for hh in range(2):
                        s = slice(64 * hh, 64 * hh + 64)
                        if c == 0:
                            ins = V.tensor_scalar(SS[s, s], bank[2][s, s], cexp[s, 0:1], None, ALU.mult)
                        else:
                            ins = V.tensor_tensor(SS[s, s], bank[2][s, s], SS[s, s], ALU.add)
                    if c:
                        link(ins)
                        ins = V.tensor_scalar(SS[:], SS[:], cexp[:, c:c + 1], None, ALU.mult)
                    ins.then_inc(p_stc, 1)
                dve.wait_ge(p_mean, e + 1)
                V.tensor_tensor(T1[:], T1[:], bank[3][:], ALU.subtract).then_inc(p_gn, 1)
                dve.wait_ge(p_gn2, e + 1)
                link(V.reciprocal(T2[:], T2[:]))
                link(V.tensor_tensor(T1[:], T1[:], T2[:], ALU.mult))
                link(V.tensor_scalar(T1[:], T1[:], par("rwkv_lnx_w", e), par("rwkv_lnx_b", e), ALU.mult, ALU.add))
                link(V.tensor_tensor(T1[:], T1[:], S5[:, e, :], ALU.add))
                V.tensor_tensor(S7[:, e, :], T1[:], S6[:, e, :], ALU.mult).then_inc(p_out, 1)
            residual("rwkv_o")
            norm("mlp0", [(S1, lambda k: par("mlp_norm_g", k))])
            residual("mlp0_out")
            norm("kv", [(S1, lambda k: par("kv_norm_g", k)), (S2, lambda k: par("attn_norm_g", k))])
            dve.wait_ge(f_rows, 1)
            link(V.tensor_scalar(T1[0:16, :], T1[0:16, :], 0.0, None, ALU.min))
            link(V.tensor_tensor(T2[0:16, :], T2[0:16, :], T1[0:16, :], ALU.subtract))
            for q in QZ:
                V.memset(q[64:128, 0, :], 0.0)
                V.memset(q[0:64, 1, :], 0.0)
            link(V.memset(T3[0:16, :], 1.0))
            V.tensor_tensor_scan(NC, T3[0:16, :], T2[0:16, :], 0.0, ALU.mult, ALU.add).then_inc(f_cum, 1)
            for e in range(KD):
                dve.wait_ge(h_rt, e + 1)
                link(V.reciprocal(T3[:], T3[:]))
                V.scalar_tensor_tensor(out=S3[:, e, :], in0=S3[:, e, :], scalar=par("k_norm_g", e), in1=T3[:],
                                       op0=ALU.mult, op1=ALU.mult).then_inc(h_out, 1)

            def attention(units, base, Pt, PTt):
                N = len(units)
                fox = units[0]["mask"]
                for i in range(N + 1):
                    if i < N:
                        u = units[i]
                        if fox and i % 8 == 0:
                            e = u["e"]
                            dve.wait_ge(h_rt, KD + e + 1)
                            link(V.reciprocal(T3[:], T3[:]))
                            if e >= 2:
                                dve.wait_ge(a_s, 8 * (e - 1))
                            for hh in range(2):
                                s = slice(64 * hh, 64 * hh + 64)
                                ins = V.scalar_tensor_tensor(out=QZ[e % 2][s, hh, :], in0=S5[s, e, :],
                                                             scalar=par("q_norm_g", e)[s], in1=T3[s, :],
                                                             op0=ALU.mult, op1=ALU.mult)
                            ins.then_inc(h_out, 1)
                        if u["rowbias"] is not None:
                            dve.wait_ge(a_cbc, u["rowbias"] + 1)
                        dve.wait_ge(a_s, base + i + 1)
                        if i >= 3:
                            dve.wait_ge(a_t, base + i - 2)
                        p = Pt[:, i % 3, 0:u["w"]]
                        m = mx[:, i % 3:i % 3 + 1]
                        link(V.tensor_tensor_reduce(p, bank[4 + i % 2][:, 0:u["w"]], u["bias"], 1.0, -3e38,
                                                    ALU.add, ALU.max, m))
                        V.tensor_scalar(m, m, -1e20, -1.0, ALU.max, ALU.mult).then_inc(a_l, 1)
                    if i >= 1:
                        n = i - 1
                        u = units[n]
                        dve.wait_ge(a_e, base + n + 1)
                        r = rs[:, n % 3:n % 3 + 1]
                        p = Pt[:, n % 3, 0:u["w"]]
                        if u["clamp"]:
                            link(V.tensor_scalar(r, r, 1e-30, None, ALU.max))
                        link(V.reciprocal(r, r))
                        if u["gate"] is None:
                            V.tensor_scalar(p, p, r, None, ALU.mult).then_inc(a_p, 1)
                        else:
                            V.tensor_scalar(p, p, r, u["gate"], ALU.mult, ALU.mult).then_inc(a_p, 1)

            attention(fox_units, 0, Pb, PTb)
            residual("fox_o")
            norm("mlp1", [(S1, lambda k: par("mlp_norm_g", 8 + k))])
            residual("mlp1_out")
            V.memset(TB[32:33, :], NEG)
            V.memset(WSM, 0.0).then_inc(s_wz, 1)
            norm("mix", [(S1, lambda k: par("g_norm_mix_2", k))])
            dve.wait_ge(s_small_w, 16 * 10)

            def evac_tm(name, dst, bias):
                first, n = pairs[name]
                for i in range(n):
                    j = first + i
                    dve.wait_ge(chunk_done, ends[j])
                    for half in range(2):
                        ins = V.tensor_tensor(dst[:, 2 * half:2 * half + 2, 256 * i:256 * i + 256],
                                              bank[2 * (j % 2) + half][:].rearrange("p (t n) -> p t n", t=2),
                                              bias[:, 256 * i:256 * i + 256].unsqueeze(1).broadcast_to([P, 2, 256]),
                                              ALU.add)
                    ins.then_inc(evacuated[j % 2], 1)

            evac_tm("mv", MVT, BMV[:])
            evac("nq", lambda e, b: V.tensor_scalar(NQT[:, e, :], b, par("b_nq", e), HD ** -0.5, ALU.add, ALU.mult))
            evac("kvc", lambda e, b: V.tensor_scalar(KVC[:, e, :], b, par("b_nkv", e), None, ALU.add))
            evac("ksw", lambda e, b: V.tensor_scalar((KS, KW)[e], b, par("b_nkv", 2 + 2 * e), None, ALU.add))
            evac_tm("vsw", VSW, BVS)
            dve.wait_ge(m_rowx, 1)
            V.tensor_scalar(RMU, RMU, small[0:4, 34:35], small[0:4, 35:36], ALU.add, ALU.add).then_inc(m_rowx2, 1)
            dve.wait_ge(m_rowx, 2)
            link(V.tensor_scalar(RMU, RMU, 0.0, None, ALU.min))
            link(V.tensor_tensor(RMU, RMU, T2[0:4, :], ALU.subtract))
            for c in range(NT):
                t = slice(c * P, (c + 1) * P)
                ins = V.tensor_tensor_scan(REM[:, t], ones[0:4, :], RMU[:, t], 0.0, ALU.mult, ALU.add)
            link(ins)
            link(V.tensor_tensor(RG, RI, REM, ALU.subtract))
            link(V.memset(small[0:4, 40:41], 0.0))
            for c in range(NT):
                t = slice(c * P, (c + 1) * P)
                mp = small[0:4, 40 + c:41 + c]
                link(V.tensor_tensor_scan(RMU[:, t], RG[:, t], RG[:, t], mp, ALU.max, ALU.max))
                V.tensor_scalar(RSI[:, t], RMU[:, t], mp, -1.0, ALU.subtract, ALU.mult)
                ins = V.tensor_tensor(REM[:, t], REM[:, t], RMU[:, t], ALU.add)
                if c < NT - 1:
                    link(ins)
                    link(V.tensor_copy(small[0:4, 41 + c:42 + c], REM[:, (c + 1) * P - 1:(c + 1) * P]))
            ins.then_inc(m_rowd, 1)
            pair_wait(dve, "mo")
            for k in range(8):
                link(V.tensor_scalar(S3[:, k, :], S2[:, k, :], par("conv_qk_2", 24 + k), None, ALU.mult))
                for j in (2, 1, 0):
                    d = 3 - j
                    ins = V.scalar_tensor_tensor(out=S3[:, k, d:T], in0=S2[:, k, 0:T - d],
                                                 scalar=par("conv_qk_2", 8 * j + k), in1=S3[:, k, d:T],
                                                 op0=ALU.mult, op1=ALU.add)
                    if j:
                        link(ins)
                ins.then_inc(m_conv, 1)
            for k in range(4, 8):
                dve.wait_ge(m_silu, k + 1)
                ins = V.tensor_scalar(S3[:, k, :], S3[:, k, :], P ** -0.5, None, ALU.mult)
            ins.then_inc(m_kscaled, 1)
            dve.wait_ge(m_kscaled, 1)
            for h in range(4):
                dve.wait_ge(m_b, h + 1)
                V.tensor_tensor(c4(T1[:]), c4(bank[4][:]), mat(LATE_POS).unsqueeze(1).broadcast_to([P, 4, P]),
                                ALU.add).then_inc(m_bd, 1)
                V.tensor_tensor(QS[:], S3[:, h, :], bank[6][:], ALU.mult)
                V.tensor_copy(DC[:], c4(bank[6][:])[:, :, P - 1])
                dve.wait_ge(m_e, h + 1)
                dve.wait_ge(m_kt, h + 1)
                V.tensor_tensor(PM[:], T1[:], bank[5][:], ALU.mult)
                for c in range(NT):
                    t = slice(c * P, (c + 1) * P)
                    ins = V.tensor_scalar(KWT[:, t], bank[7][:, t], T1[:, (c + 1) * P - 1:(c + 1) * P], None, ALU.mult)
                ins.then_inc(m_pd, 1)
                for c in range(NT - 1):
                    dve.wait_ge(m_cn, 3 * h + c + 1)
                    if c == 0:
                        ins = V.tensor_copy(CN[:, 1, :], bank[3][:, 0:256])
                    else:
                        ins = V.scalar_tensor_tensor(out=CN[:, c + 1, :], in0=CN[:, c, :], scalar=DC[:, c:c + 1],
                                                     in1=bank[3][:, 0:256], op0=ALU.mult, op1=ALU.add)
                    ins.then_inc(m_cnd, 1)
                    dve.wait_ge(m_cnd, 3 * h + c + 1)
                dve.wait_ge(m_num, h + 1)
                link(V.scalar_tensor_tensor(out=T3[:], in0=bank[1][:], scalar=-1.0, in1=T3[:],
                                            op0=ALU.mult, op1=ALU.max))
                link(V.tensor_tensor(T3[:], bank[1][:], T3[:], ALU.max))
                link(V.reciprocal(T3[:], T3[:]))
                V.tensor_tensor(T1[:], bank[0][:], T3[:], ALU.mult).then_inc(m_hq1, 1)
                dve.wait_ge(m_rt, h + 1)
                link(V.reciprocal(T2[:], T2[:]))
                link(V.tensor_tensor(T1[:], T1[:], T2[:], ALU.mult))
                V.scalar_tensor_tensor(out=YM[:, h, :], in0=T1[:], scalar=par("g_mlstm_head_2", h), in1=OG[:, h, :],
                                       op0=ALU.mult, op1=ALU.mult).then_inc(m_y, 1)
            for h in range(8):
                dve.wait_ge(z_flip, h + 2)
                V.memset(Z[h][:, 512:896], NEG)
                V.tensor_copy(Z[h][:, 0:512], bank[6 + h % 2][:]).then_inc(z_flipc, 1)
            dve.wait_ge(m_gtc, 1)
            attention(nsa_units, NF, Pn, PTn)
            for i in range(4):
                for n in range(2):
                    bufs = (T1, T2) if n == 0 else (T3, T4)
                    pair_wait(dve, f"merge{n}_{i}")
                    j = pairs[f"branch{n}_{i}"][0]
                    dve.wait_ge(chunk_done, ends[j])
                    for half in range(2):
                        b = bank[2 * (j % 2) + half][:]
                        if n == 0:
                            ins = V.tensor_tensor(S2[:, 2 * i + half, :], b, bufs[half][:], ALU.mult)
                        else:
                            link(V.tensor_tensor(bufs[half][:], b, bufs[half][:], ALU.mult))
                            ins = V.tensor_tensor(S2[:, 2 * i + half, :], S2[:, 2 * i + half, :], bufs[half][:],
                                                  ALU.add)
                    ins.then_inc(evacuated[j % 2], 1)
            residual("w_out")
            norm("ffn", [(S1, lambda k: par("g_norm_ffn_2", k))])
            for i in range(FF2 // 256):
                bufs = (T1, T2) if i % 2 == 0 else (T3, T4)
                pair_wait(dve, f"gate_{i}")
                j = pairs[f"up_{i}"][0]
                dve.wait_ge(chunk_done, ends[j])
                for half in range(2):
                    t = 2 * i + half
                    ins = V.tensor_tensor(slab[2 + t // KD][:, t % KD, :], bank[2 * (j % 2) + half][:],
                                          bufs[half][:], ALU.mult)
                ins.then_inc(evacuated[j % 2], 1)
            residual("down")
            norm("final", [(S1, lambda k: par("g_final_2", k))])


NAMES = ["x", "rwkv_norm_g", "rwkv_mu", "rwkv_w_rkv", "rwkv_w0", "rwkv_w1", "rwkv_w2", "rwkv_a0", "rwkv_a1",
         "rwkv_a2", "rwkv_g1", "rwkv_g2", "rwkv_k_k", "rwkv_k_a", "rwkv_r_k", "rwkv_lnx_w", "rwkv_lnx_b",
         "rwkv_w_o", "kv_norm_g", "kv_w", "kv_f_bias", "k_norm_g", "attn_norm_g", "attn_w_q", "q_norm_g",
         "attn_w_o", "mlp_norm_g", "mlp_w_in", "mlp_w_out", "g_norm_mix_2", "w_in_2", "b_in_2", "b_fgate_2",
         "conv_qk_2", "g_mlstm_head_2", "pe_cmp_2", "w_cmp1_2", "w_cmp2_2", "rel_bias_2", "w_branch_2",
         "w_out_2", "g_norm_ffn_2", "w_gate_2", "w_up_2", "w_down_2", "g_final_2"]


def kernel(**inputs):
    import concourse.bacc as bacc
    from concourse.bass_utils import run_bass_kernel_spmd

    nc = bacc.Bacc("TRN2", target_bir_lowering=False, num_devices=1)
    arrays, aps = {}, {}
    given = {n: np.ascontiguousarray(inputs[n]) for n in NAMES}
    given.update(constants())
    for name, v in given.items():
        arrays[f"in_{name}"] = v
        aps[name] = nc.dram_tensor(f"in_{name}", v.shape, mybir.dt.from_np(v.dtype), kind="ExternalInput").ap()
    out = nc.dram_tensor("out_0", (1, T, D), F32, kind="ExternalOutput").ap()
    scratch = nc.dram_tensor("rel_scratch", (8, 1024), F32, kind="Internal").ap()
    build(nc, aps, out, scratch)
    r = run_bass_kernel_spmd(nc, [arrays], core_ids=[0])
    return r.results[0]["out_0"]
```

```python
import math
from contextlib import ExitStack

import numpy as np
import concourse.bass as bass
from concourse import mybir
from concourse.alu_op_type import AluOpType as ALU

ACT = mybir.ActivationFunctionType
F32 = mybir.dt.float32
AX_X = mybir.AxisListType.X

P = 128
T = 512
D = 1024
KD = D // P
NT = T // P
CHUNK = 128
HD = 64
EPS = 1e-6
GN_EPS = 64e-5
FF1 = 4096
FF2 = 2816
NEG = -1e30
DECAY_UNIT = math.exp(-0.5)

MQ, MK, MV, MO, MI, MF, NQ, NKV, NG, MERGE = 0, 512, 1024, 1536, 2048, 2052, 2056, 2568, 3336, 3360
N_CMP = (T - 32) // 16 + 1
REL_N = 1023

IDENT, ONES, HALFMEAN, FLIP, CAUSAL_NEG, LATE_POS, AFTER, FROM, LEVEL = 0, 1, 2, 3, 4, 5, 6, 7, 8
SLOTS = 4


def constants():
    a = np.arange(P)
    i, j = a[:, None], a[None, :]
    mats = [
        i == j,
        np.ones((P, P)),
        (i // HD == j // HD) / HD,
        i + j == P - 1,
        np.where(j > i, NEG, 0.0),
        np.where(i > j, -NEG, 0.0),
        j > i,
        j >= i,
    ]
    for s in (1, 2, 4, 8, 16, 32, 64):
        low = (i // (2 * s) == j // (2 * s)) & ((i // s) % 2 == 1) & ((j // s) % 2 == 0)
        mats += [low, low.T]
    cmat = np.stack([np.asarray(m, np.float32) for m in mats], 1).reshape(P, -1)
    sel = np.repeat(np.eye(16, dtype=np.float32), P, axis=1)
    dist = 511 - np.arange(1024)
    n = np.maximum(dist, 0)
    nf = np.maximum(n, 1).astype(np.float32)
    large = 16 + (np.log(nf / 16) / np.float32(math.log(64)) * 16).astype(np.int32)
    bucket = np.where(n < 16, n, np.minimum(large, 31))
    onehot = np.zeros((33, 1024), np.float32)
    onehot[bucket, np.arange(1024)] = dist >= 0
    onehot[32] = dist < 0
    return {"c_mat": cmat, "c_sel": sel, "c_onehot": onehot}


def param_rows():
    spec = [("rwkv_norm_g", 8), ("rwkv_mu", 48), ("rwkv_w0", 8), ("rwkv_a0", 8), ("rwkv_k_k", 8),
            ("rwkv_k_a", 8), ("rwkv_r_k", 8), ("rwkv_lnx_w", 8), ("rwkv_lnx_b", 8),
            ("kv_norm_g", 8), ("attn_norm_g", 8),
            ("k_norm_g", 8), ("q_norm_g", 8), ("mlp_norm_g", 16), ("g_norm_mix_2", 8),
            ("b_mqk", 8), ("b_mo", 4), ("b_nq", 4), ("b_nkv", 6), ("b_merge", 16),
            ("conv_qk_2", 32), ("g_mlstm_head_2", 4), ("g_norm_ffn_2", 8), ("g_final_2", 8)]
    place, at = {}, 0
    for name, n in spec:
        if at // P != (at + n - 1) // P:
            at = (at // P + 1) * P
        place[name] = (at, n)
        at += n
    assert at <= 3 * P
    return place


N_PAR = len(param_rows()) + 1


def build(nc, a, out, scratch):
    ctx = ExitStack()
    with ctx:
        def sb(name, shape):
            return ctx.enter_context(nc.sbuf_tensor(name, shape, F32))

        def sem(name):
            return ctx.enter_context(nc.semaphore(name))

        SL = sb("slabs", [P, 9, KD, T])
        slab = [SL[:, i] for i in range(9)]
        ring = sb("ring", [P, SLOTS, KD, 256])
        cmat = sb("cmat", [P, 22, P])
        PK = sb("PK", [P, 3 * P])
        T1, T2, T3, T4 = (sb(f"T{i}", [P, T]) for i in (1, 2, 3, 4))
        AR = sb("AR", [P, NT, 2, P])
        BK = sb("BK", [P, 2, T])
        CE = sb("CE", [P, KD, 4])
        SS = sb("SS", [P, P])
        RT = sb("RT", [P, P])
        SA = sb("SA", [P, P])
        small = sb("small", [P, 64])
        eps6, eps6q, epsg, one1 = (small[:, i:i + 1] for i in range(4))
        omka = small[:, 4:12]
        cmid = small[:, 12:16]
        cend = small[:, 16:20]
        bank = [ctx.enter_context(nc.psum_tensor(f"bank{i}", [P, T], F32)) for i in range(8)]

        rows = param_rows()

        def par(name, i=0):
            r = rows[name][0] + i
            return PK[:, r:r + 1]

        def mat(i, n=1):
            return cmat[:, i:i + n, :].rearrange("p a b -> p (a b)")

        def c4(ap):
            return ap.rearrange("p (c t) -> p c t", t=CHUNK)

        S0, S1, S2, S3, S4, S5, S6, S7, S8 = slab
        rstd = T4

        def flat(s):
            return s[:].rearrange("p k t -> p (k t)")

        stream = []
        pairs = {}
        ends = []
        pair_chunks = []
        n_pairs = [0]

        def chunk(parts, nk):
            g = len(stream)
            stream.append((g % SLOTS, [(ring[:, g % SLOTS, 0:nk, c0:c0 + src.shape[-1]], src)
                                       if len(src.shape) == 3 else (dst_of(g % SLOTS, nk, c0), src)
                                       for c0, src in parts], nk))
            return g

        def dst_of(slot, nk, c0):
            return ring[:, slot, 0:nk, c0:c0 + P].rearrange("p k (g d) -> p k g d", g=2)

        def add_pair(name, k_tiles, parts_of):
            j = n_pairs[0]
            if name in pairs and pairs[name][0] + pairs[name][1] == j:
                pairs[name] = (pairs[name][0], pairs[name][1] + 1)
            else:
                pairs[name] = (j, 1)
            mine = []
            for k0 in range(0, k_tiles, KD):
                nk = min(KD, k_tiles - k0)
                mine.append((chunk(parts_of(k0, nk), nk), k0, nk))
            pair_chunks.append(mine)
            ends.append(len(stream))
            n_pairs[0] += 1

        def cols(w, c0, n=256):
            return lambda k0, nk: [(0, w[k0 * P:(k0 + nk) * P, c0:c0 + n].rearrange("(k p) n -> p k n", p=P))]

        def gemm_plan(name, w, k_tiles, c0, n):
            for i in range(n // 256):
                add_pair(name, k_tiles, cols(w, c0 + 256 * i))

        w_rkv = a["rwkv_w_rkv"][0]
        gemm_plan("r", w_rkv[0], KD, 0, D)
        gemm_plan("k", w_rkv[1], KD, 0, D)
        gemm_plan("v", w_rkv[2], KD, 0, D)
        gemm_plan("rwkv_o", a["rwkv_w_o"][0], KD, 0, D)
        gemm_plan("mlp0_in", a["mlp_w_in"][0], KD, 0, FF1)
        gemm_plan("mlp0_out", a["mlp_w_out"][0], FF1 // P, 0, D)
        gemm_plan("fk", a["kv_w"], KD, 0, D)
        gemm_plan("fv", a["kv_w"], KD, D, D)
        gemm_plan("fq", a["attn_w_q"][0], KD, 0, D)
        gemm_plan("fox_o", a["attn_w_o"][0], KD, 0, D)
        gemm_plan("mlp1_in", a["mlp_w_in"][1], KD, 0, FF1)
        gemm_plan("mlp1_out", a["mlp_w_out"][1], FF1 // P, 0, D)
        w_in = a["w_in_2"][0]
        gemm_plan("mqk", w_in, KD, MQ, 1024)
        gemm_plan("mv", w_in, KD, MV, 512)
        gemm_plan("mo", w_in, KD, MO, 512)
        nq_src = w_in[:, NQ:NQ + 512].rearrange("(k p) (g r d) -> r p k g d", p=P, g=2, r=4)

        def two(c0, c1):
            def parts(k0, nk):
                return [(0, w_in[:, c0:c0 + P].rearrange("(k p) n -> p k n", p=P)),
                        (P, w_in[:, c1:c1 + P].rearrange("(k p) n -> p k n", p=P))]
            return parts

        def nq_tile(slot_col, r):
            return [(slot_col + 64 * g, w_in[:, NQ + 256 * g + 64 * r:NQ + 256 * g + 64 * r + 64]
                     .rearrange("(k p) n -> p k n", p=P)) for g in range(2)]

        for i in range(2):
            add_pair("nq", KD, lambda k0, nk, i=i: nq_tile(0, 2 * i) + nq_tile(P, 2 * i + 1))
        add_pair("kvc", KD, two(NKV, NKV + 128))
        add_pair("ksw", KD, two(NKV + 256, NKV + 512))
        add_pair("vsw", KD, two(NKV + 384, NKV + 640))
        w_br = a["w_branch_2"][0]

        def branch_cols(n, c0):
            if n == 0:
                return lambda k0, nk: [(0, w_br[0][:, c0:c0 + 256].rearrange("(k p) n -> p k n", p=P))]
            return lambda k0, nk: [(0, w_br[1][:, c0:c0 + 256])]

        for i in range(4):
            for n in range(2):
                add_pair(f"merge{n}_{i}", KD, cols(w_in, MERGE + D * n + 256 * i))
                add_pair(f"branch{n}_{i}", 4, branch_cols(n, 256 * i))
        gemm_plan("w_out", a["w_out_2"][0], KD, 0, D)
        for i in range(FF2 // 256):
            add_pair(f"gate_{i}", KD, cols(a["w_gate_2"][0], 256 * i))
            add_pair(f"up_{i}", KD, cols(a["w_up_2"][0], 256 * i))
        gemm_plan("down", a["w_down_2"][0], FF2 // P, 0, D)

        loads, landed, total = [], [], [0] * SLOTS
        for slot, parts, nk in stream:
            dmas = []
            for dst, src in parts:
                if len(src.shape) == 2 or src.shape[0] == 512:
                    for g in range(2):
                        dmas.append((ring[64 * g:64 * g + 64, slot, 0:4, :],
                                     src[256 * g:256 * g + 256, :].rearrange("(r d) n -> d r n", d=64)))
                else:
                    dmas.append((dst, src))
            total[slot] += 16 * len(dmas)
            loads.append(dmas)
            landed.append(total[slot])

        s_const, s_x, s_par, s_lora, s_ffw, s_small_w, s_sel, s_cmp, s_bias = (
            sem(n) for n in ("const_loaded", "x_loaded", "params_loaded", "lora_loaded", "fgate_w_loaded",
                             "small_w_loaded", "sel_loaded", "cmp_w_loaded", "bias_rows_loaded"))
        s_oh, s_relst, s_hankel, s_wz = (sem(n) for n in ("onehot_loaded", "rel_stored", "hankel_loaded",
                                                          "small_w_zeroed"))
        slot_loaded = [sem(f"slot{i}_loaded") for i in range(SLOTS)]
        chunk_done = sem("chunk_multiplied")
        evacuated = [sem(f"pair_evacuated{i}") for i in range(2)]
        pe_t, pe_tc = sem("turned"), sem("turned_copied")
        norm_sq, norm_mm, norm_root, norm_out = (sem(n) for n in ("norm_squared", "norm_summed", "norm_rooted",
                                                                  "norm_written"))
        dchain, achain = sem("vector_chain"), sem("scalar_chain")
        mix_ready, lora1, lora1_out, lora2 = (sem(n) for n in ("mix_written", "lora1_done",
                                                                         "lora1_evacuated", "lora2_done"))
        lora2_out = sem("lora2_evacuated")
        setup_done = sem("setup_done")
        (p_kk, p_sq, p_c, p_exp, p_fm, p_x, p_xc, p_d, p_dc, p_t, p_tc, p_i, p_it, p_ic, p_ns,
         p_r, p_rc, p_sa, p_sac, p_st, p_stc, p_y, p_yc, p_cen2, p_out) = (
            sem("rwkv_" + n) for n in (
                "kk_raw", "kk_squared", "logs", "exps", "factors",
                "x", "x_copied", "d", "d_added", "m_turned", "m_turned_copied", "start_t", "start_turned",
                "start_copied", "n_masked", "r", "r_copied", "sa", "sa_copied", "state", "state_updated",
                "y", "y_copied", "centred_squared", "out"))
        aux_filled = sem("aux_filled")
        aux_evac = [sem(f"aux_evacuated{i}") for i in range(2)]
        (h_sq, h_mm, h_rt, h_out) = (sem("headnorm_" + n) for n in ("squared", "summed", "rooted", "written"))
        (f_mm, f_rows, f_row2, f_cum) = (sem("fgate_" + n) for n in ("product", "rows", "row_parts", "summed"))
        (a_cb, a_cbc, a_s, a_l, a_e, a_p, a_t, a_tc, a_pv, a_o) = (
            sem("attn_" + n) for n in ("rowbias", "rowbias_copied", "scores", "logits", "exp", "probs", "turned",
                                       "turned_copied", "pv", "out_copied"))
        (m_conv, m_silu, m_rows, m_rowx, m_rowd, m_gt, m_gtc) = (
            sem("mlstm_" + n) for n in ("conv", "silu", "rows", "row_parts", "row_done", "g_turned", "g_columns"))
        (m_b, m_bd, m_e, m_kt, m_pd, m_cn, m_cnd, m_num, m_hq, m_rms, m_rt, m_y) = (
            sem("mlstm_" + n) for n in ("bcast", "exponent", "exps", "kq", "probs", "state", "state_updated", "num",
                                        "h_squared", "rms", "rooted", "y"))
        (c_mm, c_hid, c_out, c_outc, z_row, z_rowc, z_flip, z_flipc) = (
            sem(n) for n in ("cmp_hidden", "cmp_silu", "cmp_out", "cmp_copied", "rel_row", "rel_row_copied",
                             "rel_flip", "rel_bias_ready"))
        q_zeroed = sem("query_halves_zeroed")
        m_kscaled = sem("mlstm_keys_scaled")
        m_rowx2, m_hq1 = (sem(n) for n in ("mlstm_f_row",
                                                             "mlstm_h"))
        y_done, fin_t, fin_c, s_out = (sem(n) for n in ("nsa_done", "final_turned", "final_copied", "stored"))

        PROD = SL[:, 2:4].rearrange("p s k t -> p (s k t)").rearrange("p (b w u n) -> p b w u n", b=2, w=4, u=8)
        rflat = ring[:].rearrange("p s k n -> p (s k n)")
        T5, T6 = rflat[:, 0:512], rflat[:, 512:1024]
        MT2, M0, M1, MTF, XX = (rflat[:, 1024 * i:1024 * (i + 1)].rearrange("p (u n) -> p u n", u=8)
                                for i in range(1, 6))
        NS = rflat[:, 6144:8192].rearrange("p (b u n) -> p b u n", b=2, u=8)
        KT = AR[:].rearrange("p c w t -> p (c w t)").rearrange("p (b t) -> p b t", b=2)
        lw1 = flat(S7)[:, 0:512].rearrange("p (k n) -> p k n", k=KD)
        la1 = flat(S7)[:, 512:1024].rearrange("p (k n) -> p k n", k=KD)
        lg1 = flat(S7)[:, 1024:2304].rearrange("p (k n) -> p k n", k=KD)
        lw2 = flat(S7)[0:64, 2304:3328]
        la2 = flat(S8)[0:64, 0:1024]
        lg2 = flat(S8)[:, 1024:2048]
        lg2b = flat(S8)[0:32, 2048:3072]
        LH = AR[:].rearrange("p c w t -> p (c w t)").rearrange("p (w t) -> p w t", w=2)
        wff = flat(S6)[:, 0:128].rearrange("p (k n) -> p k n", k=KD)
        fb = small[0:16, 24:25]
        sel = flat(S8)[0:16, 0:2048]
        NC = flat(S8)[0:16, 2048:2560]
        CB = flat(S8)[:, 2560:3584].rearrange("p (b t) -> p b t", b=2)
        Pb = flat(S6)[:, 0:2048].rearrange("p (b t) -> p b t", b=4)
        PTb = flat(S6)[:, 2048:3584].rearrange("p (b t) -> p b t", b=3)
        mx = small[:, 26:30]
        rs = small[:, 56:60]
        QZ = [S1, S2]
        FV = flat(S4).rearrange("p (t n) -> p t n", t=NT)
        ident = mat(IDENT)
        ones = mat(ONES)
        halfmean = mat(HALFMEAN)

        fox_units = []
        for e in range(KD):
            for hh in range(2):
                h = 2 * e + hh
                for tq in range(NT):
                    w = P * (tq + 1)
                    fox_units.append(dict(
                        q=QZ[hh][:, e, tq * P:tq * P + P], k=S3[:, e, 0:w], mask=True, w=w,
                        bias=CB[:, h % 2, 0:w], gate=None, clamp=False,
                        v=[FV[:, s, h * HD:h * HD + HD] for s in range(tq + 1)],
                        out=bank[e % 2][64 * hh:64 * hh + 64, tq * P:tq * P + P], first=True, last=True,
                        rowbias=h if tq == 0 else None,
                        next_rowbias=h + 1 if (tq == 1 and h + 1 < 16) else None, e=e, ends_e=(hh == 1 and tq == NT - 1)))
        SM = flat(S6)
        YM = S6[:, 0:4, :]
        YN = S6[:, 4:8, :]
        MVT = flat(S4)[:, 0:2048].rearrange("p (t n) -> p t n", t=NT)
        OG = S4[:, 4:8, :]
        NQT = S5[:, 0:4, :]
        KVC = S5[:, 4:6, :]
        KS = S5[:, 6, :]
        KW = S5[:, 7, :]
        Z = [(S7 if h < 4 else S8)[:].rearrange("p k t -> p (k t)")[:, 1024 * (h % 4):1024 * (h % 4) + 896]
             for h in range(8)]
        VSW = BK[:].rearrange("p b t -> p (b t)").rearrange("p (t n) -> p t n", t=NT)
        GT2 = sb("GT2", [P, NT, 24])
        KC = sb("KC", [P, 32])
        VC = sb("VC", [P, 2, 64])
        GC = sb("GC", [P, NT, 4])
        DC = sb("DC", [P, NT])
        PEH = sb("PEH", [P, 2])
        late = cmat[:, LEVEL:LEVEL + 14, :].rearrange("p a b -> p (a b)")
        RSI, REM, SELM, BVS = late[0:4, 0:512], late[0:4, 512:1024], late[0:4, 1024:1536], late[:, 1536:1792]
        GR, RI, RG, RMU = S6[0:24, 0, :], S6[0:4, 1, :], S6[0:4, 2, :], S6[0:4, 3, :]
        WSM = flat(S6)[:, 2048:3072].rearrange("p (k n) -> p k n", k=KD)
        OH = flat(S6)[0:33, 3072:4096]
        CN = flat(S6)[:, 2048:3072].rearrange("p (c n) -> p c n", c=4)
        KWT, PM = S6[:, 6, :], S6[:, 7, :]
        ROW = AR[0:8].rearrange("p c w t -> p (c w t)")
        BMV, QS = T3, T4
        HID = SS[:, 0:4 * N_CMP].rearrange("p (j g c) -> p j g c", j=2, g=2)
        W2C = SA[:].rearrange("p (j d) -> p j d", j=2)
        PEC, PET = RT[0:64, 0:64], RT[0:64, 64:128]
        HK = S2[:]
        TB = small[0:33, 48:56]
        nsa_units = []
        for r in range(4):
            for g in range(2):
                h = 4 * g + r
                for tq in range(NT):
                    for b, br in enumerate(("cmp", "sel", "win")):
                        w = N_CMP if br == "cmp" else P * (tq + 1)
                        keys = {"cmp": KC[64 * g:64 * g + 64, 0:N_CMP], "sel": KS[64 * g:64 * g + 64, 0:w],
                                "win": KW[64 * g:64 * g + 64, 0:w]}[br]
                        if br == "cmp":
                            y0 = 415 - P * tq
                            bias = Z[h][:, y0:y0 + 16 * (N_CMP - 1) + 1:16]
                            v = [VC[0:N_CMP, g, :]]
                        else:
                            bias = Z[h][:, 384 - P * tq:512]
                            off = (0 if br == "sel" else 128) + 64 * g
                            v = [VSW[:, s, off:off + 64] for s in range(tq + 1)]
                        nsa_units.append(dict(
                            q=NQT[64 * g:64 * g + 64, r, tq * P:tq * P + P], k=keys, mask=False, w=w, bias=bias,
                            gate=GT2[:, tq, h * 3 + b:h * 3 + b + 1], clamp=(br == "cmp"), v=v,
                            out=bank[r % 2][64 * g:64 * g + 64, tq * P:tq * P + P],
                            first=(b == 0), last=(b == 2), rowbias=None, next_rowbias=None, e=r,
                            ends_e=(g == 1 and tq == NT - 1 and b == 2)))
        NF, NN = len(fox_units), len(nsa_units)

        aux_n = {}
        for it in range(KD + 2):
            for name in ("ssq", "bon", "b0", "b1", "b2", "b3", "mean", "k0", "k1", "k2", "k3", "var",
                         "t0", "t1", "t2"):
                e = it - 2 if name in ("mean", "var") else it
                if 0 <= e < KD:
                    aux_n[name, e] = len(aux_n)

        def tiles_at(it):
            return tuple(e if 0 <= e < KD else None for e in (it - 1, it - 2, it))
        Pn = flat(S3)[:, 0:2048].rearrange("p (b t) -> p b t", b=4)
        PTn = flat(S3)[:, 2048:3584].rearrange("p (b t) -> p b t", b=3)

        def pair_wait(eng, name):
            first, n = pairs[name]
            for j in range(max(first, first + n - 2), first + n):
                eng.wait_ge(evacuated[j % 2], j // 2 + 1)

        def aux_wait(eng, name, e):
            n = aux_n[name, e]
            eng.wait_ge(aux_evac[n % 2], n // 2 + 1)

        NORMS = ["rwkv", "mlp0", "kv", "mlp1", "mix", "ffn", "final"]
        X_AFTER = {"rwkv": None, "mlp0": "rwkv_o", "kv": "mlp0_out", "mlp1": "fox_o", "mix": "mlp1_out",
                   "ffn": "w_out", "final": "down"}
        OUT_BEFORE = {}
        n_out = 0
        for n in NORMS:
            n_out += 16 if n == "kv" else 8
            OUT_BEFORE[n] = n_out

        block = ctx.enter_context(nc.Block())

        @block.sync
        def _(sp):
            for g, dmas in enumerate(loads):
                if g >= SLOTS:
                    sp.wait_ge(chunk_done, g - SLOTS + 1)
                if g == pair_chunks[pairs["rwkv_o"][0]][0][0]:
                    sp.wait_ge(p_out, KD)
                for dst, src in dmas:
                    sp.dma_start(dst, src).then_inc(slot_loaded[g % SLOTS], 16)
            for t in range(NT):
                sp.wait_ge(fin_c, 2 * (t + 1))
                sp.dma_start(out[0, t * P:(t + 1) * P, :], S2[:, 2 * t:2 * t + 2, :].rearrange("p k t -> p (k t)")
                             ).then_inc(s_out, 16)
            sp.wait_ge(s_out, 16 * NT)

        @block.gpsimd
        def _(pool):
            def load(dst, src, s):
                pool.dma_start(dst, src).then_inc(s, 16)

            load(cmat[:].rearrange("p a b -> p (a b)"), a["c_mat"], s_const)
            load(flat(S3).rearrange("p (t f) -> p t f", t=NT), a["x"][0].rearrange("(t p) f -> p t f", p=P), s_x)
            b_in = a["b_in_2"][0]
            bnq = b_in[NQ:NQ + 512].rearrange("(g r d) -> g r d", g=2, r=4)
            src = {
                "b_mqk": b_in[0:1024].rearrange("(k p) -> k p", p=P),
                "b_mo": b_in[MO:MO + 512].rearrange("(k p) -> k p", p=P),
                "b_nkv": b_in[NKV:NKV + 768].rearrange("(k p) -> k p", p=P),
                "b_merge": b_in[MERGE:MERGE + 2048].rearrange("(k p) -> k p", p=P),
                "rwkv_mu": a["rwkv_mu"][0].rearrange("m (k p) -> (m k) p", p=P),
                "rwkv_r_k": a["rwkv_r_k"][0].rearrange("(k h) d -> k (h d)", h=2),
                "k_norm_g": a["k_norm_g"].rearrange("(k h) d -> k (h d)", h=2),
                "q_norm_g": a["q_norm_g"][0].rearrange("(k h) d -> k (h d)", h=2),
                "mlp_norm_g": a["mlp_norm_g"].rearrange("m (k p) -> (m k) p", p=P),
                "conv_qk_2": a["conv_qk_2"][0].rearrange("m (k p) -> (m k) p", p=P),
                "kv_norm_g": a["kv_norm_g"].rearrange("(k p) -> k p", p=P),
                "g_final_2": a["g_final_2"].rearrange("(k p) -> k p", p=P),
            }
            pool.wait_ge(setup_done, 1)
            n = 0
            for name, (r0, k) in rows.items():
                dst = S4[r0 % P:r0 % P + k, r0 // P, 0:P]
                if name == "b_nq":
                    for g in range(2):
                        load(dst[:, 64 * g:64 * g + 64], bnq[g], s_par)
                        n += 1
                    continue
                s = src[name] if name in src else a[name][0].rearrange("(k p) -> k p", p=P)
                load(dst, s, s_par)
                n += 1
            assert n == N_PAR
            load(lw1, a["rwkv_w1"][0].rearrange("(k p) n -> p k n", p=P), s_lora)
            load(lw2, a["rwkv_w2"][0], s_lora)
            load(la1, a["rwkv_a1"][0].rearrange("(k p) n -> p k n", p=P), s_lora)
            load(la2, a["rwkv_a2"][0], s_lora)
            load(lg1, a["rwkv_g1"][0].rearrange("(k p) n -> p k n", p=P), s_lora)
            load(lg2, a["rwkv_g2"][0][0:P, :], s_lora)
            load(lg2b, a["rwkv_g2"][0][P:160, :], s_lora)
            load(fb, a["kv_f_bias"].rearrange("(p n) -> p n", n=1), s_bias)
            for F in range(KD):
                nt = PROD[:, F % 2, 0]
                aux_wait(pool, "b2", F)
                aux_wait(pool, "b3", F)
                if F:
                    pool.wait_ge(p_d, 12 * (F - 1) + 2)
                nc.gpsimd.tensor_tensor(MT2, nt, mat(LEVEL + 1).unsqueeze(1).broadcast_to([P, 8, P]), ALU.mult
                                        ).then_inc(p_i, 1)
                pool.wait_ge(p_i, 2 * F + 1)
                nc.gpsimd.tensor_tensor(MT2, MT2, ident.unsqueeze(1).broadcast_to([P, 8, P]), ALU.add
                                        ).then_inc(p_i, 1)
                for lv in range(6):
                    m = 6 * F + lv
                    if m >= 2:
                        pool.wait_ge(p_x, 2 * (m - 1))
                    nc.gpsimd.tensor_tensor(NS[:, m % 2], nt,
                                            mat(LEVEL + 3 + 2 * lv).unsqueeze(1).broadcast_to([P, 8, P]), ALU.mult
                                            ).then_inc(p_ns, 1)
            pair_wait(pool, "mlp0_out")
            load(wff, a["kv_w"][:, 2 * D:2 * D + 16].rearrange("(k p) n -> p k n", p=P), s_ffw)
            load(sel, a["c_sel"], s_sel)
            pair_wait(pool, "fq")
            pool.wait_ge(f_mm, 1)
            nc.gpsimd.memset(S1[64:128, :, :], 0.0).then_inc(q_zeroed, 1)
            nc.gpsimd.memset(S2[0:64, :, :], 0.0).then_inc(q_zeroed, 1)
            pair_wait(pool, "mlp1_out")
            for j, s in ((0, S7), (1, S8)):
                w1 = a["w_cmp1_2"][0][j].rearrange("(p d) n -> d p n", d=64)
                for half in range(2):
                    load(s[64 * half:64 * half + 64].rearrange("d k t -> d (k t)").rearrange("d (p n) -> d p n", p=32),
                         w1, s_cmp)
            load(W2C[:, 0, :], a["w_cmp2_2"][0][0], s_cmp)
            load(W2C[:, 1, :], a["w_cmp2_2"][0][1], s_cmp)
            load(PEC, a["pe_cmp_2"][0].rearrange("j p d -> (j p) d"), s_cmp)
            pool.wait_ge(s_wz, 1)
            load(WSM[:, :, 0:4], w_in[:, MI:MI + 4].rearrange("(k p) n -> p k n", p=P), s_small_w)
            load(WSM[:, :, 32:36], w_in[:, MF:MF + 4].rearrange("(k p) n -> p k n", p=P), s_small_w)
            load(WSM[:, :, 64:88], w_in[:, NG:NG + 24].rearrange("(k p) n -> p k n", p=P), s_small_w)
            load(small[0:4, 33:34], b_in[MI:MI + 4].rearrange("(p n) -> p n", n=1), s_small_w)
            load(small[0:4, 34:35], b_in[MF:MF + 4].rearrange("(p n) -> p n", n=1), s_small_w)
            load(small[0:4, 35:36], a["b_fgate_2"].rearrange("a n -> n a"), s_small_w)
            load(small[0:24, 36:37], b_in[NG:NG + 24].rearrange("(p n) -> p n", n=1), s_small_w)
            load(BMV[:], b_in[MV:MV + 512].partition_broadcast(P), s_small_w)
            load(BVS[:, 0:128], b_in[NKV + 384:NKV + 512].partition_broadcast(P), s_small_w)
            load(BVS[:, 128:256], b_in[NKV + 640:NKV + 768].partition_broadcast(P), s_small_w)
            load(OH, a["c_onehot"], s_oh)
            load(TB[0:32, :], a["rel_bias_2"], s_oh)
            load(SELM, a["c_sel"][0:4, 0:512], s_oh)
            pool.wait_ge(z_rowc, 2)
            pool.dma_start(scratch, ROW).then_inc(s_relst, 16)
            pool.wait_ge(s_relst, 16)
            pool.wait_ge(m_silu, 8)
            hank = bass.AP(scratch.tensor, 0, [[1, P], [1024, 8], [1, 512]])
            load(HK, hank, s_hankel)

        @block.tensor
        def _(pe):
            def gemm(name, rhs, tm=False):
                first, n = pairs[name]
                for j in range(first, first + n):
                    if j >= 2:
                        pe.wait_ge(evacuated[j % 2], j // 2)
                    b = 2 * (j % 2)
                    last_k = pair_chunks[j][-1][1] + pair_chunks[j][-1][2] - 1
                    for g, k0, nk in pair_chunks[j]:
                        pe.wait_ge(slot_loaded[g % SLOTS], landed[g])
                        w = ring[:, g % SLOTS]
                        if tm:
                            for t in range(NT):
                                for k in range(nk):
                                    mm = pe.matmul(bank[b + t // 2][:, 256 * (t % 2):256 * (t % 2) + 256],
                                                   rhs(k)[:, t * P:(t + 1) * P], w[:, k, :],
                                                   start=(k == 0), stop=(k == nk - 1))
                        else:
                            for half in range(2):
                                for k in range(nk):
                                    mm = pe.matmul(bank[b + half][:], w[:, k, half * P:(half + 1) * P], rhs(k0 + k),
                                                   start=(k0 + k == 0), stop=(k0 + k == last_k))
                        mm.then_inc(chunk_done, 1)

            def norm(name):
                n = NORMS.index(name)
                for k in range(KD):
                    pe.wait_ge(norm_sq, 8 * n + k + 1)
                    pe.matmul(bank[4][:], ones, (T1, T2)[k % 2][:], start=(k == 0), stop=(k == KD - 1)
                              ).then_inc(norm_mm, 1)

            pe.wait_ge(s_const, 16)
            pe.wait_ge(s_x, 16)
            xt = flat(S3).rearrange("p (t f) -> p t f", t=NT)
            for k in range(KD):
                if k >= 2:
                    pe.wait_ge(pe_tc, k - 1)
                for t in range(NT):
                    mm = pe.transpose(bank[4 + k % 2][:, t * P:(t + 1) * P], xt[:, t, k * P:(k + 1) * P], ident)
                mm.then_inc(pe_t, 1)
            pe.wait_ge(s_par, 16 * N_PAR)
            for i in range(3):
                mm = pe.transpose(bank[6][:, i * P:(i + 1) * P], S4[:, i, 0:P], ident)
            mm.then_inc(pe_t, 1)
            norm("rwkv")

            pe.wait_ge(s_lora, 16 * 7)
            w1s = [[(lw1, 0, 64)], [(la1, 0, 64)], [(lg1, 0, 128), (lg1, 128, 32)]]
            q = 0
            nl = 0
            for i in range(3):
                pe.wait_ge(mix_ready, i + 1)
                for n, (w, c0, m) in enumerate(w1s[i]):
                    if nl >= 2:
                        pe.wait_ge(lora1_out, nl - 1)
                    for k in range(KD):
                        mm = pe.matmul(bank[4 + nl % 2][0:m, :], w[:, k, c0:c0 + m], S3[:, k, :],
                                       start=(k == 0), stop=(k == KD - 1))
                    mm.then_inc(lora1, 1)
                    nl += 1
                pe.wait_ge(lora1_out, nl)
                for e in range(KD):
                    if q >= 2:
                        pe.wait_ge(lora2_out, q - 1)
                    o = bank[6 + q % 2][:]
                    if i < 2:
                        mm = pe.matmul(o, (lw2, la2)[i][:, e * P:(e + 1) * P], LH[0:64, i, :], start=True, stop=True)
                    else:
                        pe.matmul(o, lg2[:, e * P:(e + 1) * P], LH[:, 0, :], start=True, stop=False)
                        mm = pe.matmul(o, lg2b[:, e * P:(e + 1) * P], LH[0:32, 1, :], start=False, stop=True)
                    mm.then_inc(lora2, 1)
                    q += 1
            for i, name in enumerate("rkv"):
                pe.wait_ge(mix_ready, 4 + i)
                gemm(name, lambda k: S3[:, k, :])

            def aux(name, e):
                n = aux_n[name, e]
                if n >= 2:
                    pe.wait_ge(aux_evac[n % 2], n // 2)
                return bank[4 + n % 2]

            def scan_r(e, c):
                n = NT * e + c
                if c == 0:
                    pe.wait_ge(p_dc, 12 * (e + 1))
                    aux_wait(pe, "t1", e)
                    aux_wait(pe, "t2", e)
                else:
                    pe.wait_ge(p_stc, n - e)
                    pe.matmul(bank[6][:, 0:P], S4[:, e, c * P:(c + 1) * P], SS[:], start=True, stop=False)
                for hh in range(2):
                    at = c * P + 64 * hh
                    mm = pe.matmul(bank[6][:, 64 * hh:64 * hh + 64], PROD[:, e % 2, 2, 4 * hh + c],
                                   S1[:, e, at:at + 64], start=(c == 0), stop=(c == 0 or hh == 1))
                mm.then_inc(p_r, 1)

            def scan_sa(e, c):
                n = NT * e + c
                pe.wait_ge(p_rc, n + 1)
                for hh in range(2):
                    mm = pe.matmul(bank[6][:, P + 64 * hh:P + 64 * hh + 64], MTF[:, 4 * hh + c],
                                   RT[:, 64 * hh:64 * hh + 64], start=True, stop=True)
                mm.then_inc(p_sa, 1)

            def scan_y(e, c):
                n = NT * e + c
                t = slice(c * P, (c + 1) * P)
                pe.wait_ge(p_sac, n + 1)
                if c < NT - 1:
                    pe.matmul(bank[6][:, 2 * P:3 * P], S7[:, e, t], SA[:], start=True, stop=False)
                    pe.matmul(bank[6][:, 2 * P:3 * P], KT[:, e % 2, t], S1[:, e, t], start=False, stop=True
                              ).then_inc(p_st, 1)
                if c == 0 and e:
                    pe.wait_ge(p_yc, e)
                for hh in range(2):
                    u = 4 * hh + c
                    o = bank[7][64 * hh:64 * hh + 64, t]
                    hc = slice(64 * hh, 64 * hh + 64)
                    at = c * P + 64 * hh
                    if c:
                        pe.matmul(o, SS[:, hc], S8[:, e, t], start=True, stop=False)
                    pe.matmul(o, SA[:, hc], PROD[:, e % 2, 1, u], start=(c == 0), stop=False)
                    mm = pe.matmul(o, S1[:, e, at:at + 64], PROD[:, e % 2, 3, u], start=False, stop=True)
                mm.then_inc(p_y, 1)

            def products(w, b, e):
                o = aux(("b", "k")[w] + str(b), e)
                for u in (2 * b, 2 * b + 1):
                    hh, c = u // 4, u % 4
                    s = slice(64 * hh, 64 * hh + 64)
                    mm = pe.matmul(o[:, 256 * (u % 2):256 * (u % 2) + 256], BK[s, w, c * P:(c + 1) * P],
                                   SL[s, 4:9:4, e, c * P:(c + 1) * P], start=True, stop=True)
                mm.then_inc(aux_filled, 1)

            def gap(g, S, F):
                if S is not None and g < 12:
                    (scan_r, scan_sa, scan_y)[g % 3](S, g // 3)
                if F is not None:
                    if g == 1:
                        pe.wait_ge(p_sq, F + 1)
                        pe.matmul(aux("ssq", F)[:], halfmean, T2[:], start=True, stop=True).then_inc(aux_filled, 1)
                    if g == 12:
                        pe.wait_ge(p_fm, F + 1)
                        pe.matmul(aux("bon", F)[:], halfmean, T2[:], start=True, stop=True).then_inc(aux_filled, 1)
                    if 12 <= g < 16:
                        for b in (0, 1):
                            products((g - 12) // 2, 2 * (g % 2) + b, F)
                if S is not None:
                    if g == 13:
                        pe.wait_ge(p_yc, S + 1)
                        pe.matmul(aux("mean", S)[:], halfmean, T5, start=True, stop=True).then_inc(aux_filled, 1)
                    if g == 15:
                        pe.wait_ge(p_cen2, S + 1)
                        pe.matmul(aux("var", S)[:], halfmean, T6, start=True, stop=True).then_inc(aux_filled, 1)
                if F is not None:
                    if g == 16:
                        for w, src in enumerate((BK[:, 0], BK[:, 1], S1[:, F])):
                            o = aux(f"t{w}", F)
                            for c in range(NT):
                                mm = pe.transpose(o[:, c * P:(c + 1) * P], src[:, c * P:(c + 1) * P], ident)
                            mm.then_inc(aux_filled, 1)
                    if g == 17:
                        pe.wait_ge(p_i, 2 * F + 2)
                        for hh in range(2):
                            if F:
                                pe.wait_ge(p_xc, 12 * F - 1 + hh)
                            for c in range(NT):
                                mm = pe.transpose(bank[hh][:, c * P:(c + 1) * P], MT2[:, 4 * hh + c], ident)
                            mm.then_inc(p_it, 1)

            for it in range(KD + 2):
                L, S, F = tiles_at(it)
                for lv in range(6):
                    for hh in range(2):
                        if L is None:
                            continue
                        n = 12 * L + 2 * lv + hh
                        if hh == 0:
                            pe.wait_ge(p_ns, 6 * L + lv + 1)
                        if lv == 0:
                            pe.wait_ge(p_ic, 2 * L + hh + 1)
                        else:
                            pe.wait_ge(p_tc, 10 * L + 2 * (lv - 1) + hh + 1)
                        for c in range(NT):
                            mm = pe.matmul(bank[hh][:, c * P:(c + 1) * P], NS[:, (6 * L + lv) % 2, 4 * hh + c],
                                           M0[:, 4 * hh + c], start=True, stop=True)
                        mm.then_inc(p_x, 1)
                    gap(3 * lv, S, F)
                    for hh in range(2):
                        if L is None:
                            continue
                        n = 12 * L + 2 * lv + hh
                        pe.wait_ge(p_xc, n + 1)
                        if n >= 2:
                            pe.wait_ge(p_dc, n - 1)
                        mt = MT2 if lv == 0 else M1
                        for c in range(NT):
                            u = 4 * hh + c
                            if lv < 5:
                                mm = pe.matmul(bank[2 + hh][:, c * P:(c + 1) * P], mt[:, u], XX[:, u],
                                               start=True, stop=True)
                            else:
                                mm = pe.matmul(bank[2 + hh][:, c * P:(c + 1) * P], XX[:, u], mt[:, u],
                                               start=True, stop=True)
                        mm.then_inc(p_d, 1)
                    gap(3 * lv + 1, S, F)
                    for hh in range(2):
                        if L is None or lv == 5:
                            continue
                        pe.wait_ge(p_dc, 12 * L + 2 * lv + hh + 1)
                        for c in range(NT):
                            mm = pe.transpose(bank[hh][:, c * P:(c + 1) * P], M0[:, 4 * hh + c], ident)
                        mm.then_inc(p_t, 1)
                    gap(3 * lv + 2, S, F)
            pe.wait_ge(p_out, KD)
            gemm("rwkv_o", lambda k: S7[:, k, :])

            def mlp(i):
                norm(f"mlp{i}")
                pe.wait_ge(norm_out, OUT_BEFORE[f"mlp{i}"])
                gemm(f"mlp{i}_in", lambda k: S1[:, k, :])
                pair_wait(pe, f"mlp{i}_in")
                gemm(f"mlp{i}_out", lambda k: slab[2 + k // KD][:, k % KD, :])

            mlp(0)

            norm("kv")
            pe.wait_ge(norm_out, OUT_BEFORE["kv"] - 8)
            gemm("fk", lambda k: S1[:, k, :])
            gemm("fv", lambda k: S1[:, k, :], tm=True)
            pe.wait_ge(s_ffw, 16)
            for k in range(KD):
                mm = pe.matmul(bank[4][0:16, :], wff[:, k, :], S1[:, k, :], start=(k == 0), stop=(k == KD - 1))
            mm.then_inc(f_mm, 1)
            pe.wait_ge(norm_out, OUT_BEFORE["kv"])
            gemm("fq", lambda k: S2[:, k, :])
            pe.wait_ge(f_cum, 1)
            for n in range(2 * KD):
                pe.wait_ge(h_sq, n + 1)
                if n >= 2:
                    pe.wait_ge(h_rt, n - 1)
                pe.matmul(bank[4 + n % 2][:], halfmean, (T1, T2)[n % 2][:], start=True, stop=True).then_inc(h_mm, 1)

            def attention(units, base, Pt, PTt, o_base, s_banks):
                N, NS = len(units), len(s_banks)
                for i in range(N + 3):
                    if i < N:
                        u = units[i]
                        if u["rowbias"] is not None and i == 0:
                            pe.wait_ge(s_sel, 16)
                            pe.matmul(bank[2][:], sel[:, 0:P], NC, start=True, stop=True).then_inc(a_cb, 1)
                        if u["next_rowbias"] is not None:
                            h = u["next_rowbias"]
                            pe.wait_ge(a_cbc, h)
                            pe.matmul(bank[2][:], sel[:, h * P:(h + 1) * P], NC, start=True, stop=True
                                      ).then_inc(a_cb, 1)
                        if i >= NS:
                            pe.wait_ge(a_l, base + i - NS + 1)
                        s = bank[s_banks[i % NS]]
                        mm = pe.matmul(s[:, 0:u["w"]], u["q"], u["k"], start=True, stop=not u["mask"])
                        if u["mask"]:
                            mm = pe.matmul(s[:, u["w"] - P:u["w"]], ident, mat(CAUSAL_NEG), start=False, stop=True)
                        mm.then_inc(a_s, 1)
                    if 2 <= i < N + 2:
                        n = i - 2
                        u = units[n]
                        pe.wait_ge(a_p, base + n + 1)
                        if n >= 2:
                            pe.wait_ge(a_tc, base + n - 1)
                        b = bank[6 + n % 2]
                        if u["w"] == N_CMP:
                            mm = pe.transpose(b[0:N_CMP, 0:P], Pt[:, n % 4, 0:N_CMP], ident)
                        else:
                            for s in range(len(u["v"])):
                                mm = pe.transpose(b[:, s * P:(s + 1) * P], Pt[:, n % 4, s * P:(s + 1) * P], ident)
                        mm.then_inc(a_t, 1)
                    if i >= 3:
                        n = i - 3
                        u = units[n]
                        pe.wait_ge(a_tc, base + n + 1)
                        if u["first"] and u["e"] >= 2:
                            pe.wait_ge(a_o, o_base + u["e"] - 1)
                        K = N_CMP if u["w"] == N_CMP else P
                        for s, v in enumerate(u["v"]):
                            mm = pe.matmul(u["out"], v, PTt[0:K, n % 3, s * P:(s + 1) * P],
                                           start=(u["first"] and s == 0), stop=(u["last"] and s == len(u["v"]) - 1))
                        mm.then_inc(a_pv, 1)

            pe.wait_ge(h_out, 2 * KD)
            pe.wait_ge(q_zeroed, 2)
            attention(fox_units, 0, Pb, PTb, 0, (3, 4, 5))
            pe.wait_ge(a_o, KD)
            gemm("fox_o", lambda k: S7[:, k, :])
            mlp(1)

            norm("mix")
            pe.wait_ge(norm_out, OUT_BEFORE["mix"])
            u1 = lambda k: S1[:, k, :]
            gemm("mqk", u1)
            gemm("mv", u1, tm=True)
            gemm("mo", u1)
            gemm("nq", u1)
            gemm("kvc", u1)
            gemm("ksw", u1)
            gemm("vsw", u1, tm=True)
            pe.wait_ge(s_small_w, 16 * 10)
            for k in range(KD):
                mm = pe.matmul(bank[4][:], WSM[:, k, :], S1[:, k, :], start=(k == 0), stop=(k == KD - 1))
            mm.then_inc(m_rows, 1)
            pe.wait_ge(s_cmp, 16 * 7)
            pe.transpose(bank[5][0:64, 0:64], PEC, ident[0:64, 0:64]).then_inc(c_mm, 1)
            pe.wait_ge(c_hid, 1)
            for j, s in enumerate((S7, S8)):
                w1 = flat(s).rearrange("d (p n) -> d p n", p=32)
                for p in range(32):
                    mm = pe.matmul(bank[5][:, 128 + j:129 + j], w1[0:64, p, :], PET[:, 32 * j + p:32 * j + p + 1],
                                   start=(p == 0), stop=(p == 31))
            mm.then_inc(c_mm, 1)
            pair_wait(pe, "kvc")
            for g in range(2):
                for j, s in enumerate((S7, S8)):
                    w1 = flat(s).rearrange("d (p n) -> d p n", p=32)
                    for p in range(32):
                        mm = pe.matmul(bank[6 + g][:, 32 * j:32 * j + N_CMP], w1[64 * g:64 * g + 64, p, :],
                                       KVC[64 * g:64 * g + 64, j, p:p + 16 * (N_CMP - 1) + 1:16],
                                       start=(p == 0), stop=(p == 31))
            mm.then_inc(c_mm, 1)
            pe.wait_ge(c_hid, 3)
            for g in range(2):
                pe.matmul(bank[5][64 * g:64 * g + 64, 0:N_CMP], W2C[:, 0, :], HID[:, 0, g, :], start=True, stop=True)
                mm = pe.matmul(bank[5][0:N_CMP, 128 + 64 * g:192 + 64 * g], HID[:, 1, g, :], W2C[:, 1, :],
                               start=True, stop=True)
            mm.then_inc(c_out, 1)
            pe.wait_ge(s_oh, 48)
            pe.wait_ge(s_wz, 1)
            pe.wait_ge(z_row, 1)
            for i in range(2):
                mm = pe.matmul(bank[6 + i][0:8, :], TB, OH[:, i * 512:(i + 1) * 512], start=True, stop=True)
            mm.then_inc(z_flip, 1)

            pe.wait_ge(m_rowd, 1)
            for c in range(NT):
                mm = pe.transpose(bank[4][:, 4 * c:4 * c + 4], RG[0:4, c * P:(c + 1) * P], ident[0:4, 0:4])
            for c in range(NT):
                mm = pe.transpose(bank[4][:, 32 + 24 * c:32 + 24 * c + 24], GR[0:24, c * P:(c + 1) * P],
                                  ident[0:24, 0:24])
            mm.then_inc(m_gt, 1)
            pe.wait_ge(m_silu, 8)
            pe.wait_ge(z_rowc, 2)
            pe.wait_ge(m_gtc, 1)
            pe.wait_ge(m_rowx, 3)
            pe.wait_ge(m_kscaled, 1)
            for h in range(4):
                if h:
                    pe.wait_ge(m_y, h)
                sh = SELM[:, h * P:(h + 1) * P]
                for i, (row, b) in enumerate(((RMU, 4), (RSI, 6), (REM, 2))):
                    mm = pe.matmul(bank[b][:], sh, row, start=True, stop=True)
                mm.then_inc(m_b, 1)
                for c in range(NT):
                    t = slice(c * P, (c + 1) * P)
                    pe.matmul(bank[5][:, t], S3[:, 4 + h, t], S3[:, h, t], start=True, stop=True)
                for c in range(NT):
                    t = slice(c * P, (c + 1) * P)
                    mm = pe.transpose(bank[7][:, t], S3[:, 4 + h, t], ident)
                mm.then_inc(m_kt, 1)
                pe.wait_ge(m_pd, h + 1)
                for c in range(NT):
                    t = slice(c * P, (c + 1) * P)
                    v = MVT[:, c, h * P:(h + 1) * P]
                    if c:
                        pe.wait_ge(m_cnd, 3 * h + c)
                    pe.matmul(bank[0][:, t], v, PM[:, t], start=True, stop=(c == 0))
                    if c:
                        pe.matmul(bank[0][:, t], CN[:, c, 0:P], QS[:, t], start=False, stop=True)
                    mm = pe.matmul(bank[1][:, t], ones, PM[:, t], start=True, stop=(c == 0))
                    if c:
                        mm = pe.matmul(bank[1][:, t], CN[:, c, P:2 * P], QS[:, t], start=False, stop=True)
                    if c < NT - 1:
                        pe.matmul(bank[3][:, 0:P], KWT[:, t], v, start=True, stop=True)
                        pe.matmul(bank[3][:, P:2 * P], KWT[:, t], ones, start=True, stop=True).then_inc(m_cn, 1)
                mm.then_inc(m_num, 1)
                pe.wait_ge(m_hq, h + 1)
                pe.matmul(bank[4][:], ones, T2[:], start=True, stop=True).then_inc(m_rms, 1)
            pe.wait_ge(s_hankel, 16)
            pe.wait_ge(m_y, 4)
            for h in range(8):
                if h >= 2:
                    pe.wait_ge(z_flipc, h - 1)
                pe.matmul(bank[6 + h % 2][:], mat(FLIP), HK[:, h, :], start=True, stop=True).then_inc(z_flip, 1)
            pe.wait_ge(z_flipc, 8)
            attention(nsa_units, NF, Pn, PTn, KD, (2, 3, 4, 5))
            pe.wait_ge(a_o, KD + 4)
            for i in range(4):
                for n in range(2):
                    gemm(f"merge{n}_{i}", u1)
                    gemm(f"branch{n}_{i}", lambda k, n=n: S6[:, 4 * n + k, :])
            pair_wait(pe, "branch1_3")
            gemm("w_out", lambda k: S2[:, k, :])
            norm("ffn")
            pe.wait_ge(norm_out, OUT_BEFORE["ffn"])
            for i in range(FF2 // 256):
                gemm(f"gate_{i}", u1)
                gemm(f"up_{i}", u1)
            pair_wait(pe, f"up_{FF2 // 256 - 1}")
            gemm("down", lambda k: slab[2 + k // KD][:, k % KD, :])
            norm("final")
            pe.wait_ge(norm_out, OUT_BEFORE["final"])
            for t in range(NT):
                for half in range(2):
                    n = 2 * t + half
                    if n >= 2:
                        pe.wait_ge(fin_c, n - 1)
                    for k in range(4):
                        mm = pe.transpose(bank[6 + n % 2][:, k * P:(k + 1) * P],
                                          S1[:, 4 * half + k, t * P:(t + 1) * P], ident)
                    mm.then_inc(fin_t, 1)

        @block.scalar
        def _(act):
            count = [0]
            A = nc.scalar.activation

            def link(ins):
                count[0] += 1
                ins.then_inc(achain, 1)
                act.wait_ge(achain, count[0])

            def evac(name, op):
                first, n = pairs[name]
                for i in range(n):
                    j = first + i
                    act.wait_ge(chunk_done, ends[j])
                    for half in range(2):
                        ins = op(2 * i + half, bank[2 * (j % 2) + half][:])
                    ins.then_inc(evacuated[j % 2], 1)

            def norm(name):
                n = NORMS.index(name)
                if X_AFTER[name]:
                    pair_wait(act, X_AFTER[name])
                for k in range(KD):
                    if k >= 2:
                        act.wait_ge(norm_mm, 8 * n + k - 1)
                    A((T1, T2)[k % 2][:], S0[:, k, :], ACT.Square).then_inc(norm_sq, 1)
                act.wait_ge(norm_mm, 8 * (n + 1))
                A(rstd[:], bank[4][:], ACT.Sqrt, bias=eps6, scale=1.0 / D).then_inc(norm_root, 1)

            act.wait_ge(setup_done, 2)
            act.wait_ge(pe_tc, KD)
            norm("rwkv")
            n1 = q = 0
            for i in range(3):
                for part in range(1 if i < 2 else 2):
                    act.wait_ge(lora1, n1 + 1)
                    if i == 2 and part == 0:
                        act.wait_ge(lora2, 2 * KD)
                    m = 64 if i < 2 else (128, 32)[part]
                    A(LH[0:m, i if i < 2 else part, :], bank[4 + n1 % 2][0:m, :],
                      (ACT.Tanh, ACT.Copy, ACT.Sigmoid)[i]).then_inc(lora1_out, 1)
                    n1 += 1
                for e in range(KD):
                    act.wait_ge(lora2, q + 1)
                    b = bank[6 + q % 2][:]
                    if i == 0:
                        ins = A(S4[:, e, :], b, ACT.Sigmoid, bias=par("rwkv_w0", e))
                    elif i == 1:
                        ins = A(S5[:, e, :], b, ACT.Sigmoid, bias=par("rwkv_a0", e))
                    else:
                        ins = A(S6[:, e, :], b, ACT.Copy)
                    ins.then_inc(lora2_out, 1)
                    q += 1
            evac("r", lambda e, b: A(S7[:, e, :], b, ACT.Copy))
            evac("k", lambda e, b: A(S8[:, e, :], b, ACT.Copy))
            evac("v", lambda e, b: A(S1[:, e, :], b, ACT.Copy))

            def aux_read(name, e):
                n = aux_n[name, e]
                act.wait_ge(aux_filled, n + 1)
                return bank[4 + n % 2][:], aux_evac[n % 2]

            def gap(g, S, F):
                if S is not None and g < 12:
                    c = g // 3
                    n = NT * S + c
                    if g % 3 == 0:
                        act.wait_ge(p_r, n + 1)
                        A(RT[:], bank[6][:, 0:P], ACT.Copy).then_inc(p_rc, 1)
                    if g % 3 == 1:
                        act.wait_ge(p_sa, n + 1)
                        if n:
                            act.wait_ge(p_y, n)
                        A(SA[:], bank[6][:, P:2 * P], ACT.Copy).then_inc(p_sac, 1)
                if F is not None:
                    if g == 0:
                        act.wait_ge(p_kk, F + 1)
                        A(T2[:], T1[:], ACT.Square).then_inc(p_sq, 1)
                    if g == 2:
                        b, done = aux_read("ssq", F)
                        A(T2[:], b, ACT.Sqrt, scale=float(HD)).then_inc(done, 1)
                    if g == 3:
                        act.wait_ge(p_c, F + 1)
                        A(S4[:, F, :], S4[:, F, :], ACT.Exp, scale=-DECAY_UNIT)
                        A(T4[:], T3[:], ACT.Exp, scale=-DECAY_UNIT)
                        link(A(CE[:, F], CE[:, F], ACT.Exp, scale=-DECAY_UNIT))
                        A(T3[:], T3[:], ACT.Exp, scale=DECAY_UNIT).then_inc(p_exp, 1)
                if S is not None:
                    if g == 12:
                        act.wait_ge(p_y, NT * (S + 1))
                        if S:
                            act.wait_ge(p_out, S)
                        A(T5, bank[7][:], ACT.Copy).then_inc(p_yc, 1)
                    if g == 14:
                        aux_wait(act, "mean", S)
                        A(T6, T5, ACT.Square).then_inc(p_cen2, 1)
                    if g == 15:
                        b, done = aux_read("var", S)
                        A(T6, b, ACT.Sqrt, bias=epsg).then_inc(done, 1)
                if F is not None:
                    if g == 16:
                        aux_wait(act, "bon", F)
                        for w, dst in enumerate((S7[:, F, :], KT[:, F % 2, :], S1[:, F, :])):
                            b, done = aux_read(f"t{w}", F)
                            A(dst, b, ACT.Copy).then_inc(done, 1)
                    if g == 17:
                        for hh in range(2):
                            act.wait_ge(p_it, 2 * F + hh + 1)
                            A(M0[:, 4 * hh:4 * hh + 4].rearrange("p u n -> p (u n)"), bank[hh][:], ACT.Copy
                              ).then_inc(p_ic, 1)

            for it in range(KD + 2):
                L, S, F = tiles_at(it)
                for lv in range(6):
                    for hh in range(2):
                        if L is None:
                            continue
                        n = 12 * L + 2 * lv + hh
                        act.wait_ge(p_x, n + 1)
                        if n >= 2:
                            act.wait_ge(p_d, n - 1)
                        A(XX[:, 4 * hh:4 * hh + 4].rearrange("p u n -> p (u n)"), bank[hh][:], ACT.Copy
                          ).then_inc(p_xc, 1)
                    gap(3 * lv, S, F)
                    gap(3 * lv + 1, S, F)
                    for hh in range(2):
                        if L is None or lv == 5:
                            continue
                        act.wait_ge(p_t, 10 * L + 2 * lv + hh + 1)
                        A(M1[:, 4 * hh:4 * hh + 4].rearrange("p u n -> p (u n)"), bank[hh][:], ACT.Copy
                          ).then_inc(p_tc, 1)
                    gap(3 * lv + 2, S, F)

            def mlp(i):
                norm(f"mlp{i}")

                def relu2(e, b):
                    h = slab[2 + e // KD][:, e % KD, :]
                    link(A(h, b, ACT.Relu))
                    return A(h, h, ACT.Square)
                evac(f"mlp{i}_in", relu2)

            mlp(0)
            norm("kv")
            evac("fk", lambda e, b: A(S3[:, e, :], b, ACT.Copy))
            first, n = pairs["fv"]
            for i in range(n):
                j = first + i
                act.wait_ge(chunk_done, ends[j])
                for half in range(2):
                    ins = A(FV[:, 2 * half:2 * half + 2, 256 * i:256 * i + 256],
                            bank[2 * (j % 2) + half][:].rearrange("p (t n) -> p t n", t=2), ACT.Copy)
                ins.then_inc(evacuated[j % 2], 1)
            evac("fq", lambda e, b: A(S5[:, e, :], b, ACT.Copy))
            act.wait_ge(f_mm, 1)
            act.wait_ge(s_bias, 16)
            link(A(T1[0:16, :], bank[4][0:16, :], ACT.Identity, bias=fb))
            link(A(T2[0:16, :], T1[0:16, :], ACT.Abs))
            link(A(T2[0:16, :], T2[0:16, :], ACT.Exp, scale=-1.0))
            A(T2[0:16, :], T2[0:16, :], ACT.Ln, bias=one1[0:16]).then_inc(f_rows, 1)
            act.wait_ge(f_cum, 1)
            for n in range(2 * KD + 1):
                if n < 2 * KD:
                    if n >= 2:
                        act.wait_ge(h_mm, n - 1)
                    src = S3[:, n, :] if n < KD else S5[:, n - KD, :]
                    A((T1, T2)[n % 2][:], src, ACT.Square).then_inc(h_sq, 1)
                if n >= 1:
                    r = n - 1
                    act.wait_ge(h_mm, r + 1)
                    if r >= 2:
                        act.wait_ge(h_out, r - 1)
                    A((T3, T4)[r % 2][:], bank[4 + r % 2][:], ACT.Sqrt, bias=eps6 if r < KD else eps6q,
                      scale=1.0 if r < KD else 64.0).then_inc(h_rt, 1)

            def attention(units, base, Pt, PTt, o_base):
                N = len(units)
                fox = units[0]["mask"]
                for i in range(N + 4):
                    if i < N:
                        u = units[i]
                        if u["rowbias"] is not None and i == 0:
                            act.wait_ge(a_cb, 1)
                            A(CB[:, 0, :], bank[2][:], ACT.Copy).then_inc(a_cbc, 1)
                        act.wait_ge(a_l, base + i + 1)
                        p = Pt[:, i % 4, 0:u["w"]]
                        A(p, p, ACT.Exp, bias=mx[:, i % 4:i % 4 + 1], accum_out=rs[:, i % 4:i % 4 + 1]
                          ).then_inc(a_e, 1)
                        if u["next_rowbias"] is not None:
                            h = u["next_rowbias"]
                            act.wait_ge(a_cb, h + 1)
                            A(CB[:, h % 2, :], bank[2][:], ACT.Copy).then_inc(a_cbc, 1)
                    if 2 <= i < N + 2:
                        n = i - 2
                        u = units[n]
                        act.wait_ge(a_t, base + n + 1)
                        if n >= 3:
                            act.wait_ge(a_pv, base + n - 2)
                        K = N_CMP if u["w"] == N_CMP else P
                        w = P if u["w"] == N_CMP else u["w"]
                        A(PTt[0:K, n % 3, 0:w], bank[6 + n % 2][0:K, 0:w], ACT.Copy).then_inc(a_tc, 1)
                    if 4 <= i and units[i - 4]["ends_e"]:
                        e = units[i - 4]["e"]
                        act.wait_ge(a_pv, base + i - 3)
                        dst = S7[:, e, :] if fox else YN[:, e, :]
                        A(dst, bank[e % 2][:], ACT.Copy).then_inc(a_o, 1)

            attention(fox_units, 0, Pb, PTb, 0)
            mlp(1)
            norm("mix")
            act.wait_ge(s_small_w, 16 * 10)
            evac("mqk", lambda e, b: A(S2[:, e, :], b, ACT.Identity, bias=par("b_mqk", e)))
            pair_wait(act, "mv")
            evac("mo", lambda e, b: A(OG[:, e, :], b, ACT.Sigmoid, bias=par("b_mo", e)))
            pair_wait(act, "vsw")
            act.wait_ge(m_rows, 1)
            A(RI[0:4, :], bank[4][0:4, :], ACT.Identity, bias=small[0:4, 33:34])
            A(RMU[0:4, :], bank[4][32:36, :], ACT.Copy)
            A(GR[0:24, :], bank[4][64:88, :], ACT.Copy).then_inc(m_rowx, 1)
            act.wait_ge(m_rowx2, 1)
            link(A(T2[0:4, :], RMU[0:4, :], ACT.Abs))
            link(A(T2[0:4, :], T2[0:4, :], ACT.Exp, scale=-1.0))
            A(T2[0:4, :], T2[0:4, :], ACT.Ln, bias=one1[0:4])
            A(GR[0:24, :], GR[0:24, :], ACT.Sigmoid, bias=small[0:24, 36:37]).then_inc(m_rowx, 1)
            act.wait_ge(c_mm, 1)
            A(PET[:, :], bank[5][0:64, 0:64], ACT.Copy).then_inc(c_hid, 1)
            act.wait_ge(c_mm, 2)
            link(A(PEH[:], bank[5][:, 128:130], ACT.Copy))
            act.wait_ge(c_mm, 3)
            for g in range(2):
                for j in range(2):
                    ins = A(HID[:, j, g, :], bank[6 + g][:, 32 * j:32 * j + N_CMP], ACT.Silu, bias=PEH[:, j:j + 1])
                ins.then_inc(c_hid, 1)
            act.wait_ge(c_out, 1)
            A(KC[:, 0:N_CMP], bank[5][:, 0:N_CMP], ACT.Copy)
            A(VC[0:N_CMP].rearrange("p g d -> p (g d)"), bank[5][0:N_CMP, 128:256], ACT.Copy).then_inc(z_row, 1)
            act.wait_ge(z_flip, 1)
            for i in range(2):
                A(ROW[:, i * 512:(i + 1) * 512], bank[6 + i][0:8, :], ACT.Copy).then_inc(z_rowc, 1)
            act.wait_ge(m_conv, 8)
            for k in range(8):
                A(S3[:, k, :], S3[:, k, :], ACT.Silu).then_inc(m_silu, 1)
            act.wait_ge(m_rowd, 1)
            A(RSI, RSI, ACT.Exp)
            A(REM, REM, ACT.Exp, scale=-1.0).then_inc(m_rowx, 1)
            act.wait_ge(m_gt, 1)
            A(GC[:].rearrange("p c h -> p (c h)"), bank[4][:, 0:16], ACT.Copy)
            A(GT2[:].rearrange("p c h -> p (c h)"), bank[4][:, 32:128], ACT.Copy).then_inc(m_gtc, 1)
            for h in range(4):
                act.wait_ge(m_b, h + 1)
                A(T3[:], bank[2][:], ACT.Copy)
                act.wait_ge(m_bd, h + 1)
                for c in range(NT):
                    t = slice(c * P, (c + 1) * P)
                    ins = A(T1[:, t], T1[:, t], ACT.Exp, scale=-1.0, bias=GC[:, c, h:h + 1])
                ins.then_inc(m_e, 1)
                act.wait_ge(m_hq1, h + 1)
                A(T2[:], T1[:], ACT.Square).then_inc(m_hq, 1)
                act.wait_ge(m_rms, h + 1)
                A(T2[:], bank[4][:], ACT.Sqrt, bias=eps6, scale=1.0 / P).then_inc(m_rt, 1)
            attention(nsa_units, NF, Pn, PTn, KD)

            def sigs(name, func, bufs, bias, prev):
                first, n = pairs[name]
                if prev is not None:
                    pair_wait(act, prev)
                act.wait_ge(chunk_done, ends[first])
                for half in range(2):
                    b = bank[2 * (first % 2) + half][:]
                    if bias is None:
                        ins = A(bufs[half][:], b, func)
                    else:
                        ins = A(bufs[half][:], b, func, bias=bias[half])
                ins.then_inc(evacuated[first % 2], 1)

            for i in range(4):
                for n in range(2):
                    prev = f"branch{n}_{i - 1}" if i else None
                    sigs(f"merge{n}_{i}", ACT.Sigmoid, (T1, T2) if n == 0 else (T3, T4),
                         [par("b_merge", 8 * n + 2 * i + half) for half in range(2)], prev)
            norm("ffn")
            for i in range(FF2 // 256):
                if i == 1:
                    act.wait_ge(norm_out, OUT_BEFORE["ffn"])
                sigs(f"gate_{i}", ACT.Silu, (T1, T2) if i % 2 == 0 else (T3, T4), None,
                     f"up_{i - 2}" if i >= 2 else None)
            norm("final")
            for n in range(2 * NT):
                act.wait_ge(fin_t, n + 1)
                A(S2[:, n, :], bank[6 + n % 2][:], ACT.Copy).then_inc(fin_c, 1)

        @block.vector
        def _(dve):
            V = nc.vector
            count = [0]

            def link(ins):
                count[0] += 1
                ins.then_inc(dchain, 1)
                dve.wait_ge(dchain, count[0])

            def evac(name, op):
                first, n = pairs[name]
                for i in range(n):
                    j = first + i
                    dve.wait_ge(chunk_done, ends[j])
                    for half in range(2):
                        ins = op(2 * i + half, bank[2 * (j % 2) + half][:])
                    ins.then_inc(evacuated[j % 2], 1)

            def residual(name):
                evac(name, lambda e, b: V.tensor_tensor(S0[:, e, :], b, S0[:, e, :], ALU.add))

            def norm(name, outs):
                n = NORMS.index(name)
                dve.wait_ge(norm_root, n + 1)
                link(V.reciprocal(rstd[:], rstd[:]))
                for dst, gain in outs:
                    for k in range(KD):
                        V.scalar_tensor_tensor(out=dst[:, k, :], in0=S0[:, k, :], scalar=gain(k), in1=rstd[:],
                                               op0=ALU.mult, op1=ALU.mult).then_inc(norm_out, 1)

            V.memset(S4[:, 0:3, 0:P], 0.0).then_inc(setup_done, 1)
            V.memset(eps6, EPS)
            V.memset(eps6q, EPS * 64)
            V.memset(epsg, GN_EPS)
            V.memset(one1, 1.0).then_inc(setup_done, 1)
            for k in range(KD):
                dve.wait_ge(pe_t, k + 1)
                V.tensor_copy(S0[:, k, :], bank[4 + k % 2][:]).then_inc(pe_tc, 1)
            dve.wait_ge(pe_t, KD + 1)
            link(V.tensor_copy(PK[:], bank[6][:, 0:3 * P]))
            r0 = rows["rwkv_k_a"][0]
            V.tensor_scalar(omka, PK[:, r0:r0 + 8], -1.0, 1.0, ALU.mult, ALU.add)
            norm("rwkv", [(S1, lambda k: par("rwkv_norm_g", k))])
            dve.wait_ge(norm_out, KD)
            V.tensor_scalar(S2[:, :, 0:1], S1[:, :, 0:1], -1.0, None, ALU.mult)
            link(V.tensor_tensor(S2[:, :, 1:T], S1[:, :, 0:T - 1], S1[:, :, 1:T], ALU.subtract))
            for n, m in enumerate((1, 4, 5, 0, 2, 3)):
                if n >= 1:
                    if n <= 3:
                        dve.wait_ge(lora1, (1, 2, 4)[n - 1])
                    else:
                        dve.wait_ge(chunk_done, ends[sum(pairs["rk"[n - 4]]) - 1])
                for k in range(KD):
                    ins = V.scalar_tensor_tensor(out=S3[:, k, :], in0=S2[:, k, :], scalar=par("rwkv_mu", 8 * m + k),
                                                 in1=S1[:, k, :], op0=ALU.mult, op1=ALU.add)
                ins.then_inc(mix_ready, 1)
            pair_wait(dve, "v")

            V.memset(SS[:], 0.0)

            def bc(ap, n):
                return ap.unsqueeze(2).broadcast_to([P, NT, n])

            def aux_read(name, e):
                n = aux_n[name, e]
                dve.wait_ge(aux_filled, n + 1)
                return bank[4 + n % 2][:], aux_evac[n % 2]

            def masked(w, b, e):
                src, done = aux_read(("b", "k")[w] + str(b), e)
                V.tensor_tensor(PROD[:, e % 2, 2 * w:2 * w + 2, 2 * b:2 * b + 2, :].rearrange("p w u n -> p u w n"),
                                src.rearrange("p (u w n) -> p u w n", u=2, w=2),
                                cmat[:, AFTER:AFTER + 2, :].unsqueeze(1).broadcast_to([P, 2, 2, P]), ALU.mult
                                ).then_inc(done, 1)

            def gap(g, S, F):
                if S is not None and g < 12 and g % 3 == 2 and g // 3 < NT - 1:
                    c = g // 3
                    dve.wait_ge(p_st, 3 * S + c + 1)
                    dve.wait_ge(p_y, NT * S + c + 1)
                    for hh in range(2):
                        s = slice(64 * hh, 64 * hh + 64)
                        if c == 0:
                            ins = V.tensor_scalar(SS[s, s], bank[6][s, 2 * P + 64 * hh:2 * P + 64 * hh + 64],
                                                  CE[s, S, 0:1], None, ALU.mult)
                        else:
                            ins = V.tensor_tensor(SS[s, s], bank[6][s, 2 * P + 64 * hh:2 * P + 64 * hh + 64],
                                                  SS[s, s], ALU.add)
                    if c:
                        link(ins)
                        ins = V.tensor_scalar(SS[:], SS[:], CE[:, S, c:c + 1], None, ALU.mult)
                    ins.then_inc(p_stc, 1)
                if F is not None:
                    if g == 0:
                        if F:
                            dve.wait_ge(p_fm, F)
                        V.tensor_scalar(T1[:], S8[:, F, :], par("rwkv_k_k", F), None, ALU.mult).then_inc(p_kk, 1)
                        for c in range(NT):
                            t = slice(c * P, (c + 1) * P)
                            ins = V.tensor_tensor_scan(T3[:, t], ones, S4[:, F, t], 0.0, ALU.mult, ALU.add)
                        link(ins)
                    if g == 1:
                        V.tensor_copy(cmid, c4(T3[:])[:, :, P // 2 - 1])
                        link(V.tensor_copy(cend, c4(T3[:])[:, :, P - 1]))
                        link(V.tensor_tensor(c4(T3[:]), c4(T3[:]), bc(cmid, P), ALU.subtract))
                        V.tensor_tensor(S4[:, F, :], T3[:], S4[:, F, :], ALU.subtract)
                        link(V.tensor_tensor(CE[:, F], cend, cmid, ALU.subtract))
                        V.tensor_tensor(CE[:, F, 0:3], CE[:, F, 0:3], cmid[:, 1:4], ALU.add).then_inc(p_c, 1)
                    if g == 3:
                        aux_wait(dve, "ssq", F)
                        link(V.tensor_scalar(T2[:], T2[:], 1e-12, None, ALU.max))
                        link(V.reciprocal(T2[:], T2[:]))
                    if g == 4:
                        link(V.tensor_tensor(T1[:], T1[:], T2[:], ALU.mult))
                        V.tensor_scalar(T2[:], S5[:, F, :], par("rwkv_k_a", F), omka[:, F:F + 1], ALU.mult, ALU.add)
                    if g == 5:
                        dve.wait_ge(p_exp, F + 1)
                        link(V.scalar_tensor_tensor(out=S4[:, F, :], in0=T1[:], scalar=-1.0, in1=S4[:, F, :],
                                                    op0=ALU.mult, op1=ALU.mult))
                        link(V.tensor_tensor(S8[:, F, :], S8[:, F, :], T2[:], ALU.mult))
                    if g == 6:
                        V.scalar_tensor_tensor(out=T2[:], in0=S7[:, F, :], scalar=par("rwkv_r_k", F),
                                               in1=S8[:, F, :], op0=ALU.mult, op1=ALU.mult)
                        link(V.tensor_tensor(T1[:], T1[:], S5[:, F, :], ALU.mult))
                    if g == 7:
                        if F:
                            dve.wait_ge(aux_filled, aux_n["t1", F - 1] + 1)
                        link(V.tensor_tensor(BK[:, 1, :], S8[:, F, :], T3[:], ALU.mult))
                        V.tensor_tensor(BK[:, 0, :], T1[:], T3[:], ALU.mult)
                    if g == 8:
                        V.tensor_tensor(S8[:, F, :], S7[:, F, :], T4[:], ALU.mult).then_inc(p_fm, 1)
                    if g == 12:
                        b, done = aux_read("bon", F)
                        V.scalar_tensor_tensor(out=S5[:, F, :], in0=b, scalar=float(HD), in1=S1[:, F, :],
                                               op0=ALU.mult, op1=ALU.mult).then_inc(done, 1)
                        if S is not None:
                            dve.wait_ge(p_y, NT * (S + 1))
                    if 12 <= g < 16:
                        for b in (0, 1):
                            masked((g - 12) // 2, 2 * (g % 2) + b, F)
                if S is not None:
                    if g == 13:
                        b, done = aux_read("mean", S)
                        V.tensor_tensor(T5, T5, b, ALU.subtract).then_inc(done, 1)
                    if g == 17:
                        aux_wait(dve, "var", S)
                        link(V.reciprocal(T6, T6))
                        link(V.tensor_tensor(T5, T5, T6, ALU.mult))
                        link(V.tensor_scalar(T5, T5, par("rwkv_lnx_w", S), par("rwkv_lnx_b", S), ALU.mult, ALU.add))
                        link(V.tensor_tensor(T5, T5, S5[:, S, :], ALU.add))
                        V.tensor_tensor(S7[:, S, :], T5, S6[:, S, :], ALU.mult).then_inc(p_out, 1)

            for it in range(KD + 2):
                L, S, F = tiles_at(it)
                for lv in range(6):
                    gap(3 * lv, S, F)
                    for hh in range(2):
                        if L is None:
                            continue
                        n = 12 * L + 2 * lv + hh
                        dve.wait_ge(p_d, n + 1)
                        u4 = slice(4 * hh, 4 * hh + 4)
                        if lv < 5:
                            V.tensor_tensor(M0[:, u4], c4(bank[2 + hh][:]), M0[:, u4], ALU.add).then_inc(p_dc, 1)
                        else:
                            if hh == 0 and S is not None:
                                dve.wait_ge(p_y, NT * (S + 1))
                            V.tensor_tensor(MTF[:, u4], c4(bank[2 + hh][:]), M1[:, u4], ALU.add).then_inc(p_dc, 1)
                    gap(3 * lv + 1, S, F)
                    gap(3 * lv + 2, S, F)
            residual("rwkv_o")
            norm("mlp0", [(S1, lambda k: par("mlp_norm_g", k))])
            residual("mlp0_out")
            norm("kv", [(S1, lambda k: par("kv_norm_g", k)), (S2, lambda k: par("attn_norm_g", k))])
            dve.wait_ge(f_rows, 1)
            link(V.tensor_scalar(T1[0:16, :], T1[0:16, :], 0.0, None, ALU.min))
            link(V.tensor_tensor(T2[0:16, :], T2[0:16, :], T1[0:16, :], ALU.subtract))
            link(V.memset(T3[0:16, :], 1.0))
            V.tensor_tensor_scan(NC, T3[0:16, :], T2[0:16, :], 0.0, ALU.mult, ALU.add).then_inc(f_cum, 1)
            for n in range(2 * KD):
                e = n % KD
                r = (T3, T4)[n % 2][:]
                dve.wait_ge(h_rt, n + 1)
                link(V.reciprocal(r, r))
                if n < KD:
                    ins = V.scalar_tensor_tensor(out=S3[:, e, :], in0=S3[:, e, :], scalar=par("k_norm_g", e), in1=r,
                                                 op0=ALU.mult, op1=ALU.mult)
                else:
                    for hh in range(2):
                        s = slice(64 * hh, 64 * hh + 64)
                        ins = V.scalar_tensor_tensor(out=QZ[hh][s, e, :], in0=S5[s, e, :],
                                                     scalar=par("q_norm_g", e)[s], in1=r[s],
                                                     op0=ALU.mult, op1=ALU.mult)
                ins.then_inc(h_out, 1)

            def attention(units, base, Pt, PTt, s_banks):
                N, NS = len(units), len(s_banks)
                for i in range(N + 1):
                    if i < N:
                        u = units[i]
                        if u["rowbias"] is not None:
                            dve.wait_ge(a_cbc, u["rowbias"] + 1)
                        dve.wait_ge(a_s, base + i + 1)
                        if i >= 4:
                            dve.wait_ge(a_t, base + i - 3)
                        p = Pt[:, i % 4, 0:u["w"]]
                        m = mx[:, i % 4:i % 4 + 1]
                        link(V.tensor_tensor_reduce(p, bank[s_banks[i % NS]][:, 0:u["w"]], u["bias"], 1.0, -3e38,
                                                    ALU.add, ALU.max, m))
                        V.tensor_scalar(m, m, -1e20, -1.0, ALU.max, ALU.mult).then_inc(a_l, 1)
                    if i >= 1:
                        n = i - 1
                        u = units[n]
                        dve.wait_ge(a_e, base + n + 1)
                        r = rs[:, n % 4:n % 4 + 1]
                        p = Pt[:, n % 4, 0:u["w"]]
                        if u["clamp"]:
                            link(V.tensor_scalar(r, r, 1e-30, None, ALU.max))
                        link(V.reciprocal(r, r))
                        if u["gate"] is None:
                            V.tensor_scalar(p, p, r, None, ALU.mult).then_inc(a_p, 1)
                        else:
                            V.tensor_scalar(p, p, r, u["gate"], ALU.mult, ALU.mult).then_inc(a_p, 1)

            attention(fox_units, 0, Pb, PTb, (3, 4, 5))
            residual("fox_o")
            norm("mlp1", [(S1, lambda k: par("mlp_norm_g", 8 + k))])
            residual("mlp1_out")
            V.memset(TB[32:33, :], NEG)
            V.memset(WSM, 0.0).then_inc(s_wz, 1)
            norm("mix", [(S1, lambda k: par("g_norm_mix_2", k))])
            dve.wait_ge(s_small_w, 16 * 10)

            def evac_tm(name, dst, bias):
                first, n = pairs[name]
                for i in range(n):
                    j = first + i
                    dve.wait_ge(chunk_done, ends[j])
                    for half in range(2):
                        ins = V.tensor_tensor(dst[:, 2 * half:2 * half + 2, 256 * i:256 * i + 256],
                                              bank[2 * (j % 2) + half][:].rearrange("p (t n) -> p t n", t=2),
                                              bias[:, 256 * i:256 * i + 256].unsqueeze(1).broadcast_to([P, 2, 256]),
                                              ALU.add)
                    ins.then_inc(evacuated[j % 2], 1)

            evac_tm("mv", MVT, BMV[:])
            evac("nq", lambda e, b: V.tensor_scalar(NQT[:, e, :], b, par("b_nq", e), HD ** -0.5, ALU.add, ALU.mult))
            evac("kvc", lambda e, b: V.tensor_scalar(KVC[:, e, :], b, par("b_nkv", e), None, ALU.add))
            evac("ksw", lambda e, b: V.tensor_scalar((KS, KW)[e], b, par("b_nkv", 2 + 2 * e), None, ALU.add))
            evac_tm("vsw", VSW, BVS)
            dve.wait_ge(m_rowx, 1)
            V.tensor_scalar(RMU, RMU, small[0:4, 34:35], small[0:4, 35:36], ALU.add, ALU.add).then_inc(m_rowx2, 1)
            dve.wait_ge(m_rowx, 2)
            link(V.tensor_scalar(RMU, RMU, 0.0, None, ALU.min))
            link(V.tensor_tensor(RMU, RMU, T2[0:4, :], ALU.subtract))
            for c in range(NT):
                t = slice(c * P, (c + 1) * P)
                ins = V.tensor_tensor_scan(REM[:, t], ones[0:4, :], RMU[:, t], 0.0, ALU.mult, ALU.add)
            link(ins)
            link(V.tensor_tensor(RG, RI, REM, ALU.subtract))
            link(V.memset(small[0:4, 40:41], 0.0))
            for c in range(NT):
                t = slice(c * P, (c + 1) * P)
                mp = small[0:4, 40 + c:41 + c]
                link(V.tensor_tensor_scan(RMU[:, t], RG[:, t], RG[:, t], mp, ALU.max, ALU.max))
                V.tensor_scalar(RSI[:, t], RMU[:, t], mp, -1.0, ALU.subtract, ALU.mult)
                ins = V.tensor_tensor(REM[:, t], REM[:, t], RMU[:, t], ALU.add)
                if c < NT - 1:
                    link(ins)
                    link(V.tensor_copy(small[0:4, 41 + c:42 + c], REM[:, (c + 1) * P - 1:(c + 1) * P]))
            ins.then_inc(m_rowd, 1)
            pair_wait(dve, "mo")
            for k in range(8):
                link(V.tensor_scalar(S3[:, k, :], S2[:, k, :], par("conv_qk_2", 24 + k), None, ALU.mult))
                for j in (2, 1, 0):
                    d = 3 - j
                    ins = V.scalar_tensor_tensor(out=S3[:, k, d:T], in0=S2[:, k, 0:T - d],
                                                 scalar=par("conv_qk_2", 8 * j + k), in1=S3[:, k, d:T],
                                                 op0=ALU.mult, op1=ALU.add)
                    if j:
                        link(ins)
                ins.then_inc(m_conv, 1)
            for k in range(4, 8):
                dve.wait_ge(m_silu, k + 1)
                ins = V.tensor_scalar(S3[:, k, :], S3[:, k, :], P ** -0.5, None, ALU.mult)
            ins.then_inc(m_kscaled, 1)
            dve.wait_ge(m_kscaled, 1)
            for h in range(4):
                dve.wait_ge(m_b, h + 1)
                V.tensor_tensor(c4(T1[:]), c4(bank[4][:]), mat(LATE_POS).unsqueeze(1).broadcast_to([P, 4, P]),
                                ALU.add).then_inc(m_bd, 1)
                V.tensor_tensor(QS[:], S3[:, h, :], bank[6][:], ALU.mult)
                V.tensor_copy(DC[:], c4(bank[6][:])[:, :, P - 1])
                dve.wait_ge(m_e, h + 1)
                dve.wait_ge(m_kt, h + 1)
                V.tensor_tensor(PM[:], T1[:], bank[5][:], ALU.mult)
                for c in range(NT):
                    t = slice(c * P, (c + 1) * P)
                    ins = V.tensor_scalar(KWT[:, t], bank[7][:, t], T1[:, (c + 1) * P - 1:(c + 1) * P], None, ALU.mult)
                ins.then_inc(m_pd, 1)
                for c in range(NT - 1):
                    dve.wait_ge(m_cn, 3 * h + c + 1)
                    if c == 0:
                        ins = V.tensor_copy(CN[:, 1, :], bank[3][:, 0:256])
                    else:
                        ins = V.scalar_tensor_tensor(out=CN[:, c + 1, :], in0=CN[:, c, :], scalar=DC[:, c:c + 1],
                                                     in1=bank[3][:, 0:256], op0=ALU.mult, op1=ALU.add)
                    ins.then_inc(m_cnd, 1)
                    dve.wait_ge(m_cnd, 3 * h + c + 1)
                dve.wait_ge(m_num, h + 1)
                link(V.scalar_tensor_tensor(out=T3[:], in0=bank[1][:], scalar=-1.0, in1=T3[:],
                                            op0=ALU.mult, op1=ALU.max))
                link(V.tensor_tensor(T3[:], bank[1][:], T3[:], ALU.max))
                link(V.reciprocal(T3[:], T3[:]))
                V.tensor_tensor(T1[:], bank[0][:], T3[:], ALU.mult).then_inc(m_hq1, 1)
                dve.wait_ge(m_rt, h + 1)
                link(V.reciprocal(T2[:], T2[:]))
                link(V.tensor_tensor(T1[:], T1[:], T2[:], ALU.mult))
                V.scalar_tensor_tensor(out=YM[:, h, :], in0=T1[:], scalar=par("g_mlstm_head_2", h), in1=OG[:, h, :],
                                       op0=ALU.mult, op1=ALU.mult).then_inc(m_y, 1)
            for h in range(8):
                dve.wait_ge(z_flip, h + 2)
                V.memset(Z[h][:, 512:896], NEG)
                V.tensor_copy(Z[h][:, 0:512], bank[6 + h % 2][:]).then_inc(z_flipc, 1)
            dve.wait_ge(m_gtc, 1)
            attention(nsa_units, NF, Pn, PTn, (2, 3, 4, 5))
            for i in range(4):
                for n in range(2):
                    bufs = (T1, T2) if n == 0 else (T3, T4)
                    pair_wait(dve, f"merge{n}_{i}")
                    j = pairs[f"branch{n}_{i}"][0]
                    dve.wait_ge(chunk_done, ends[j])
                    for half in range(2):
                        b = bank[2 * (j % 2) + half][:]
                        if n == 0:
                            ins = V.tensor_tensor(S2[:, 2 * i + half, :], b, bufs[half][:], ALU.mult)
                        else:
                            link(V.tensor_tensor(bufs[half][:], b, bufs[half][:], ALU.mult))
                            ins = V.tensor_tensor(S2[:, 2 * i + half, :], S2[:, 2 * i + half, :], bufs[half][:],
                                                  ALU.add)
                    ins.then_inc(evacuated[j % 2], 1)
            residual("w_out")
            norm("ffn", [(S1, lambda k: par("g_norm_ffn_2", k))])
            for i in range(FF2 // 256):
                bufs = (T1, T2) if i % 2 == 0 else (T3, T4)
                pair_wait(dve, f"gate_{i}")
                j = pairs[f"up_{i}"][0]
                dve.wait_ge(chunk_done, ends[j])
                for half in range(2):
                    t = 2 * i + half
                    ins = V.tensor_tensor(slab[2 + t // KD][:, t % KD, :], bank[2 * (j % 2) + half][:],
                                          bufs[half][:], ALU.mult)
                ins.then_inc(evacuated[j % 2], 1)
            residual("down")
            norm("final", [(S1, lambda k: par("g_final_2", k))])


NAMES = ["x", "rwkv_norm_g", "rwkv_mu", "rwkv_w_rkv", "rwkv_w0", "rwkv_w1", "rwkv_w2", "rwkv_a0", "rwkv_a1",
         "rwkv_a2", "rwkv_g1", "rwkv_g2", "rwkv_k_k", "rwkv_k_a", "rwkv_r_k", "rwkv_lnx_w", "rwkv_lnx_b",
         "rwkv_w_o", "kv_norm_g", "kv_w", "kv_f_bias", "k_norm_g", "attn_norm_g", "attn_w_q", "q_norm_g",
         "attn_w_o", "mlp_norm_g", "mlp_w_in", "mlp_w_out", "g_norm_mix_2", "w_in_2", "b_in_2", "b_fgate_2",
         "conv_qk_2", "g_mlstm_head_2", "pe_cmp_2", "w_cmp1_2", "w_cmp2_2", "rel_bias_2", "w_branch_2",
         "w_out_2", "g_norm_ffn_2", "w_gate_2", "w_up_2", "w_down_2", "g_final_2"]


def kernel(**inputs):
    import concourse.bacc as bacc
    from concourse.bass_utils import run_bass_kernel_spmd

    nc = bacc.Bacc("TRN2", target_bir_lowering=False, num_devices=1)
    arrays, aps = {}, {}
    given = {n: np.ascontiguousarray(inputs[n]) for n in NAMES}
    given.update(constants())
    for name, v in given.items():
        arrays[f"in_{name}"] = v
        aps[name] = nc.dram_tensor(f"in_{name}", v.shape, mybir.dt.from_np(v.dtype), kind="ExternalInput").ap()
    out = nc.dram_tensor("out_0", (1, T, D), F32, kind="ExternalOutput").ap()
    scratch = nc.dram_tensor("rel_scratch", (8, 1024), F32, kind="Internal").ap()
    build(nc, aps, out, scratch)
    r = run_bass_kernel_spmd(nc, [arrays], core_ids=[0])
    return r.results[0]["out_0"]
```

```python
import math
from contextlib import ExitStack

import numpy as np
import concourse.bass as bass
from concourse import mybir
from concourse.alu_op_type import AluOpType as ALU

ACT = mybir.ActivationFunctionType
F32 = mybir.dt.float32
F32R = mybir.dt.float32r
AX_X = mybir.AxisListType.X

P = 128
T = 512
D = 1024
KD = D // P
NT = T // P
CHUNK = 128
HD = 64
EPS = 1e-6
GN_EPS = 64e-5
FF1 = 4096
FF2 = 2816
NEG = -1e30
DECAY_UNIT = math.exp(-0.5)

MQ, MK, MV, MO, MI, MF, NQ, NKV, NG, MERGE = 0, 512, 1024, 1536, 2048, 2052, 2056, 2568, 3336, 3360
N_CMP = (T - 32) // 16 + 1
REL_N = 1023

IDENT, ONES, HALFMEAN, FLIP, CAUSAL_NEG, LATE_POS, AFTER, FROM, LEVEL = 0, 1, 2, 3, 4, 5, 6, 7, 8
SLOTS = 4


def constants():
    a = np.arange(P)
    i, j = a[:, None], a[None, :]
    mats = [
        i == j,
        np.ones((P, P)),
        (i // HD == j // HD) / HD,
        i + j == P - 1,
        np.where(j > i, NEG, 0.0),
        np.where(i > j, -NEG, 0.0),
        j > i,
        j >= i,
    ]
    for s in (1, 2, 4, 8, 16, 32, 64):
        low = (i // (2 * s) == j // (2 * s)) & ((i // s) % 2 == 1) & ((j // s) % 2 == 0)
        mats += [low, low.T]
    cmat = np.stack([np.asarray(m, np.float32) for m in mats], 1).reshape(P, -1)
    sel = np.repeat(np.eye(16, dtype=np.float32), P, axis=1)
    dist = 511 - np.arange(1024)
    n = np.maximum(dist, 0)
    nf = np.maximum(n, 1).astype(np.float32)
    large = 16 + (np.log(nf / 16) / np.float32(math.log(64)) * 16).astype(np.int32)
    bucket = np.where(n < 16, n, np.minimum(large, 31))
    onehot = np.zeros((33, 1024), np.float32)
    onehot[bucket, np.arange(1024)] = dist >= 0
    onehot[32] = dist < 0
    return {"c_mat": cmat, "c_sel": sel, "c_onehot": onehot}


def param_rows():
    spec = [("rwkv_norm_g", 8), ("rwkv_mu", 48), ("rwkv_w0", 8), ("rwkv_a0", 8), ("rwkv_k_k", 8),
            ("rwkv_k_a", 8), ("rwkv_r_k", 8), ("rwkv_lnx_w", 8), ("rwkv_lnx_b", 8),
            ("kv_norm_g", 8), ("attn_norm_g", 8),
            ("k_norm_g", 8), ("q_norm_g", 8), ("mlp_norm_g", 16), ("g_norm_mix_2", 8),
            ("b_mqk", 8), ("b_mo", 4), ("b_nq", 4), ("b_nkv", 6), ("b_merge", 16),
            ("conv_qk_2", 32), ("g_mlstm_head_2", 4), ("g_norm_ffn_2", 8), ("g_final_2", 8)]
    place, at = {}, 0
    for name, n in spec:
        if at // P != (at + n - 1) // P:
            at = (at // P + 1) * P
        place[name] = (at, n)
        at += n
    assert at <= 3 * P
    return place


N_PAR = len(param_rows()) + 1


def build(nc, a, out, scratch):
    ctx = ExitStack()
    with ctx:
        def sb(name, shape):
            return ctx.enter_context(nc.sbuf_tensor(name, shape, F32))

        def sem(name):
            return ctx.enter_context(nc.semaphore(name))

        slabs_at = -(-nc.sbuf_base // 32) * 32
        SL = sb("slabs", [P, 9, KD, T])
        SR = [nc.alloc_sbuf_tensor_at(f"slab{i}_rounded", [P, KD, T], F32R, offset=slabs_at + 4 * KD * T * i)
              for i in range(9)]
        slab = [SL[:, i] for i in range(9)]
        ring = sb("ring", [P, SLOTS, KD, 256])
        cmat = sb("cmat", [P, 22, P])
        PK = sb("PK", [P, 3 * P])
        T1, T2, T3, T4 = (sb(f"T{i}", [P, T]) for i in (1, 2, 3, 4))
        ar_at = -(-nc.sbuf_base // 32) * 32
        AR = sb("AR", [P, NT, 2, P])
        AR_rounded = nc.alloc_sbuf_tensor_at("AR_rounded", [P, NT * 2 * P], F32R, offset=ar_at)
        BK = sb("BK", [P, 2, T])
        CE = sb("CE", [P, KD, 4])
        SS = sb("SS", [P, P])
        RT = sb("RT", [P, P])
        SA = sb("SA", [P, P])
        small = sb("small", [P, 64])
        eps6, eps6q, epsg, one1 = (small[:, i:i + 1] for i in range(4))
        omka = small[:, 4:12]
        cmid = small[:, 12:16]
        cend = small[:, 16:20]
        bank = [ctx.enter_context(nc.psum_tensor(f"bank{i}", [P, T], F32)) for i in range(8)]

        rows = param_rows()

        def par(name, i=0):
            r = rows[name][0] + i
            return PK[:, r:r + 1]

        def mat(i, n=1):
            return cmat[:, i:i + n, :].rearrange("p a b -> p (a b)")

        def c4(ap):
            return ap.rearrange("p (c t) -> p c t", t=CHUNK)

        S0, S1, S2, S3, S4, S5, S6, S7, S8 = slab
        rstd = T4

        def flat(s):
            return s[:].rearrange("p k t -> p (k t)")

        stream = []
        pairs = {}
        ends = []
        pair_chunks = []
        split = {}
        n_pairs = [0]

        def chunk(parts, nk):
            g = len(stream)
            stream.append((g % SLOTS, [(ring[:, g % SLOTS, 0:nk, c0:c0 + src.shape[-1]], src)
                                       for c0, src in parts], nk))
            return g

        def add_pair(name, k_tiles, parts_of, halves=False):
            j = n_pairs[0]
            if name in pairs and pairs[name][0] + pairs[name][1] == j:
                pairs[name] = (pairs[name][0], pairs[name][1] + 1)
            else:
                pairs[name] = (j, 1)
            mine = []
            for k0 in range(0, k_tiles, KD):
                nk = min(KD, k_tiles - k0)
                mine.append((chunk(parts_of(k0, nk), nk), k0, nk))
                if halves:
                    split[mine[-1][0]] = len(split)
            pair_chunks.append(mine)
            ends.append(len(stream))
            n_pairs[0] += 1

        def cols(w, c0, n=256):
            return lambda k0, nk: [(0, w[k0 * P:(k0 + nk) * P, c0:c0 + n].rearrange("(k p) n -> p k n", p=P))]

        def gemm_plan(name, w, k_tiles, c0, n, halves=False):
            for i in range(n // 256):
                add_pair(name, k_tiles, cols(w, c0 + 256 * i), halves)

        def mlp_order(parts):
            order = [("in", 0)]
            for q in range(1, parts):
                order += [("in", q)] + ([("out", q - 1)] if q else [])
            return order + [("out", parts - 1)]

        MLP_PARTS = FF1 // 1024

        def mlp_plan(i):
            w1, w2 = a["mlp_w_in"][i], a["mlp_w_out"][i]
            for kind, q in mlp_order(MLP_PARTS):
                if kind == "in":
                    gemm_plan(f"mlp{i}_in{q}", w1, KD, D * q, D, True)
                else:
                    gemm_plan(f"mlp{i}_out{q}", w2[D * q:D * (q + 1), :], KD, 0, D, True)

        w_rkv = a["rwkv_w_rkv"][0]
        gemm_plan("r", w_rkv[0], KD, 0, D)
        gemm_plan("k", w_rkv[1], KD, 0, D)
        gemm_plan("v", w_rkv[2], KD, 0, D)
        gemm_plan("rwkv_o", a["rwkv_w_o"][0], KD, 0, D)
        mlp_plan(0)
        gemm_plan("fk", a["kv_w"], KD, 0, D, True)
        gemm_plan("fv", a["kv_w"], KD, D, D, True)
        gemm_plan("fq", a["attn_w_q"][0], KD, 0, D, True)
        gemm_plan("fox_o", a["attn_w_o"][0], KD, 0, D, True)
        mlp_plan(1)
        w_in = a["w_in_2"][0]
        gemm_plan("mqk", w_in, KD, MQ, 1024)
        gemm_plan("mv", w_in, KD, MV, 512)
        gemm_plan("mo", w_in, KD, MO, 512)

        def two(c0, c1):
            def parts(k0, nk):
                return [(0, w_in[:, c0:c0 + P].rearrange("(k p) n -> p k n", p=P)),
                        (P, w_in[:, c1:c1 + P].rearrange("(k p) n -> p k n", p=P))]
            return parts

        add_pair("kvc", KD, two(NKV, NKV + 128))

        def nq_tile(slot_col, r):
            return [(slot_col + 64 * g, w_in[:, NQ + 256 * g + 64 * r:NQ + 256 * g + 64 * r + 64]
                     .rearrange("(k p) n -> p k n", p=P)) for g in range(2)]

        for i in range(2):
            add_pair("nq", KD, lambda k0, nk, i=i: nq_tile(0, 2 * i) + nq_tile(P, 2 * i + 1))
        add_pair("ksw", KD, two(NKV + 256, NKV + 512))
        add_pair("vsw", KD, two(NKV + 384, NKV + 640))
        w_br = a["w_branch_2"][0]

        def branch_cols(n, c0):
            if n == 0:
                return lambda k0, nk: [(0, w_br[0][:, c0:c0 + 256].rearrange("(k p) n -> p k n", p=P))]
            return lambda k0, nk: [(0, w_br[1][:, c0:c0 + 256])]

        for i in range(4):
            for n in range(2):
                add_pair(f"merge{n}_{i}", KD, cols(w_in, MERGE + D * n + 256 * i), True)
                add_pair(f"branch{n}_{i}", 4, branch_cols(n, 256 * i), True)
        gemm_plan("w_out", a["w_out_2"][0], KD, 0, D, True)
        FFN_PARTS = -(-FF2 // 1024)
        ffn_part = [range(4 * q, min(4 * q + 4, FF2 // 256)) for q in range(FFN_PARTS)]
        for kind, q in mlp_order(FFN_PARTS):
            if kind == "in":
                for i in ffn_part[q]:
                    add_pair(f"gate_{i}", KD, cols(a["w_gate_2"][0], 256 * i), True)
                    add_pair(f"up_{i}", KD, cols(a["w_up_2"][0], 256 * i), True)
            else:
                gemm_plan(f"down{q}", a["w_down_2"][0][D * q:D * q + 256 * len(ffn_part[q]), :],
                          2 * len(ffn_part[q]), 0, D, True)

        loads, landed, total = [], [], [0] * SLOTS
        for slot, parts, nk in stream:
            dmas = []
            for dst, src in parts:
                if len(src.shape) == 2 or src.shape[0] == 512:
                    for g in range(2):
                        dmas.append((ring[64 * g:64 * g + 64, slot, 0:4, :],
                                     src[256 * g:256 * g + 256, :].rearrange("(r d) n -> d r n", d=64)))
                else:
                    dmas.append((dst, src))
            total[slot] += 16 * len(dmas)
            loads.append(dmas)
            landed.append(total[slot])

        def split_range(name0, name1):
            first = split[pair_chunks[pairs[name0][0]][0][0]]
            last = split[pair_chunks[sum(pairs[name1]) - 1][-1][0]]
            return first, last

        s_const, s_x, s_par, s_lora, s_ffw, s_small_w, s_cmp, s_bias = (
            sem(n) for n in ("const_loaded", "x_loaded", "params_loaded", "lora_loaded", "fgate_w_loaded",
                             "small_w_loaded", "cmp_w_loaded", "bias_rows_loaded"))
        s_x = [s_x, sem("x_second_half_loaded")]
        s_const2 = sem("const_rest_loaded")
        s_oh, s_relst, s_hankel, s_wz = (sem(n) for n in ("onehot_loaded", "rel_stored", "hankel_loaded",
                                                          "small_w_zeroed"))
        slot_loaded = [sem(f"slot{i}_loaded") for i in range(SLOTS)]
        chunk_done = sem("chunk_multiplied")
        evacuated = [sem(f"pair_evacuated{i}") for i in range(2)]
        pe_t, pe_tc = sem("turned"), sem("turned_copied")
        norm_sq, norm_mm, norm_root, norm_out = (sem(n) for n in ("norm_squared", "norm_summed", "norm_rooted",
                                                                  "norm_written"))
        dchain, achain = sem("vector_chain"), sem("scalar_chain")
        mix_ready, lora1, lora1_out, lora2 = (sem(n) for n in ("mix_written", "lora1_done",
                                                                         "lora1_evacuated", "lora2_done"))
        lora2_out = sem("lora2_evacuated")
        setup_done = sem("setup_done")
        (p_kk, p_sq, p_c, p_exp, p_fm, p_x, p_xc, p_d, p_dc, p_t, p_tc, p_i, p_it, p_ic, p_ns,
         p_r, p_rc, p_sa, p_sac, p_st, p_stc, p_y, p_yc, p_cen2, p_out) = (
            sem("rwkv_" + n) for n in (
                "kk_raw", "kk_squared", "logs", "exps", "factors",
                "x", "x_copied", "d", "d_added", "m_turned", "m_turned_copied", "start_t", "start_turned",
                "start_copied", "n_masked", "r", "r_copied", "sa", "sa_copied", "state", "state_updated",
                "y", "y_copied", "centred_squared", "out"))
        aux_filled = sem("aux_filled")
        aux_evac = [sem(f"aux_evacuated{i}") for i in range(2)]
        (h_sq, h_mm, h_rt, h_out) = (sem("headnorm_" + n) for n in ("squared", "summed", "rooted", "written"))
        (f_mm, f_rows, f_cum) = (sem("fgate_" + n) for n in ("product", "rows", "summed"))
        (a_cb, a_cbc, a_s, a_l, a_e, a_p, a_t, a_tc, a_pv, a_o) = (
            sem("attn_" + n) for n in ("rowbias", "rowbias_copied", "scores", "logits", "exp", "probs", "turned",
                                       "turned_copied", "pv", "out_copied"))
        a_olo, f_w = sem("attn_out_split"), sem("fgate_w_split")
        (m_conv, m_silu, m_rows, m_rowx, m_rowd, m_gt, m_gtc) = (
            sem("mlstm_" + n) for n in ("conv", "silu", "rows", "row_parts", "row_done", "g_turned", "g_columns"))
        (m_b, m_bd, m_e, m_kt, m_pd, m_cn, m_cnd, m_num, m_hq, m_rms, m_rt, m_y) = (
            sem("mlstm_" + n) for n in ("bcast", "exponent", "exps", "kq", "probs", "state", "state_updated", "num",
                                        "h_squared", "rms", "rooted", "y"))
        (c_mm, c_hid, c_out, c_outc, z_row, z_rowc, z_flip, z_flipc) = (
            sem(n) for n in ("cmp_hidden", "cmp_silu", "cmp_out", "cmp_copied", "rel_row", "rel_row_copied",
                             "rel_flip", "rel_bias_ready"))
        w_hi, w_lo = sem("weights_hi"), sem("weights_lo")
        norm_h, norm_hi, hidden_lo = sem("norm_value"), sem("norm_hi"), sem("hidden_lo")
        q_zeroed = sem("query_halves_zeroed")
        m_kscaled = sem("mlstm_keys_scaled")
        m_rowx2, m_hq1, m_em, m_emc = (sem(n) for n in ("mlstm_f_row", "mlstm_h", "mlstm_bound",
                                                        "mlstm_bound_copied"))
        s_dup = sem("cmp_inputs_doubled")
        u_hi, u_lo, y_hi, y_lo = (sem(n) for n in ("mix_input_hi", "mix_input_lo", "mixers_out_hi", "mixers_out_lo"))
        fin_t, fin_c, s_out = (sem(n) for n in ("final_turned", "final_copied", "stored"))

        PROD = SL[:, 2:4].rearrange("p s k t -> p (s k t)").rearrange("p (b w u n) -> p b w u n", b=2, w=4, u=8)
        rflat = ring[:].rearrange("p s k n -> p (s k n)")
        T5, T6 = rflat[:, 0:512], rflat[:, 512:1024]
        MT2, M0, M1, MTF, XX = (rflat[:, 1024 * i:1024 * (i + 1)].rearrange("p (u n) -> p u n", u=8)
                                for i in range(1, 6))
        NS = rflat[:, 6144:8192].rearrange("p (b u n) -> p b u n", b=2, u=8)
        KT = AR[:].rearrange("p c w t -> p (c w t)").rearrange("p (b t) -> p b t", b=2)
        lw1 = flat(S7)[:, 0:512].rearrange("p (k n) -> p k n", k=KD)
        la1 = flat(S7)[:, 512:1024].rearrange("p (k n) -> p k n", k=KD)
        lg1 = flat(S7)[:, 1024:2304].rearrange("p (k n) -> p k n", k=KD)
        lw2 = flat(S7)[0:64, 2304:3328]
        la2 = flat(S8)[0:64, 0:1024]
        lg2 = flat(S8)[:, 1024:2048]
        lg2b = flat(S8)[0:32, 2048:3072]
        KMIX = [T1[:], T2[:], T3[:], T4[:], BK[:, 0], BK[:, 1]] + [
            AR[:].rearrange("p c w t -> p (c w t)")[:, T * i:T * (i + 1)] for i in range(2)]
        LH = AR[:].rearrange("p c w t -> p (c w t)").rearrange("p (w t) -> p w t", w=2)
        HHI, HLO = SR[1][:], SR[2][:]
        HID_HI = [SR[3][:], SR[5][:]]
        HID_LO = [SR[4][:], SR[6][:]]
        w_hi_buf, w_lo_buf, w_hi_buf_o, w_lo_buf_o = (
            SR[i][:].rearrange("p k t -> p (k t)").rearrange("p (b k n) -> p b k n", b=2, k=KD) for i in (7, 8, 1, 2))

        def weights_split(ci):
            first, last = split_range("fox_o", "fox_o")
            hi, lo = (w_hi_buf_o, w_lo_buf_o) if first <= ci <= last else (w_hi_buf, w_lo_buf)
            return hi[:, ci % 2], lo[:, ci % 2]

        wff = RT[:].rearrange("p (k n) -> p k n", k=KD)
        WFF_HI, WFF_LO = (AR_rounded[:, 128 * i:128 * (i + 1)].rearrange("p (k n) -> p k n", k=KD) for i in range(2))
        KV_IN, Q_IN, FOX_OUT = [SR[1][:], SR[2][:]], [SR[5][:], SR[6][:]], [SR[7][:], SR[5][:]]
        fb = small[0:16, 24:25]
        NC, FLOGIT = BK[0:16, 0], BK[0:16, 1]
        FPLUS, FONES = (AR[:].rearrange("p c w t -> p (c w t)")[0:16, T * i:T * (i + 1)] for i in range(2))
        CB = flat(S8)[:, 2560:3584].rearrange("p (b t) -> p b t", b=2)
        Pb = S6
        PTS = (T1, T2, T3, T4)
        P_BUFS, TURN_LAG, VALUE_LAG = KD, 3, 5
        mx = small[:, 26:31]
        rs = small[:, 56:61]
        QZ = [S2, S1]
        FV = flat(S4).rearrange("p (t n) -> p t n", t=NT)
        ident = mat(IDENT)
        ones = mat(ONES)
        halfmean = mat(HALFMEAN)

        fox_units = []
        for e in range(KD):
            for hh in range(2):
                h = 2 * e + hh
                for tq in range(NT):
                    w = P * (tq + 1)
                    fox_units.append(dict(
                        q=QZ[hh][:, e, tq * P:tq * P + P], k=S3[:, e, 0:w], mask=True, w=w,
                        bias=CB[:, h % 2, 0:w], gate=None, clamp=False,
                        v=[FV[:, s, h * HD:h * HD + HD] for s in range(tq + 1)],
                        out=bank[e % 2][64 * hh:64 * hh + 64, tq * P:tq * P + P], first=True, last=True,
                        rowbias=h if tq == 0 else None,
                        next_rowbias=h + 1 if (tq == 1 and h + 1 < 16) else None, e=e, ends_e=(hh == 1 and tq == NT - 1)))
        SM = flat(S6)
        YM = S6[:, 0:4, :]
        YN = S6[:, 4:8, :]
        MVT = flat(S4)[:, 0:2048].rearrange("p (t n) -> p t n", t=NT)
        OG = S4[:, 4:8, :]
        NQT = S5[:, 0:4, :]
        KVC = S5[:, 4:6, :]
        KS = S5[:, 6, :]
        KW = S5[:, 7, :]
        Z = [(S7 if h < 4 else S8)[:].rearrange("p k t -> p (k t)")[:, 1024 * (h % 4):1024 * (h % 4) + 896]
             for h in range(8)]
        VSW = BK[:].rearrange("p b t -> p (b t)").rearrange("p (t n) -> p t n", t=NT)
        U, Y, MIXED = [SR[4][:], SR[2][:]], [SR[3][:], SR[6][:]], [SR[5][:], SR[1][:]]
        GT2 = sb("GT2", [P, NT, 24])
        KC = sb("KC", [P, 32])
        VC = sb("VC", [P, 2, 64])
        GC = sb("GC", [P, NT, 4])
        DC = sb("DC", [P, NT])
        PEH = sb("PEH", [P, 2])
        late = cmat[:, LEVEL:LEVEL + 14, :].rearrange("p a b -> p (a b)")
        RSI, REM, SELM, BVS = late[0:4, 0:512], late[0:4, 512:1024], late[0:4, 1024:1536], late[:, 1536:1792]
        GR, RI, RG, RMU = S6[0:24, 0, :], S6[0:4, 1, :], S6[0:4, 2, :], S6[0:4, 3, :]
        WSM = flat(S6)[:, 2048:3072].rearrange("p (k n) -> p k n", k=KD)
        OH = flat(S6)[0:33, 3072:4096]
        CN = flat(S6)[:, 2048:3072].rearrange("p (c n) -> p c n", c=4)
        KWT, PM = S6[:, 6, :], S6[:, 7, :]
        ROW = AR[0:8].rearrange("p c w t -> p (c w t)")
        BMV, QS = T3, T4
        HID = SS[:, 0:4 * N_CMP].rearrange("p (j g c) -> p j g c", j=2, g=2)
        W2C = SA[:].rearrange("p (j d) -> p j d", j=2)
        W1C = flat(S7).rearrange("p (j q n) -> p j q n", j=2, q=16)
        DUP = flat(S8)[:, 0:4 * T].rearrange("p (j g t) -> p j g t", j=2, g=2)
        PEC, PET = RT[0:32, :], CE[:].rearrange("p k c -> p (k c)")
        BETWEEN = [("mo", 0), ("mo", 1), ("kvc", 0), ("nq", 0), ("nq", 1), ("ksw", 0), ("vsw", 0)]
        HK = S2[:]
        TB = small[0:33, 48:56]
        nsa_units = []
        for r in range(4):
            for g in range(2):
                h = 4 * g + r
                for tq in range(NT):
                    for b, br in enumerate(("cmp", "sel", "win")):
                        w = N_CMP if br == "cmp" else P * (tq + 1)
                        keys = {"cmp": KC[64 * g:64 * g + 64, 0:N_CMP], "sel": KS[64 * g:64 * g + 64, 0:w],
                                "win": KW[64 * g:64 * g + 64, 0:w]}[br]
                        if br == "cmp":
                            y0 = 415 - P * tq
                            bias = Z[h][:, y0:y0 + 16 * (N_CMP - 1) + 1:16]
                            v = [VC[0:N_CMP, g, :]]
                        else:
                            bias = Z[h][:, 384 - P * tq:512]
                            off = (0 if br == "sel" else 128) + 64 * g
                            v = [VSW[:, s, off:off + 64] for s in range(tq + 1)]
                        nsa_units.append(dict(
                            q=NQT[64 * g:64 * g + 64, r, tq * P:tq * P + P], k=keys, mask=False, w=w, bias=bias,
                            gate=GT2[:, tq, h * 3 + b:h * 3 + b + 1], clamp=(br == "cmp"), v=v,
                            out=bank[r % 2][64 * g:64 * g + 64, tq * P:tq * P + P],
                            first=(b == 0), last=(b == 2), rowbias=None, next_rowbias=None, e=r,
                            ends_e=(g == 1 and tq == NT - 1 and b == 2)))
        NF, NN = len(fox_units), len(nsa_units)

        aux_n = {}
        for it in range(KD + 2):
            for name in ("ssq", "bon", "b0", "b1", "b2", "b3", "mean", "k0", "k1", "k2", "k3", "var",
                         "t0", "t1", "t2"):
                e = it - 2 if name in ("mean", "var") else it
                if 0 <= e < KD:
                    aux_n[name, e] = len(aux_n)

        def tiles_at(it):
            return tuple(e if 0 <= e < KD else None for e in (it - 1, it - 2, it))
        Pn = S3

        def merge_gates(n, i):
            return (T3, T4) if n else (T1, T2) if i % 2 == 0 else (BK[:, 0], BK[:, 1])

        def pair_wait(eng, name):
            first, n = pairs[name]
            for j in range(max(first, first + n - 2), first + n):
                eng.wait_ge(evacuated[j % 2], j // 2 + 1)

        chunk_of = {ci: g for g, ci in split.items()}

        def aux_wait(eng, name, e):
            n = aux_n[name, e]
            eng.wait_ge(aux_evac[n % 2], n // 2 + 1)

        NORMS = ["rwkv", "mlp0", "kv", "mlp1", "mix", "ffn", "final"]
        SPLIT_BEFORE = {"mlp0": 0, "kv": KD, "mlp1": 3 * KD, "ffn": 4 * KD}
        X_AFTER = {"rwkv": None, "mlp0": "rwkv_o", "kv": "mlp0_out3", "mlp1": "fox_o", "mix": "mlp1_out3",
                   "ffn": "w_out", "final": "down2"}
        OUT_BEFORE = {}
        n_out = 0
        for n in NORMS:
            n_out += 16 if n == "kv" else 8
            OUT_BEFORE[n] = n_out

        block = ctx.enter_context(nc.Block())

        @block.sync
        def _(sp):
            def load(dst, src, s):
                sp.dma_start(dst, src).then_inc(s, 16)

            for half in range(2):
                f = slice(half * T, (half + 1) * T)
                load(flat(S3).rearrange("p (t f) -> p t f", t=NT)[:, :, f],
                     a["x"][0].rearrange("(t p) f -> p t f", p=P)[:, :, f], s_x[half])
            b_in = a["b_in_2"][0]
            bnq = b_in[NQ:NQ + 512].rearrange("(g r d) -> g r d", g=2, r=4)
            src = {
                "b_mqk": b_in[0:1024].rearrange("(k p) -> k p", p=P),
                "b_mo": b_in[MO:MO + 512].rearrange("(k p) -> k p", p=P),
                "b_nkv": b_in[NKV:NKV + 768].rearrange("(k p) -> k p", p=P),
                "b_merge": b_in[MERGE:MERGE + 2048].rearrange("(k p) -> k p", p=P),
                "rwkv_mu": a["rwkv_mu"][0].rearrange("m (k p) -> (m k) p", p=P),
                "rwkv_r_k": a["rwkv_r_k"][0].rearrange("(k h) d -> k (h d)", h=2),
                "k_norm_g": a["k_norm_g"].rearrange("(k h) d -> k (h d)", h=2),
                "q_norm_g": a["q_norm_g"][0].rearrange("(k h) d -> k (h d)", h=2),
                "mlp_norm_g": a["mlp_norm_g"].rearrange("m (k p) -> (m k) p", p=P),
                "conv_qk_2": a["conv_qk_2"][0].rearrange("m (k p) -> (m k) p", p=P),
                "kv_norm_g": a["kv_norm_g"].rearrange("(k p) -> k p", p=P),
                "g_final_2": a["g_final_2"].rearrange("(k p) -> k p", p=P),
            }
            sp.wait_ge(setup_done, 1)
            n = 0
            for name, (r0, k) in rows.items():
                dst = S4[r0 % P:r0 % P + k, r0 // P, 0:P]
                if name == "b_nq":
                    for g in range(2):
                        load(dst[:, 64 * g:64 * g + 64], bnq[g], s_par)
                        n += 1
                    continue
                s = src[name] if name in src else a[name][0].rearrange("(k p) -> k p", p=P)
                load(dst, s, s_par)
                n += 1
            assert n == N_PAR
            sp.wait_ge(s_x[1], 16)
            for g, dmas in enumerate(loads):
                if g >= SLOTS and g - SLOTS in split:
                    sp.wait_ge(w_lo, split[g - SLOTS] + 1)
                elif g >= SLOTS:
                    sp.wait_ge(chunk_done, g - SLOTS + 1)
                if g == pair_chunks[pairs["rwkv_o"][0]][0][0]:
                    sp.wait_ge(p_out, KD)
                for dst, src in dmas:
                    sp.dma_start(dst, src).then_inc(slot_loaded[g % SLOTS], 16)
            for t in range(NT):
                sp.wait_ge(fin_c, 2 * (t + 1))
                sp.dma_start(out[0, t * P:(t + 1) * P, :], S2[:, 2 * t:2 * t + 2, :].rearrange("p k t -> p (k t)")
                             ).then_inc(s_out, 16)
            sp.wait_ge(s_out, 16 * NT)

        @block.gpsimd
        def _(pool):
            def load(dst, src, s):
                pool.dma_start(dst, src).then_inc(s, 16)

            def split_lo(name0, name1):
                split_lo_chunks(*split_range(name0, name1))

            def split_lo_chunks(first, last):
                for ci in range(first, last + 1):
                    g = chunk_of[ci]
                    nk = stream[g][2]
                    hi, lo = weights_split(ci)
                    pool.wait_ge(w_hi, ci + 1)
                    nc.gpsimd.tensor_tensor(lo[:, 0:nk], ring[:, g % SLOTS, 0:nk], hi[:, 0:nk].bitcast(F32),
                                            ALU.subtract).then_inc(w_lo, 1)

            b_in = a["b_in_2"][0]
            early = cmat[:].rearrange("p a b -> p (a b)")[:, 0:HALFMEAN * P]
            load(early, a["c_mat"][:, 0:HALFMEAN * P], s_const)
            load(lw1, a["rwkv_w1"][0].rearrange("(k p) n -> p k n", p=P), s_lora)
            load(lw2, a["rwkv_w2"][0], s_lora)
            load(la1, a["rwkv_a1"][0].rearrange("(k p) n -> p k n", p=P), s_lora)
            load(la2, a["rwkv_a2"][0], s_lora)
            load(lg1, a["rwkv_g1"][0].rearrange("(k p) n -> p k n", p=P), s_lora)
            load(lg2, a["rwkv_g2"][0][0:P, :], s_lora)
            load(lg2b, a["rwkv_g2"][0][P:160, :], s_lora)
            load(cmat[:].rearrange("p a b -> p (a b)")[:, HALFMEAN * P:], a["c_mat"][:, HALFMEAN * P:], s_const2)
            load(fb, a["kv_f_bias"].rearrange("(p n) -> p n", n=1), s_bias)
            pool.wait_ge(s_const2, 16)
            for F in range(KD):
                nt = PROD[:, F % 2, 0]
                aux_wait(pool, "b2", F)
                aux_wait(pool, "b3", F)
                if F:
                    pool.wait_ge(p_d, 12 * (F - 1) + 2)
                nc.gpsimd.tensor_tensor(MT2, nt, mat(LEVEL + 1).unsqueeze(1).broadcast_to([P, 8, P]), ALU.mult
                                        ).then_inc(p_i, 1)
                pool.wait_ge(p_i, 2 * F + 1)
                nc.gpsimd.tensor_tensor(MT2, MT2, ident.unsqueeze(1).broadcast_to([P, 8, P]), ALU.add
                                        ).then_inc(p_i, 1)
                for lv in range(6):
                    m = 6 * F + lv
                    if m >= 2:
                        pool.wait_ge(p_x, 2 * (m - 1))
                    nc.gpsimd.tensor_tensor(NS[:, m % 2], nt,
                                            mat(LEVEL + 3 + 2 * lv).unsqueeze(1).broadcast_to([P, 8, P]), ALU.mult
                                            ).then_inc(p_ns, 1)
            pool.wait_ge(p_out, KD)
            load(wff, a["kv_w"][:, 2 * D:2 * D + 16].rearrange("(k p) n -> p k n", p=P), s_ffw)
            split_lo("mlp0_in0", "mlp0_out3")
            split_lo("fk", "fv")
            first, last = split_range("fq", "fq")
            split_lo_chunks(first, first + 1)
            pool.wait_ge(f_mm, 1)
            pool.wait_ge(w_lo, first + 2)
            nc.gpsimd.memset(S2[64:128, :, :], 0.0).then_inc(q_zeroed, 1)
            pool.wait_ge(q_zeroed, 1)
            split_lo_chunks(first + 2, last)
            for e in range(0, KD, 2):
                pool.wait_ge(h_out, KD + e + 2)
                nc.gpsimd.memset(S1[0:64, e:e + 2, :], 0.0).then_inc(q_zeroed, 1)
                pool.wait_ge(q_zeroed, e // 2 + 2)
            split_lo("fox_o", "fox_o")
            split_lo("mlp1_in0", "mlp1_out3")
            pair_wait(pool, "mlp1_out3")
            pool.wait_ge(s_wz, 1)
            load(WSM[:, :, 0:4], w_in[:, MI:MI + 4].rearrange("(k p) n -> p k n", p=P), s_small_w)
            load(WSM[:, :, 32:36], w_in[:, MF:MF + 4].rearrange("(k p) n -> p k n", p=P), s_small_w)
            load(WSM[:, :, 64:88], w_in[:, NG:NG + 24].rearrange("(k p) n -> p k n", p=P), s_small_w)
            load(small[0:4, 33:34], b_in[MI:MI + 4].rearrange("(p n) -> p n", n=1), s_small_w)
            load(small[0:4, 34:35], b_in[MF:MF + 4].rearrange("(p n) -> p n", n=1), s_small_w)
            load(small[0:4, 35:36], a["b_fgate_2"].rearrange("a n -> n a"), s_small_w)
            load(small[0:24, 36:37], b_in[NG:NG + 24].rearrange("(p n) -> p n", n=1), s_small_w)
            load(BMV[:], b_in[MV:MV + 512].partition_broadcast(P), s_small_w)
            load(BVS[:, 0:128], b_in[NKV + 384:NKV + 512].partition_broadcast(P), s_small_w)
            load(BVS[:, 128:256], b_in[NKV + 640:NKV + 768].partition_broadcast(P), s_small_w)
            load(PEC, a["pe_cmp_2"][0].rearrange("j (q h) d -> (j q) (h d)", h=2), s_oh)
            load(OH, a["c_onehot"], s_oh)
            load(TB[0:32, :], a["rel_bias_2"], s_oh)
            load(SELM, a["c_sel"][0:4, 0:512], s_oh)
            for j in range(2):
                load(W1C[:, j], a["w_cmp1_2"][0][j].rearrange("(q r) n -> r q n", r=P), s_cmp)
            load(W2C[:, 0, :], a["w_cmp2_2"][0][0], s_cmp)
            load(W2C[:, 1, :], a["w_cmp2_2"][0][1], s_cmp)
            pool.wait_ge(z_rowc, 2)
            pool.dma_start(scratch, ROW).then_inc(s_relst, 16)
            pool.wait_ge(s_relst, 16)
            pool.wait_ge(m_conv, 8)
            hank = bass.AP(scratch.tensor, 0, [[1, P], [1024, 8], [1, 512]])
            load(HK, hank, s_hankel)
            pair_wait(pool, "kvc")
            for odd in range(2):
                for g in range(2):
                    load(DUP[64 * odd:64 * odd + 64, :, g, 0:T - odd], KVC[64 * g:64 * g + 64, :, odd:T], s_dup)
            pool.wait_ge(u_hi, 1)
            pool.wait_ge(z_flip, 9)
            for half in range(2):
                k = slice(4 * half, 4 * half + 4)
                nc.gpsimd.tensor_tensor(U[1][:, k], S1[:, k], U[0][:, k].bitcast(F32), ALU.subtract
                                        ).then_inc(u_lo, 1)
            first, _ = split_range("merge0_0", "merge0_0")
            for n in range(8):
                if n:
                    pool.wait_ge(w_lo, first + 2 * n + 1)
                    split_lo_chunks(first + 2 * n + 1, first + 2 * n + 1)
                else:
                    split_lo_chunks(first, first + 1)
            split_lo("w_out", "w_out")
            split_lo("gate_0", "down2")

        @block.tensor
        def _(pe):
            def norm_sums(name, k0, k1):
                n = NORMS.index(name)
                for k in range(k0, k1):
                    pe.wait_ge(norm_sq, 8 * n + k + 1)
                    pe.matmul(bank[4][:], ones, (T1, T2)[k % 2][:], start=(k == 0), stop=(k == KD - 1)
                              ).then_inc(norm_mm, 1)

            def gemm(name, rhs, tm=False, pair=None, then=None):
                first, n = pairs[name]
                for j in range(first, first + n) if pair is None else (first + pair,):
                    if j >= 2:
                        pe.wait_ge(evacuated[j % 2], j // 2)
                    b = 2 * (j % 2)
                    last_k = pair_chunks[j][-1][1] + pair_chunks[j][-1][2] - 1
                    for g, k0, nk in pair_chunks[j]:
                        pe.wait_ge(slot_loaded[g % SLOTS], landed[g])
                        w = ring[:, g % SLOTS]
                        if tm:
                            for t in range(NT):
                                for k in range(nk):
                                    mm = pe.matmul(bank[b + t // 2][:, 256 * (t % 2):256 * (t % 2) + 256],
                                                   rhs(k)[:, t * P:(t + 1) * P], w[:, k, :],
                                                   start=(k == 0), stop=(k == nk - 1))
                        else:
                            for half in range(2):
                                for k in range(nk):
                                    mm = pe.matmul(bank[b + half][:], w[:, k, half * P:(half + 1) * P], rhs(k0 + k),
                                                   start=(k0 + k == 0), stop=(k0 + k == last_k))
                        mm.then_inc(chunk_done, 1)
                    if then and j > first:
                        norm_sums(then, 2 * (j - first) - 2, 2 * (j - first))

            def gemm_split(name, rhs, ready=None, tm=False, pair=None, then=None):
                first, n = pairs[name]
                for j in range(first, first + n) if pair is None else (first + pair,):
                    if j >= 2:
                        pe.wait_ge(evacuated[j % 2], j // 2)
                    b = 2 * (j % 2)
                    (g, k0, nk), = pair_chunks[j]
                    w_hi_of, w_lo_of = weights_split(split[g])
                    pe.wait_ge(w_lo, split[g] + 1)
                    if tm:
                        for t in range(NT):
                            o = bank[b + t // 2][:, 256 * (t % 2):256 * (t % 2) + 256]
                            for k in range(nk):
                                hi, lo = (x[:, t * P:(t + 1) * P] for x in rhs(k))
                                pe.matmul(o, hi, w_hi_of[:, k], start=(k == 0), stop=False)
                                pe.matmul(o, hi, w_lo_of[:, k], start=False, stop=False)
                                mm = pe.matmul(o, lo, w_hi_of[:, k], start=False, stop=(k == nk - 1))
                        mm.then_inc(chunk_done, 1)
                        continue
                    for half in range(2):
                        h = slice(half * P, (half + 1) * P)
                        for k in range(nk):
                            if ready is not None and j == first and half == 0:
                                ready(k)
                            hi, lo = rhs(k)
                            pe.matmul(bank[b + half][:], w_hi_of[:, k, h], hi, start=(k == 0), stop=False)
                            pe.matmul(bank[b + half][:], w_hi_of[:, k, h], lo, start=False, stop=False)
                            mm = pe.matmul(bank[b + half][:], w_lo_of[:, k, h], hi, start=False, stop=(k == nk - 1))
                    mm.then_inc(chunk_done, 1)
                    if then and j > first:
                        norm_sums(then, 2 * (j - first) - 2, 2 * (j - first))

            def norm(name):
                norm_sums(name, KD - 2 if X_AFTER[name] else 0, KD)

            pe.wait_ge(s_const, 16)
            xt = flat(S3).rearrange("p (t f) -> p t f", t=NT)
            for k in range(KD):
                pe.wait_ge(s_x[k // 4], 16)
                if k >= 2:
                    pe.wait_ge(pe_tc, k - 1)
                for t in range(NT):
                    mm = pe.transpose(bank[4 + k % 2][:, t * P:(t + 1) * P], xt[:, t, k * P:(k + 1) * P], ident)
                mm.then_inc(pe_t, 1)
            pe.wait_ge(pe_tc, KD)
            norm("rwkv")
            pe.wait_ge(s_par, 16 * N_PAR)
            for i in range(3):
                mm = pe.transpose(bank[6][:, i * P:(i + 1) * P], S4[:, i, 0:P], ident)
            mm.then_inc(pe_t, 1)

            pe.wait_ge(s_lora, 16 * 7)
            w1s = [[(lw1, 0, 64)], [(la1, 0, 64)], [(lg1, 0, 128), (lg1, 128, 32)]]
            q = 0
            nl = 0
            for i in range(3):
                for n, (w, c0, m) in enumerate(w1s[i]):
                    if nl >= 2:
                        pe.wait_ge(lora1_out, nl - 1)
                    for k in range(KD):
                        pe.wait_ge(mix_ready, KD * i + k + 1)
                        mm = pe.matmul(bank[4 + nl % 2][0:m, :], w[:, k, c0:c0 + m], S3[:, k, :],
                                       start=(k == 0), stop=(k == KD - 1))
                    mm.then_inc(lora1, 1)
                    nl += 1
                pe.wait_ge(lora1_out, nl)
                for e in range(KD):
                    if q >= 2:
                        pe.wait_ge(lora2_out, q - 1)
                    o = bank[6 + q % 2][:]
                    if i < 2:
                        mm = pe.matmul(o, (lw2, la2)[i][:, e * P:(e + 1) * P], LH[0:64, i, :], start=True, stop=True)
                    else:
                        pe.matmul(o, lg2[:, e * P:(e + 1) * P], LH[:, 0, :], start=True, stop=False)
                        mm = pe.matmul(o, lg2b[:, e * P:(e + 1) * P], LH[0:32, 1, :], start=False, stop=True)
                    mm.then_inc(lora2, 1)
                    q += 1
            for i, name in enumerate("rkv"):
                pe.wait_ge(mix_ready, KD * (4 + i))
                gemm(name, (lambda k: KMIX[k]) if name == "k" else (lambda k: S3[:, k, :]))

            pe.wait_ge(s_const2, 16)

            def aux(name, e):
                n = aux_n[name, e]
                if n >= 2:
                    pe.wait_ge(aux_evac[n % 2], n // 2)
                return bank[4 + n % 2]

            def scan_r(e, c):
                n = NT * e + c
                if c == 0:
                    pe.wait_ge(p_dc, 12 * (e + 1))
                    aux_wait(pe, "t1", e)
                    aux_wait(pe, "t2", e)
                else:
                    pe.wait_ge(p_stc, n - e)
                    pe.matmul(bank[6][:, 0:P], S4[:, e, c * P:(c + 1) * P], SS[:], start=True, stop=False)
                for hh in range(2):
                    at = c * P + 64 * hh
                    mm = pe.matmul(bank[6][:, 64 * hh:64 * hh + 64], PROD[:, e % 2, 2, 4 * hh + c],
                                   S1[:, e, at:at + 64], start=(c == 0), stop=(c == 0 or hh == 1))
                mm.then_inc(p_r, 1)

            def scan_sa(e, c):
                n = NT * e + c
                pe.wait_ge(p_rc, n + 1)
                for hh in range(2):
                    mm = pe.matmul(bank[6][:, P + 64 * hh:P + 64 * hh + 64], MTF[:, 4 * hh + c],
                                   RT[:, 64 * hh:64 * hh + 64], start=True, stop=True)
                mm.then_inc(p_sa, 1)

            def scan_y(e, c):
                n = NT * e + c
                t = slice(c * P, (c + 1) * P)
                pe.wait_ge(p_sac, n + 1)
                if c < NT - 1:
                    pe.matmul(bank[6][:, 2 * P:3 * P], S7[:, e, t], SA[:], start=True, stop=False)
                    pe.matmul(bank[6][:, 2 * P:3 * P], KT[:, e % 2, t], S1[:, e, t], start=False, stop=True
                              ).then_inc(p_st, 1)
                if c == 0 and e:
                    pe.wait_ge(p_yc, e)
                for hh in range(2):
                    u = 4 * hh + c
                    o = bank[7][64 * hh:64 * hh + 64, t]
                    hc = slice(64 * hh, 64 * hh + 64)
                    at = c * P + 64 * hh
                    if c:
                        pe.matmul(o, SS[:, hc], S8[:, e, t], start=True, stop=False)
                    pe.matmul(o, SA[:, hc], PROD[:, e % 2, 1, u], start=(c == 0), stop=False)
                    mm = pe.matmul(o, S1[:, e, at:at + 64], PROD[:, e % 2, 3, u], start=False, stop=True)
                mm.then_inc(p_y, 1)

            def products(w, b, e):
                o = aux(("b", "k")[w] + str(b), e)
                for u in (2 * b, 2 * b + 1):
                    hh, c = u // 4, u % 4
                    s = slice(64 * hh, 64 * hh + 64)
                    mm = pe.matmul(o[:, 256 * (u % 2):256 * (u % 2) + 256], BK[s, w, c * P:(c + 1) * P],
                                   SL[s, 4:9:4, e, c * P:(c + 1) * P], start=True, stop=True)
                mm.then_inc(aux_filled, 1)

            def gap(g, S, F):
                if S is not None and g < 12:
                    (scan_r, scan_sa, scan_y)[g % 3](S, g // 3)
                if F is not None:
                    if g == 1:
                        pe.wait_ge(p_sq, F + 1)
                        pe.matmul(aux("ssq", F)[:], halfmean, T2[:], start=True, stop=True).then_inc(aux_filled, 1)
                    if g == 12:
                        pe.wait_ge(p_fm, F + 1)
                        pe.matmul(aux("bon", F)[:], halfmean, T2[:], start=True, stop=True).then_inc(aux_filled, 1)
                    if 12 <= g < 16:
                        for b in (0, 1):
                            products((g - 12) // 2, 2 * (g % 2) + b, F)
                if S is not None:
                    if g == 13:
                        pe.wait_ge(p_yc, S + 1)
                        pe.matmul(aux("mean", S)[:], halfmean, T5, start=True, stop=True).then_inc(aux_filled, 1)
                    if g == 15:
                        pe.wait_ge(p_cen2, S + 1)
                        pe.matmul(aux("var", S)[:], halfmean, T6, start=True, stop=True).then_inc(aux_filled, 1)
                if F is not None:
                    if g == 16:
                        for w, src in enumerate((BK[:, 0], BK[:, 1], S1[:, F])):
                            o = aux(f"t{w}", F)
                            for c in range(NT):
                                mm = pe.transpose(o[:, c * P:(c + 1) * P], src[:, c * P:(c + 1) * P], ident)
                            mm.then_inc(aux_filled, 1)
                    if g == 17:
                        pe.wait_ge(p_i, 2 * F + 2)
                        for hh in range(2):
                            if F:
                                pe.wait_ge(p_xc, 12 * F - 1 + hh)
                            for c in range(NT):
                                mm = pe.transpose(bank[hh][:, c * P:(c + 1) * P], MT2[:, 4 * hh + c], ident)
                            mm.then_inc(p_it, 1)

            for it in range(KD + 2):
                L, S, F = tiles_at(it)
                for lv in range(6):
                    for hh in range(2):
                        if L is None:
                            continue
                        n = 12 * L + 2 * lv + hh
                        if hh == 0:
                            pe.wait_ge(p_ns, 6 * L + lv + 1)
                        if lv == 0:
                            pe.wait_ge(p_ic, 2 * L + hh + 1)
                        else:
                            pe.wait_ge(p_tc, 10 * L + 2 * (lv - 1) + hh + 1)
                        for c in range(NT):
                            mm = pe.matmul(bank[hh][:, c * P:(c + 1) * P], NS[:, (6 * L + lv) % 2, 4 * hh + c],
                                           M0[:, 4 * hh + c], start=True, stop=True)
                        mm.then_inc(p_x, 1)
                    gap(3 * lv, S, F)
                    for hh in range(2):
                        if L is None:
                            continue
                        n = 12 * L + 2 * lv + hh
                        pe.wait_ge(p_xc, n + 1)
                        if n >= 2:
                            pe.wait_ge(p_dc, n - 1)
                        mt = MT2 if lv == 0 else M1
                        for c in range(NT):
                            u = 4 * hh + c
                            if lv < 5:
                                mm = pe.matmul(bank[2 + hh][:, c * P:(c + 1) * P], mt[:, u], XX[:, u],
                                               start=True, stop=True)
                            else:
                                mm = pe.matmul(bank[2 + hh][:, c * P:(c + 1) * P], XX[:, u], mt[:, u],
                                               start=True, stop=True)
                        mm.then_inc(p_d, 1)
                    gap(3 * lv + 1, S, F)
                    for hh in range(2):
                        if L is None or lv == 5:
                            continue
                        pe.wait_ge(p_dc, 12 * L + 2 * lv + hh + 1)
                        for c in range(NT):
                            mm = pe.transpose(bank[hh][:, c * P:(c + 1) * P], M0[:, 4 * hh + c], ident)
                        mm.then_inc(p_t, 1)
                    gap(3 * lv + 2, S, F)
            pe.wait_ge(p_out, KD)
            gemm("rwkv_o", lambda k: S7[:, k, :], then="mlp0")

            def normed(name):
                return lambda k: pe.wait_ge(norm_out, OUT_BEFORE[name] - KD + k + 1)

            def h_of(k):
                return HHI[:, k], HLO[:, k]

            def hidden_of(q):
                return lambda k: (HID_HI[q % 2][:, k], HID_LO[q % 2][:, k])

            def mlp(i):
                norm(f"mlp{i}")
                for kind, q in mlp_order(MLP_PARTS):
                    if kind == "in":
                        gemm_split(f"mlp{i}_in{q}", h_of, normed(f"mlp{i}") if q == 0 else None)
                    else:
                        pe.wait_ge(hidden_lo, 4 * (MLP_PARTS * i + q + 1))
                        gemm_split(f"mlp{i}_out{q}", hidden_of(q),
                                   then=("kv", "mix")[i] if q == MLP_PARTS - 1 else None)

            mlp(0)

            def row_of(h):
                return ident[0:16, h:h + 1].broadcast_to([16, P])

            def head_norm(n):
                pe.wait_ge(h_sq, n + 1)
                if n >= 2:
                    pe.wait_ge(h_rt, n - 1)
                pe.matmul(bank[4 + n % 2][:], halfmean, (T1, T2)[n % 2][:], start=True, stop=True).then_inc(h_mm, 1)

            norm("kv")
            kv_in = lambda k: tuple(x[:, k] for x in KV_IN)
            q_in = lambda k: tuple(x[:, k] for x in Q_IN)
            gemm_split("fk", kv_in, lambda k: pe.wait_ge(norm_out, OUT_BEFORE["kv"] - 2 * KD + k + 1))
            for i in range(4):
                gemm_split("fv", kv_in, tm=True, pair=i)
                head_norm(2 * i)
                head_norm(2 * i + 1)
            pe.wait_ge(f_w, 2)
            for k in range(KD):
                hi, lo = kv_in(k)
                pe.matmul(bank[6][0:16, :], WFF_HI[:, k], hi, start=(k == 0), stop=False)
                pe.matmul(bank[6][0:16, :], WFF_HI[:, k], lo, start=False, stop=False)
                mm = pe.matmul(bank[6][0:16, :], WFF_LO[:, k], hi, start=False, stop=(k == KD - 1))
            mm.then_inc(f_mm, 1)
            pe.wait_ge(norm_out, OUT_BEFORE["kv"])
            for i in range(5):
                if i < 4:
                    gemm_split("fq", q_in, pair=i)
                if i >= 1:
                    head_norm(KD + 2 * i - 2)
                    head_norm(KD + 2 * i - 1)
            pe.wait_ge(f_cum, 1)

            def attention(units, base, Pt, o_sem, o_base, s_banks):
                N, NS = len(units), len(s_banks)
                for i in range(N + VALUE_LAG):
                    if i < N:
                        u = units[i]
                        if u["rowbias"] is not None and u["rowbias"] % 2 == 0:
                            pe.wait_ge(h_out, KD + u["e"] + 1)
                            pe.wait_ge(q_zeroed, u["e"] // 2 + 2)
                        if u["rowbias"] is not None and i == 0:
                            pe.matmul(bank[2][:], row_of(0), NC, start=True, stop=True).then_inc(a_cb, 1)
                        if u["next_rowbias"] is not None:
                            h = u["next_rowbias"]
                            pe.wait_ge(a_cbc, h)
                            pe.matmul(bank[2][:], row_of(h), NC, start=True, stop=True
                                      ).then_inc(a_cb, 1)
                        if i >= NS:
                            pe.wait_ge(a_l, base + i - NS + 1)
                        s = bank[s_banks[i % NS]]
                        mm = pe.matmul(s[:, 0:u["w"]], u["q"], u["k"], start=True, stop=not u["mask"])
                        if u["mask"]:
                            mm = pe.matmul(s[:, u["w"] - P:u["w"]], ident, mat(CAUSAL_NEG), start=False, stop=True)
                        mm.then_inc(a_s, 1)
                    if TURN_LAG <= i < N + TURN_LAG:
                        n = i - TURN_LAG
                        u = units[n]
                        pe.wait_ge(a_p, base + n + 1)
                        if n >= 2:
                            pe.wait_ge(a_tc, base + n - 1)
                        b = bank[6 + n % 2]
                        if u["w"] == N_CMP:
                            mm = pe.transpose(b[0:N_CMP, 0:P], Pt[:, n % P_BUFS, 0:N_CMP], ident)
                        else:
                            for s in range(len(u["v"])):
                                mm = pe.transpose(b[:, s * P:(s + 1) * P], Pt[:, n % P_BUFS, s * P:(s + 1) * P], ident)
                        mm.then_inc(a_t, 1)
                    if i >= VALUE_LAG:
                        n = i - VALUE_LAG
                        u = units[n]
                        pe.wait_ge(a_tc, base + n + 1)
                        if u["first"] and u["e"] >= 2:
                            pe.wait_ge(o_sem, o_base + u["e"] - 1)
                        K = N_CMP if u["w"] == N_CMP else P
                        for s, v in enumerate(u["v"]):
                            mm = pe.matmul(u["out"], v, PTS[n % 4][0:K, s * P:(s + 1) * P],
                                           start=(u["first"] and s == 0), stop=(u["last"] and s == len(u["v"]) - 1))
                        mm.then_inc(a_pv, 1)

            attention(fox_units, 0, Pb, a_olo, 0, (3, 4, 5))
            gemm_split("fox_o", lambda k: tuple(x[:, k] for x in FOX_OUT), lambda k: pe.wait_ge(a_olo, k + 1),
                       then="mlp1")
            mlp(1)

            norm("mix")
            pe.wait_ge(norm_out, OUT_BEFORE["mix"])
            u1 = lambda k: S1[:, k, :]
            pe.wait_ge(s_small_w, 16 * 10)
            for k in range(KD):
                mm = pe.matmul(bank[4][:], WSM[:, k, :], S1[:, k, :], start=(k == 0), stop=(k == KD - 1))
            mm.then_inc(m_rows, 1)
            pe.wait_ge(s_oh, 16 * 4)
            for i in range(2):
                mm = pe.matmul(bank[6 + i][0:8, :], TB, OH[:, i * 512:(i + 1) * 512], start=True, stop=True)
            mm.then_inc(z_flip, 1)
            pe.transpose(bank[5][:, 0:32], PEC, ident[0:32, 0:32]).then_inc(c_mm, 1)
            gemm("mqk", u1)
            pe.wait_ge(c_hid, 1)
            pe.wait_ge(s_cmp, 16 * 4)
            for j in range(2):
                for q in range(16):
                    mm = pe.matmul(bank[5][:, 128 + j:129 + j], W1C[:, j, q, :], PET[:, 16 * j + q:16 * j + q + 1],
                                   start=(q == 0), stop=(q == 15))
            mm.then_inc(c_mm, 1)
            pe.wait_ge(m_rowd, 1)
            for c in range(NT):
                mm = pe.transpose(bank[4][:, 4 * c:4 * c + 4], RG[0:4, c * P:(c + 1) * P], ident[0:4, 0:4])
            for c in range(NT):
                mm = pe.transpose(bank[4][:, 32 + 24 * c:32 + 24 * c + 24], GR[0:24, c * P:(c + 1) * P],
                                  ident[0:24, 0:24])
            mm.then_inc(m_gt, 1)
            gemm("mv", u1, tm=True)

            def between(n):
                if n < len(BETWEEN):
                    name, i = BETWEEN[n]
                    gemm(name, u1, tm=(name == "vsw"), pair=i)
                else:
                    pair_wait(pe, "vsw")
                    pe.wait_ge(s_dup, 16 * 4)
                    for j in range(2):
                        for q in range(16):
                            mm = pe.matmul(bank[2][:, 64 * j:64 * j + 2 * N_CMP], W1C[:, j, q, :],
                                           DUP[:, j, :, 2 * q:2 * q + 16 * (N_CMP - 1) + 1:16],
                                           start=(q == 0), stop=(q == 15))
                    mm.then_inc(c_mm, 1)

            pe.wait_ge(m_silu, 8)
            pe.wait_ge(z_rowc, 2)
            pe.wait_ge(m_gtc, 1)
            pe.wait_ge(m_rowx, 3)
            pe.wait_ge(m_kscaled, 1)
            pair_wait(pe, "mv")
            for h in range(4):
                if h:
                    pe.wait_ge(m_y, h)
                sh = SELM[:, h * P:(h + 1) * P]
                pe.matmul(bank[4][:], sh, RMU, start=True, stop=True)
                pe.matmul(bank[6][:], sh, RSI, start=True, stop=True).then_inc(m_b, 1)
                for c in range(NT):
                    t = slice(c * P, (c + 1) * P)
                    pe.matmul(bank[5][:, t], S3[:, 4 + h, t], S3[:, h, t], start=True, stop=True)
                for c in range(NT):
                    t = slice(c * P, (c + 1) * P)
                    mm = pe.transpose(bank[7][:, t], S3[:, 4 + h, t], ident)
                mm.then_inc(m_kt, 1)
                pe.wait_ge(m_bd, h + 1)
                pe.matmul(bank[4][:], sh, REM, start=True, stop=True).then_inc(m_em, 1)
                between(2 * h)
                pe.wait_ge(m_pd, h + 1)
                for c in range(NT):
                    t = slice(c * P, (c + 1) * P)
                    v = MVT[:, c, h * P:(h + 1) * P]
                    if c < NT - 1:
                        if c == 1:
                            pe.wait_ge(m_emc, h + 1)
                        if c == 2:
                            pe.wait_ge(m_cnd, 3 * h + 1)
                        b = bank[5 - c % 2]
                        pe.matmul(b[:, 0:P], KWT[:, t], v, start=True, stop=True)
                        pe.matmul(b[:, P:2 * P], KWT[:, t], ones, start=True, stop=True).then_inc(m_cn, 1)
                    pe.matmul(bank[6][:, t], v, PM[:, t], start=True, stop=(c == 0))
                    mm = pe.matmul(bank[7][:, t], ones, PM[:, t], start=True, stop=(c == 0))
                    if c:
                        pe.wait_ge(m_cnd, 3 * h + c)
                        pe.matmul(bank[6][:, t], CN[:, c, 0:P], QS[:, t], start=False, stop=True)
                        mm = pe.matmul(bank[7][:, t], CN[:, c, P:2 * P], QS[:, t], start=False, stop=True)
                mm.then_inc(m_num, 1)
                between(2 * h + 1)
                pe.wait_ge(m_hq, h + 1)
                pe.matmul(bank[4][:], ones, T2[:], start=True, stop=True).then_inc(m_rms, 1)
            pe.wait_ge(c_hid, 3)
            for g in range(2):
                pe.matmul(bank[5][64 * g:64 * g + 64, 0:N_CMP], W2C[:, 0, :], HID[:, 0, g, :], start=True, stop=True)
                mm = pe.matmul(bank[5][0:N_CMP, 128 + 64 * g:192 + 64 * g], HID[:, 1, g, :], W2C[:, 1, :],
                               start=True, stop=True)
            mm.then_inc(c_out, 1)
            pe.wait_ge(s_hankel, 16)
            pe.wait_ge(m_y, 4)
            for h in range(8):
                if h >= 2:
                    pe.wait_ge(z_flipc, h - 1)
                pe.matmul(bank[6 + h % 2][:], mat(FLIP), HK[:, h, :], start=True, stop=True).then_inc(z_flip, 1)
            pe.wait_ge(z_flipc, 8)
            pe.wait_ge(c_outc, 1)
            attention(nsa_units, NF, Pn, a_o, KD, (2, 3, 4, 5))
            pe.wait_ge(a_o, KD + 4)
            pe.wait_ge(u_lo, 2)
            for i in range(4):
                for n in range(2):
                    gemm_split(f"merge{n}_{i}", lambda k: (U[0][:, k], U[1][:, k]))
                    pe.wait_ge(y_lo, n + 1)
                    gemm_split(f"branch{n}_{i}", lambda k, n=n: (Y[0][:, 4 * n + k], Y[1][:, 4 * n + k]))
            pair_wait(pe, "branch1_3")
            gemm_split("w_out", lambda k: (MIXED[0][:, k], MIXED[1][:, k]), then="ffn")
            norm("ffn")
            for kind, q in mlp_order(FFN_PARTS):
                if kind == "in":
                    for i in ffn_part[q]:
                        gemm_split(f"gate_{i}", h_of, normed("ffn") if i == 0 else None)
                        gemm_split(f"up_{i}", h_of)
                else:
                    pair_wait(pe, f"up_{ffn_part[q][-1]}")
                    gemm_split(f"down{q}", hidden_of(q), then="final" if q == FFN_PARTS - 1 else None)
            norm("final")
            pe.wait_ge(norm_out, OUT_BEFORE["final"])
            for t in range(NT):
                for half in range(2):
                    n = 2 * t + half
                    if n >= 2:
                        pe.wait_ge(fin_c, n - 1)
                    for k in range(4):
                        mm = pe.transpose(bank[6 + n % 2][:, k * P:(k + 1) * P],
                                          S1[:, 4 * half + k, t * P:(t + 1) * P], ident)
                    mm.then_inc(fin_t, 1)

        @block.scalar
        def _(act):
            count = [0]
            A = nc.scalar.activation

            def link(ins):
                count[0] += 1
                ins.then_inc(achain, 1)
                act.wait_ge(achain, count[0])

            def evac(name, op, pair=None):
                first, n = pairs[name]
                for i in range(n) if pair is None else (pair,):
                    j = first + i
                    act.wait_ge(chunk_done, ends[j])
                    for half in range(2):
                        ins = op(2 * i + half, bank[2 * (j % 2) + half][:])
                    ins.then_inc(evacuated[j % 2], 1)

            def norm_squares(name, k0, k1):
                n = NORMS.index(name)
                for k in range(k0, k1):
                    if X_AFTER[name]:
                        j = pairs[X_AFTER[name]][0] + k // 2
                        act.wait_ge(evacuated[j % 2], j // 2 + 1)
                    else:
                        act.wait_ge(pe_tc, k + 1)
                    if k >= 2:
                        act.wait_ge(norm_mm, 8 * n + k - 1)
                    A((T1, T2)[k % 2][:], S0[:, k, :], ACT.Square).then_inc(norm_sq, 1)

            def norm(name):
                n = NORMS.index(name)
                norm_squares(name, KD - 2 if X_AFTER[name] else 0, KD)
                act.wait_ge(norm_mm, 8 * (n + 1))
                A(rstd[:], bank[4][:], ACT.Sqrt, bias=eps6, scale=1.0 / D).then_inc(norm_root, 1)

            act.wait_ge(setup_done, 2)
            norm("rwkv")
            n1 = q = 0
            for i in range(3):
                for part in range(1 if i < 2 else 2):
                    act.wait_ge(lora1, n1 + 1)
                    if i == 2 and part == 0:
                        act.wait_ge(lora2, 2 * KD)
                    m = 64 if i < 2 else (128, 32)[part]
                    A(LH[0:m, i if i < 2 else part, :], bank[4 + n1 % 2][0:m, :],
                      (ACT.Tanh, ACT.Copy, ACT.Sigmoid)[i]).then_inc(lora1_out, 1)
                    n1 += 1
                for e in range(KD):
                    act.wait_ge(lora2, q + 1)
                    b = bank[6 + q % 2][:]
                    if i == 0:
                        ins = A(S4[:, e, :], b, ACT.Sigmoid, bias=par("rwkv_w0", e))
                    elif i == 1:
                        ins = A(S5[:, e, :], b, ACT.Sigmoid, bias=par("rwkv_a0", e))
                    else:
                        ins = A(S6[:, e, :], b, ACT.Copy)
                    ins.then_inc(lora2_out, 1)
                    q += 1
            evac("r", lambda e, b: A(S7[:, e, :], b, ACT.Copy))
            evac("k", lambda e, b: A(S8[:, e, :], b, ACT.Copy))
            evac("v", lambda e, b: A(S1[:, e, :], b, ACT.Copy))

            def aux_read(name, e):
                n = aux_n[name, e]
                act.wait_ge(aux_filled, n + 1)
                return bank[4 + n % 2][:], aux_evac[n % 2]

            def gap(g, S, F):
                if S is not None and g < 12:
                    c = g // 3
                    n = NT * S + c
                    if g % 3 == 0:
                        act.wait_ge(p_r, n + 1)
                        A(RT[:], bank[6][:, 0:P], ACT.Copy).then_inc(p_rc, 1)
                    if g % 3 == 1:
                        act.wait_ge(p_sa, n + 1)
                        if n:
                            act.wait_ge(p_y, n)
                        A(SA[:], bank[6][:, P:2 * P], ACT.Copy).then_inc(p_sac, 1)
                if F is not None:
                    if g == 0:
                        act.wait_ge(p_kk, F + 1)
                        A(T2[:], T1[:], ACT.Square).then_inc(p_sq, 1)
                    if g == 2:
                        b, done = aux_read("ssq", F)
                        A(T2[:], b, ACT.Sqrt, scale=float(HD)).then_inc(done, 1)
                    if g == 3:
                        act.wait_ge(p_c, F + 1)
                        A(S4[:, F, :], S4[:, F, :], ACT.Exp, scale=-DECAY_UNIT)
                        A(T4[:], T3[:], ACT.Exp, scale=-DECAY_UNIT)
                        link(A(CE[:, F], CE[:, F], ACT.Exp, scale=-DECAY_UNIT))
                        A(T3[:], T3[:], ACT.Exp, scale=DECAY_UNIT).then_inc(p_exp, 1)
                if S is not None:
                    if g == 12:
                        act.wait_ge(p_y, NT * (S + 1))
                        if S:
                            act.wait_ge(p_out, S)
                        A(T5, bank[7][:], ACT.Copy).then_inc(p_yc, 1)
                    if g == 14:
                        aux_wait(act, "mean", S)
                        A(T6, T5, ACT.Square).then_inc(p_cen2, 1)
                    if g == 15:
                        b, done = aux_read("var", S)
                        A(T6, b, ACT.Sqrt, bias=epsg).then_inc(done, 1)
                if F is not None:
                    if g == 16:
                        aux_wait(act, "bon", F)
                        for w, dst in enumerate((S7[:, F, :], KT[:, F % 2, :], S1[:, F, :])):
                            b, done = aux_read(f"t{w}", F)
                            A(dst, b, ACT.Copy).then_inc(done, 1)
                    if g == 17:
                        for hh in range(2):
                            act.wait_ge(p_it, 2 * F + hh + 1)
                            A(M0[:, 4 * hh:4 * hh + 4].rearrange("p u n -> p (u n)"), bank[hh][:], ACT.Copy
                              ).then_inc(p_ic, 1)

            for it in range(KD + 2):
                L, S, F = tiles_at(it)
                for lv in range(6):
                    for hh in range(2):
                        if L is None:
                            continue
                        n = 12 * L + 2 * lv + hh
                        act.wait_ge(p_x, n + 1)
                        if n >= 2:
                            act.wait_ge(p_d, n - 1)
                        A(XX[:, 4 * hh:4 * hh + 4].rearrange("p u n -> p (u n)"), bank[hh][:], ACT.Copy
                          ).then_inc(p_xc, 1)
                    gap(3 * lv, S, F)
                    gap(3 * lv + 1, S, F)
                    for hh in range(2):
                        if L is None or lv == 5:
                            continue
                        act.wait_ge(p_t, 10 * L + 2 * lv + hh + 1)
                        A(M1[:, 4 * hh:4 * hh + 4].rearrange("p u n -> p (u n)"), bank[hh][:], ACT.Copy
                          ).then_inc(p_tc, 1)
                    gap(3 * lv + 2, S, F)

            at = [0]

            def split_hi(upto, last):
                while at[0] <= min(upto, last):
                    ci = at[0]
                    g = chunk_of[ci]
                    nk = stream[g][2]
                    act.wait_ge(slot_loaded[g % SLOTS], landed[g])
                    if ci >= 2:
                        act.wait_ge(chunk_done, chunk_of[ci - 2] + 1)
                    A(weights_split(ci)[0][:, 0:nk], ring[:, g % SLOTS, 0:nk], ACT.Copy).then_inc(w_hi, 1)
                    at[0] += 1

            def norm_halves(name, outs=(HHI,)):
                for k in range(KD * len(outs)):
                    act.wait_ge(norm_h, SPLIT_BEFORE[name] + k + 1)
                    A(outs[k // KD][:, k % KD], (T1, T2, T3)[k % 3][:], ACT.Copy).then_inc(norm_hi, 1)

            hidden_pairs = [0]

            def mlp(i):
                if i == 0:
                    for half in range(1, 4):
                        norm_squares("mlp0", 2 * half - 2, 2 * half)
                norm(f"mlp{i}")
                first, last = split_range(f"mlp{i}_in0", f"mlp{i}_out{MLP_PARTS - 1}")
                split_hi(first + 1, last)
                norm_halves(f"mlp{i}")
                for kind, q in mlp_order(MLP_PARTS):
                    j0, n = pairs[f"mlp{i}_{kind}{q}"]
                    for j in range(j0, j0 + n):
                        split_hi(split[pair_chunks[j][0][0]] + 1, last)
                        if kind == "out" and q == MLP_PARTS - 1 and j > j0:
                            norm_squares(("kv", "mix")[i], 2 * (j - j0) - 2, 2 * (j - j0))
                        if kind == "in":
                            p = hidden_pairs[0]
                            act.wait_ge(chunk_done, ends[j])
                            if p:
                                act.wait_ge(hidden_lo, p)
                            for half in range(2):
                                ins = A((T1, T2)[half][:], bank[2 * (j % 2) + half][:], ACT.Relu)
                            ins.then_inc(evacuated[j % 2], 1)
                            hidden_pairs[0] += 1

            mlp(0)
            norm("kv")
            first, last = split_range("fk", "fq")
            split_hi(first + 1, last)
            norm_halves("kv", (KV_IN[0], Q_IN[0]))

            def head_square(n):
                if n >= 2:
                    act.wait_ge(h_mm, n - 1)
                A((T1, T2)[n % 2][:], S3[:, n, :] if n < KD else S1[:, n - KD, :], ACT.Square).then_inc(h_sq, 1)

            def head_root(n):
                act.wait_ge(h_mm, n + 1)
                if n >= 2:
                    act.wait_ge(h_out, n - 1)
                A((T3, T4)[n % 2][:], bank[4 + n % 2][:], ACT.Sqrt, bias=eps6 if n < KD else eps6q,
                  scale=1.0 if n < KD else 64.0).then_inc(h_rt, 1)

            for i in range(4):
                split_hi(first + i + 1, last)
                evac("fk", lambda e, b: A(S3[:, e, :], b, ACT.Copy), i)
            pair_wait(act, "fk")
            act.wait_ge(norm_out, OUT_BEFORE["kv"])
            for i in range(4):
                split_hi(first + 4 + i + 1, last)
                head_square(2 * i)
                head_square(2 * i + 1)
                j = pairs["fv"][0] + i
                act.wait_ge(chunk_done, ends[j])
                for half in range(2):
                    ins = A(FV[:, 2 * half:2 * half + 2, 256 * i:256 * i + 256],
                            bank[2 * (j % 2) + half][:].rearrange("p (t n) -> p t n", t=2), ACT.Copy)
                ins.then_inc(evacuated[j % 2], 1)
                head_root(2 * i)
                head_root(2 * i + 1)
            act.wait_ge(f_mm, 1)
            act.wait_ge(s_bias, 16)
            link(A(FLOGIT, bank[6][0:16, :], ACT.Identity, bias=fb))
            link(A(FPLUS, FLOGIT, ACT.Abs))
            link(A(FPLUS, FPLUS, ACT.Exp, scale=-1.0))
            A(FPLUS, FPLUS, ACT.Ln, bias=one1[0:16]).then_inc(f_rows, 1)
            for i in range(5):
                if i < 4:
                    split_hi(first + 8 + i + 1, last)
                    evac("fq", lambda e, b: A(S1[:, e, :], b, ACT.Copy), i)
                    j = pairs["fq"][0] + i
                    act.wait_ge(evacuated[j % 2], j // 2 + 1)
                    head_square(KD + 2 * i)
                    head_square(KD + 2 * i + 1)
                if i >= 1:
                    head_root(KD + 2 * i - 2)
                    head_root(KD + 2 * i - 1)

            def attention(units, base, Pt, o_base):
                N = len(units)
                fox = units[0]["mask"]
                for i in range(N + VALUE_LAG + 1):
                    if i < N:
                        u = units[i]
                        if u["rowbias"] is not None and i == 0:
                            act.wait_ge(a_cb, 1)
                            A(CB[:, 0, :], bank[2][:], ACT.Copy).then_inc(a_cbc, 1)
                        act.wait_ge(a_l, base + i + 1)
                        p = Pt[:, i % P_BUFS, 0:u["w"]]
                        A(p, p, ACT.Exp, bias=mx[:, i % 5:i % 5 + 1], accum_out=rs[:, i % 5:i % 5 + 1]
                          ).then_inc(a_e, 1)
                        if u["next_rowbias"] is not None:
                            h = u["next_rowbias"]
                            act.wait_ge(a_cb, h + 1)
                            A(CB[:, h % 2, :], bank[2][:], ACT.Copy).then_inc(a_cbc, 1)
                    if TURN_LAG <= i < N + TURN_LAG:
                        n = i - TURN_LAG
                        u = units[n]
                        act.wait_ge(a_t, base + n + 1)
                        if n >= 4:
                            act.wait_ge(a_pv, base + n - 3)
                        K = N_CMP if u["w"] == N_CMP else P
                        w = P if u["w"] == N_CMP else u["w"]
                        A(PTS[n % 4][0:K, 0:w], bank[6 + n % 2][0:K, 0:w], ACT.Copy).then_inc(a_tc, 1)
                    n = i - VALUE_LAG - 1
                    if n >= 0 and units[n]["ends_e"]:
                        e = units[n]["e"]
                        act.wait_ge(a_pv, base + n + 1)
                        dst = FOX_OUT[0][:, e] if fox else YN[:, e, :]
                        A(dst, bank[e % 2][:], ACT.Copy).then_inc(a_o, 1)
                    if not fox and i == N // 2 + 2:
                        split_hi(split_range("merge0_0", "merge0_0")[0], last_m)
                    if fox and i in (N, N + 1):
                        split_hi(split_range("fox_o", "fox_o")[0] + i - N, last_o)

            first_o, last_o = split_range("fox_o", "fox_o")
            attention(fox_units, 0, Pb, 0)
            for i in range(4):
                act.wait_ge(chunk_done, chunk_of[first_o + i] + 1)
                split_hi(first_o + i + 2, last_o)
                if i < 3:
                    norm_squares("mlp1", 2 * i, 2 * i + 2)
            mlp(1)
            norm("mix")
            act.wait_ge(s_small_w, 16 * 10)
            act.wait_ge(m_rows, 1)
            A(RI[0:4, :], bank[4][0:4, :], ACT.Identity, bias=small[0:4, 33:34])
            A(RMU[0:4, :], bank[4][32:36, :], ACT.Copy)
            A(GR[0:24, :], bank[4][64:88, :], ACT.Copy).then_inc(m_rowx, 1)
            act.wait_ge(m_rowx2, 1)
            link(A(T2[0:4, :], RMU[0:4, :], ACT.Abs))
            link(A(T2[0:4, :], T2[0:4, :], ACT.Exp, scale=-1.0))
            A(T2[0:4, :], T2[0:4, :], ACT.Ln, bias=one1[0:4])
            A(GR[0:24, :], GR[0:24, :], ACT.Sigmoid, bias=small[0:24, 36:37]).then_inc(m_rowx, 1)
            act.wait_ge(z_flip, 1)
            for i in range(2):
                A(ROW[:, i * 512:(i + 1) * 512], bank[6 + i][0:8, :], ACT.Copy).then_inc(z_rowc, 1)
            act.wait_ge(c_mm, 1)
            A(PET, bank[5][:, 0:32], ACT.Copy).then_inc(c_hid, 1)
            evac("mqk", lambda e, b: A(S2[:, e, :], b, ACT.Identity, bias=par("b_mqk", e)))
            act.wait_ge(c_mm, 2)
            link(A(PEH[:], bank[5][:, 128:130], ACT.Copy))
            act.wait_ge(m_rowd, 1)
            A(RSI, RSI, ACT.Exp)
            A(REM, REM, ACT.Exp, scale=-1.0).then_inc(m_rowx, 1)
            act.wait_ge(m_gt, 1)
            A(GC[:].rearrange("p c h -> p (c h)"), bank[4][:, 0:16], ACT.Copy)
            A(GT2[:].rearrange("p c h -> p (c h)"), bank[4][:, 32:128], ACT.Copy).then_inc(m_gtc, 1)
            for k in (4, 5, 6, 7, 0, 1, 2, 3):
                act.wait_ge(m_conv, k + 1)
                A(S3[:, k, :], S3[:, k, :], ACT.Silu).then_inc(m_silu, 1)

            def between(n):
                if n < 2:
                    evac("mo", lambda e, b: A(OG[:, e, :], b, ACT.Sigmoid, bias=par("b_mo", e)), n)
                elif n == 7:
                    act.wait_ge(c_mm, 3)
                    for j in range(2):
                        A(HID[:, j].rearrange("p g c -> p (g c)"), bank[2][:, 64 * j:64 * j + 2 * N_CMP], ACT.Silu,
                          bias=PEH[:, j:j + 1]).then_inc(c_hid, 1)

            for h in range(4):
                act.wait_ge(m_bd, h + 1)
                for c in range(NT):
                    t = slice(c * P, (c + 1) * P)
                    ins = A(T1[:, t], T1[:, t], ACT.Exp, scale=-1.0, bias=GC[:, c, h:h + 1])
                ins.then_inc(m_e, 1)
                act.wait_ge(m_em, h + 1)
                A(T3[:], bank[4][:], ACT.Copy).then_inc(m_emc, 1)
                between(2 * h)
                act.wait_ge(m_hq1, h + 1)
                A(T2[:], T1[:], ACT.Square).then_inc(m_hq, 1)
                between(2 * h + 1)
                act.wait_ge(m_rms, h + 1)
                A(T2[:], bank[4][:], ACT.Sqrt, bias=eps6, scale=1.0 / P).then_inc(m_rt, 1)
            act.wait_ge(c_out, 1)
            A(KC[:, 0:N_CMP], bank[5][:, 0:N_CMP], ACT.Copy)
            A(VC[0:N_CMP].rearrange("p g d -> p (g d)"), bank[5][0:N_CMP, 128:256], ACT.Copy).then_inc(c_outc, 1)
            first_m, last_m = split_range("merge0_0", "w_out")
            assert first_m % 2 == 0
            act.wait_ge(m_y, 4)
            A(U[0], S1, ACT.Copy).then_inc(u_hi, 1)
            attention(nsa_units, NF, Pn, KD)
            split_hi(first_m + 1, last_m)
            act.wait_ge(a_o, KD + 4)
            for n in range(2):
                A(Y[0][:, 4 * n:4 * n + 4], S6[:, 4 * n:4 * n + 4, :], ACT.Copy).then_inc(y_hi, 1)

            def sigs(name, func, bufs, bias, prev):
                first, n = pairs[name]
                if prev is not None:
                    pair_wait(act, prev)
                act.wait_ge(chunk_done, ends[first])
                for half in range(2):
                    b = bank[2 * (first % 2) + half][:]
                    if bias is None:
                        ins = A(bufs[half][:], b, func)
                    else:
                        ins = A(bufs[half][:], b, func, bias=bias[half])
                ins.then_inc(evacuated[first % 2], 1)

            for i in range(4):
                for n in range(2):
                    last_use = i - 1 if n else i - 2
                    prev = f"branch1_{last_use}" if last_use >= 0 else None
                    ci = first_m + 4 * i + 2 * n
                    split_hi(ci + 1, last_m)
                    split_hi(ci + 2, last_m)
                    sigs(f"merge{n}_{i}", ACT.Sigmoid, merge_gates(n, i),
                         [par("b_merge", 8 * n + 2 * i + half) for half in range(2)], prev)
            for i in range(1, 4):
                split_hi(last_m - 3 + i + 1, last_m)
                norm_squares("ffn", 2 * i - 2, 2 * i)
            norm("ffn")
            first, last = split_range("gate_0", f"down{FFN_PARTS - 1}")
            split_hi(first + 1, last)
            norm_halves("ffn")
            for kind, q in mlp_order(FFN_PARTS):
                if kind == "in":
                    for i in ffn_part[q]:
                        split_hi(split[pair_chunks[pairs[f"gate_{i}"][0]][0][0]] + 1, last)
                        sigs(f"gate_{i}", ACT.Silu, (T1, T2), None, f"up_{i - 1}" if i else None)
                        split_hi(split[pair_chunks[pairs[f"up_{i}"][0]][0][0]] + 1, last)
                else:
                    j0, n = pairs[f"down{q}"]
                    for j in range(j0, j0 + n):
                        split_hi(split[pair_chunks[j][0][0]] + 1, last)
                        if q == FFN_PARTS - 1 and j > j0:
                            norm_squares("final", 2 * (j - j0) - 2, 2 * (j - j0))
            norm("final")
            for n in range(2 * NT):
                act.wait_ge(fin_t, n + 1)
                A(S2[:, n, :], bank[6 + n % 2][:], ACT.Copy).then_inc(fin_c, 1)

        @block.vector
        def _(dve):
            V = nc.vector
            count = [0]

            def link(ins):
                count[0] += 1
                ins.then_inc(dchain, 1)
                dve.wait_ge(dchain, count[0])

            def mark(ins):
                count[0] += 1
                ins.then_inc(dchain, 1)
                return count[0]

            def evac(name, op, pair=None):
                first, n = pairs[name]
                for i in range(n) if pair is None else (pair,):
                    j = first + i
                    dve.wait_ge(chunk_done, ends[j])
                    for half in range(2):
                        ins = op(2 * i + half, bank[2 * (j % 2) + half][:])
                    ins.then_inc(evacuated[j % 2], 1)

            def residual(name):
                evac(name, lambda e, b: V.tensor_tensor(S0[:, e, :], b, S0[:, e, :], ALU.add))

            def norm(name, outs):
                n = NORMS.index(name)
                dve.wait_ge(norm_root, n + 1)
                link(V.reciprocal(rstd[:], rstd[:]))
                for dst, gain in outs:
                    for k in range(KD):
                        V.scalar_tensor_tensor(out=dst[:, k, :], in0=S0[:, k, :], scalar=gain(k), in1=rstd[:],
                                               op0=ALU.mult, op1=ALU.mult).then_inc(norm_out, 1)

            def norm_split(name, outs):
                n = NORMS.index(name)
                dve.wait_ge(norm_root, n + 1)
                link(V.reciprocal(rstd[:], rstd[:]))
                N = KD * len(outs)
                for k in range(N + 1):
                    if k < N:
                        if k >= 3:
                            dve.wait_ge(norm_out, OUT_BEFORE[name] - N + k - 2)
                        V.scalar_tensor_tensor(out=(T1, T2, T3)[k % 3][:], in0=S0[:, k % KD, :],
                                               scalar=outs[k // KD][2](k % KD),
                                               in1=rstd[:], op0=ALU.mult, op1=ALU.mult).then_inc(norm_h, 1)
                    if k:
                        hi, lo, _ = outs[(k - 1) // KD]
                        at = (k - 1) % KD
                        dve.wait_ge(norm_hi, SPLIT_BEFORE[name] + k)
                        V.tensor_tensor(lo[:, at], (T1, T2, T3)[(k - 1) % 3][:], hi[:, at].bitcast(F32),
                                        ALU.subtract).then_inc(norm_out, 1)

            def rounded(dst_hi, dst_lo, q):
                link(V.tensor_copy(dst_hi, q))
                return V.tensor_tensor(dst_lo, q, dst_hi.bitcast(F32), ALU.subtract)

            def mlp(i):
                norm_split(f"mlp{i}", [(HHI, HLO, lambda k: par("mlp_norm_g", 8 * i + k))])
                for kind, q in mlp_order(MLP_PARTS):
                    if kind == "out":
                        residual(f"mlp{i}_out{q}")
                        continue
                    j0, n = pairs[f"mlp{i}_in{q}"]
                    for j in range(j0, j0 + n):
                        dve.wait_ge(evacuated[j % 2], j // 2 + 1)
                        for half in range(2):
                            t = 2 * (j - j0) + half
                            link(V.tensor_tensor((T3, T4)[half][:], (T1, T2)[half][:], (T1, T2)[half][:], ALU.mult))
                            ins = rounded(HID_HI[q % 2][:, t], HID_LO[q % 2][:, t], (T3, T4)[half][:])
                        ins.then_inc(hidden_lo, 1)
                        dve.wait_ge(hidden_lo, 4 * (MLP_PARTS * i + q) + j - j0 + 1)

            V.memset(S4[:, 0:3, 0:P], 0.0).then_inc(setup_done, 1)
            V.memset(eps6, EPS)
            V.memset(eps6q, EPS * 64)
            V.memset(epsg, GN_EPS)
            V.memset(one1, 1.0).then_inc(setup_done, 1)
            for k in range(KD):
                dve.wait_ge(pe_t, k + 1)
                V.tensor_copy(S0[:, k, :], bank[4 + k % 2][:]).then_inc(pe_tc, 1)
            dve.wait_ge(pe_t, KD + 1)
            link(V.tensor_copy(PK[:], bank[6][:, 0:3 * P]))
            r0 = rows["rwkv_k_a"][0]
            V.tensor_scalar(omka, PK[:, r0:r0 + 8], -1.0, 1.0, ALU.mult, ALU.add)
            dve.wait_ge(norm_root, 1)
            link(V.reciprocal(rstd[:], rstd[:]))
            for k in range(KD):
                V.scalar_tensor_tensor(out=S1[:, k, :], in0=S0[:, k, :], scalar=par("rwkv_norm_g", k), in1=rstd[:],
                                       op0=ALU.mult, op1=ALU.mult).then_inc(norm_out, 1)
                dve.wait_ge(norm_out, k + 1)
                V.tensor_scalar(S2[:, k, 0:1], S1[:, k, 0:1], -1.0, None, ALU.mult)
                link(V.tensor_tensor(S2[:, k, 1:T], S1[:, k, 0:T - 1], S1[:, k, 1:T], ALU.subtract))
                V.scalar_tensor_tensor(out=S3[:, k, :], in0=S2[:, k, :], scalar=par("rwkv_mu", 8 + k),
                                       in1=S1[:, k, :], op0=ALU.mult, op1=ALU.add).then_inc(mix_ready, 1)
            for n, m in enumerate((4, 5, 0, 2, 3), 1):
                if n <= 3:
                    dve.wait_ge(lora1, (1, 2, 4)[n - 1])
                elif n == 4:
                    dve.wait_ge(lora2, 3 * KD)
                else:
                    dve.wait_ge(chunk_done, ends[sum(pairs["r"]) - 1])
                for k in range(KD):
                    V.scalar_tensor_tensor(out=KMIX[k] if n == 4 else S3[:, k, :], in0=S2[:, k, :],
                                           scalar=par("rwkv_mu", 8 * m + k), in1=S1[:, k, :],
                                           op0=ALU.mult, op1=ALU.add).then_inc(mix_ready, 1)
            pair_wait(dve, "v")
            dve.wait_ge(s_const2, 16)

            V.memset(SS[:], 0.0)

            def bc(ap, n):
                return ap.unsqueeze(2).broadcast_to([P, NT, n])

            def aux_read(name, e):
                n = aux_n[name, e]
                dve.wait_ge(aux_filled, n + 1)
                return bank[4 + n % 2][:], aux_evac[n % 2]

            def masked(w, b, e):
                src, done = aux_read(("b", "k")[w] + str(b), e)
                V.tensor_tensor(PROD[:, e % 2, 2 * w:2 * w + 2, 2 * b:2 * b + 2, :].rearrange("p w u n -> p u w n"),
                                src.rearrange("p (u w n) -> p u w n", u=2, w=2),
                                cmat[:, AFTER:AFTER + 2, :].unsqueeze(1).broadcast_to([P, 2, 2, P]), ALU.mult
                                ).then_inc(done, 1)

            def gap(g, S, F):
                if S is not None and g < 12 and g % 3 == 2 and g // 3 < NT - 1:
                    c = g // 3
                    dve.wait_ge(p_st, 3 * S + c + 1)
                    dve.wait_ge(p_y, NT * S + c + 1)
                    for hh in range(2):
                        s = slice(64 * hh, 64 * hh + 64)
                        if c == 0:
                            ins = V.tensor_scalar(SS[s, s], bank[6][s, 2 * P + 64 * hh:2 * P + 64 * hh + 64],
                                                  CE[s, S, 0:1], None, ALU.mult)
                        else:
                            ins = V.tensor_tensor(SS[s, s], bank[6][s, 2 * P + 64 * hh:2 * P + 64 * hh + 64],
                                                  SS[s, s], ALU.add)
                    if c:
                        link(ins)
                        ins = V.tensor_scalar(SS[:], SS[:], CE[:, S, c:c + 1], None, ALU.mult)
                    ins.then_inc(p_stc, 1)
                if F is not None:
                    if g == 0:
                        if F:
                            dve.wait_ge(p_fm, F)
                        V.tensor_scalar(T1[:], S8[:, F, :], par("rwkv_k_k", F), None, ALU.mult).then_inc(p_kk, 1)
                        for c in range(NT):
                            t = slice(c * P, (c + 1) * P)
                            ins = V.tensor_tensor_scan(T3[:, t], ones, S4[:, F, t], 0.0, ALU.mult, ALU.add)
                        link(ins)
                    if g == 1:
                        V.tensor_copy(cmid, c4(T3[:])[:, :, P // 2 - 1])
                        link(V.tensor_copy(cend, c4(T3[:])[:, :, P - 1]))
                        link(V.tensor_tensor(c4(T3[:]), c4(T3[:]), bc(cmid, P), ALU.subtract))
                        V.tensor_tensor(S4[:, F, :], T3[:], S4[:, F, :], ALU.subtract)
                        link(V.tensor_tensor(CE[:, F], cend, cmid, ALU.subtract))
                        V.tensor_tensor(CE[:, F, 0:3], CE[:, F, 0:3], cmid[:, 1:4], ALU.add).then_inc(p_c, 1)
                    if g == 3:
                        aux_wait(dve, "ssq", F)
                        link(V.tensor_scalar(T2[:], T2[:], 1e-12, None, ALU.max))
                        link(V.reciprocal(T2[:], T2[:]))
                    if g == 4:
                        link(V.tensor_tensor(T1[:], T1[:], T2[:], ALU.mult))
                        V.tensor_scalar(T2[:], S5[:, F, :], par("rwkv_k_a", F), omka[:, F:F + 1], ALU.mult, ALU.add)
                    if g == 5:
                        dve.wait_ge(p_exp, F + 1)
                        link(V.scalar_tensor_tensor(out=S4[:, F, :], in0=T1[:], scalar=-1.0, in1=S4[:, F, :],
                                                    op0=ALU.mult, op1=ALU.mult))
                        link(V.tensor_tensor(S8[:, F, :], S8[:, F, :], T2[:], ALU.mult))
                    if g == 6:
                        V.scalar_tensor_tensor(out=T2[:], in0=S7[:, F, :], scalar=par("rwkv_r_k", F),
                                               in1=S8[:, F, :], op0=ALU.mult, op1=ALU.mult)
                        link(V.tensor_tensor(T1[:], T1[:], S5[:, F, :], ALU.mult))
                    if g == 7:
                        if F:
                            dve.wait_ge(aux_filled, aux_n["t1", F - 1] + 1)
                        link(V.tensor_tensor(BK[:, 1, :], S8[:, F, :], T3[:], ALU.mult))
                        V.tensor_tensor(BK[:, 0, :], T1[:], T3[:], ALU.mult)
                    if g == 8:
                        V.tensor_tensor(S8[:, F, :], S7[:, F, :], T4[:], ALU.mult).then_inc(p_fm, 1)
                    if g == 12:
                        b, done = aux_read("bon", F)
                        V.scalar_tensor_tensor(out=S5[:, F, :], in0=b, scalar=float(HD), in1=S1[:, F, :],
                                               op0=ALU.mult, op1=ALU.mult).then_inc(done, 1)
                        if S is not None:
                            dve.wait_ge(p_y, NT * (S + 1))
                    if 12 <= g < 16:
                        for b in (0, 1):
                            masked((g - 12) // 2, 2 * (g % 2) + b, F)
                if S is not None:
                    if g == 13:
                        b, done = aux_read("mean", S)
                        V.tensor_tensor(T5, T5, b, ALU.subtract).then_inc(done, 1)
                    if g == 17:
                        aux_wait(dve, "var", S)
                        link(V.reciprocal(T6, T6))
                        link(V.tensor_tensor(T5, T5, T6, ALU.mult))
                        link(V.tensor_scalar(T5, T5, par("rwkv_lnx_w", S), par("rwkv_lnx_b", S), ALU.mult, ALU.add))
                        link(V.tensor_tensor(T5, T5, S5[:, S, :], ALU.add))
                        V.tensor_tensor(S7[:, S, :], T5, S6[:, S, :], ALU.mult).then_inc(p_out, 1)

            for it in range(KD + 2):
                L, S, F = tiles_at(it)
                for lv in range(6):
                    gap(3 * lv, S, F)
                    for hh in range(2):
                        if L is None:
                            continue
                        n = 12 * L + 2 * lv + hh
                        dve.wait_ge(p_d, n + 1)
                        u4 = slice(4 * hh, 4 * hh + 4)
                        if lv < 5:
                            V.tensor_tensor(M0[:, u4], c4(bank[2 + hh][:]), M0[:, u4], ALU.add).then_inc(p_dc, 1)
                        else:
                            if hh == 0 and S is not None:
                                dve.wait_ge(p_y, NT * (S + 1))
                            V.tensor_tensor(MTF[:, u4], c4(bank[2 + hh][:]), M1[:, u4], ALU.add).then_inc(p_dc, 1)
                    gap(3 * lv + 1, S, F)
                    gap(3 * lv + 2, S, F)
            residual("rwkv_o")
            mlp(0)
            norm_split("kv", [(*KV_IN, lambda k: par("kv_norm_g", k)), (*Q_IN, lambda k: par("attn_norm_g", k))])
            dve.wait_ge(s_ffw, 16)
            V.tensor_copy(WFF_HI, wff).then_inc(f_w, 1)
            dve.wait_ge(f_w, 1)
            V.tensor_tensor(WFF_LO, wff, WFF_HI.bitcast(F32), ALU.subtract).then_inc(f_w, 1)
            for n in range(2 * KD):
                if n == KD:
                    dve.wait_ge(f_rows, 1)
                    link(V.tensor_scalar(FLOGIT, FLOGIT, 0.0, None, ALU.min))
                    link(V.tensor_tensor(FPLUS, FPLUS, FLOGIT, ALU.subtract))
                    link(V.memset(FONES, 1.0))
                    V.tensor_tensor_scan(NC, FONES, FPLUS, 0.0, ALU.mult, ALU.add).then_inc(f_cum, 1)
                e = n % KD
                r = (T3, T4)[n % 2][:]
                dve.wait_ge(h_rt, n + 1)
                link(V.reciprocal(r, r))
                if n < KD:
                    ins = V.scalar_tensor_tensor(out=S3[:, e, :], in0=S3[:, e, :], scalar=par("k_norm_g", e), in1=r,
                                                 op0=ALU.mult, op1=ALU.mult)
                else:
                    for hh in range(2):
                        s = slice(64 * hh, 64 * hh + 64)
                        ins = V.scalar_tensor_tensor(out=QZ[hh][s, e, :], in0=S1[s, e, :],
                                                     scalar=par("q_norm_g", e)[s], in1=r[s],
                                                     op0=ALU.mult, op1=ALU.mult)
                ins.then_inc(h_out, 1)

            def attention(units, base, Pt, s_banks):
                N, NS = len(units), len(s_banks)
                fox = units[0]["mask"]
                for i in range(N + VALUE_LAG + 3):
                    if i < N:
                        u = units[i]
                        if u["rowbias"] is not None:
                            dve.wait_ge(a_cbc, u["rowbias"] + 1)
                        dve.wait_ge(a_s, base + i + 1)
                        if i >= P_BUFS:
                            dve.wait_ge(a_t, base + i - P_BUFS + 1)
                        p = Pt[:, i % P_BUFS, 0:u["w"]]
                        m = mx[:, i % 5:i % 5 + 1]
                        scored = mark(V.tensor_tensor_reduce(p, bank[s_banks[i % NS]][:, 0:u["w"]], u["bias"],
                                                             1.0, -3e38, ALU.add, ALU.max, m))
                    if 1 <= i <= N:
                        last = units[i - 1]
                        r = rs[:, (i - 1) % 5:(i - 1) % 5 + 1]
                        dve.wait_ge(a_e, base + i)
                        if last["clamp"]:
                            summed = mark(V.tensor_scalar(r, r, 1e-30, None, ALU.max))
                        else:
                            summed = mark(V.reciprocal(r, r))
                    if i < N:
                        dve.wait_ge(dchain, scored)
                        V.tensor_scalar(m, m, -1e20, -1.0, ALU.max, ALU.mult).then_inc(a_l, 1)
                    if 1 <= i <= N:
                        dve.wait_ge(dchain, summed)
                        if last["clamp"]:
                            link(V.reciprocal(r, r))
                        p = Pt[:, (i - 1) % P_BUFS, 0:last["w"]]
                        if last["gate"] is None:
                            V.tensor_scalar(p, p, r, None, ALU.mult).then_inc(a_p, 1)
                        else:
                            V.tensor_scalar(p, p, r, last["gate"], ALU.mult, ALU.mult).then_inc(a_p, 1)
                    n = i - VALUE_LAG - 3
                    if fox and n >= 0 and units[n]["ends_e"]:
                        e = units[n]["e"]
                        dve.wait_ge(a_o, e + 1)
                        V.tensor_tensor(FOX_OUT[1][:, e], bank[e % 2][:], FOX_OUT[0][:, e].bitcast(F32),
                                        ALU.subtract).then_inc(a_olo, 1)

            attention(fox_units, 0, Pb, (3, 4, 5))
            residual("fox_o")
            mlp(1)
            V.memset(TB[32:33, :], NEG)
            V.memset(WSM, 0.0).then_inc(s_wz, 1)
            norm("mix", [(S1, lambda k: par("g_norm_mix_2", k))])
            dve.wait_ge(s_small_w, 16 * 10)

            def evac_tm(name, dst, bias):
                first, n = pairs[name]
                for i in range(n):
                    j = first + i
                    dve.wait_ge(chunk_done, ends[j])
                    for half in range(2):
                        ins = V.tensor_tensor(dst[:, 2 * half:2 * half + 2, 256 * i:256 * i + 256],
                                              bank[2 * (j % 2) + half][:].rearrange("p (t n) -> p t n", t=2),
                                              bias[:, 256 * i:256 * i + 256].unsqueeze(1).broadcast_to([P, 2, 256]),
                                              ALU.add)
                    ins.then_inc(evacuated[j % 2], 1)

            dve.wait_ge(m_rowx, 1)
            V.tensor_scalar(RMU, RMU, small[0:4, 34:35], small[0:4, 35:36], ALU.add, ALU.add).then_inc(m_rowx2, 1)
            dve.wait_ge(m_rowx, 2)
            link(V.tensor_scalar(RMU, RMU, 0.0, None, ALU.min))
            link(V.tensor_tensor(RMU, RMU, T2[0:4, :], ALU.subtract))
            for c in range(NT):
                t = slice(c * P, (c + 1) * P)
                ins = V.tensor_tensor_scan(REM[:, t], ones[0:4, :], RMU[:, t], 0.0, ALU.mult, ALU.add)
            link(ins)
            link(V.tensor_tensor(RG, RI, REM, ALU.subtract))
            link(V.memset(small[0:4, 40:41], 0.0))
            for c in range(NT):
                t = slice(c * P, (c + 1) * P)
                mp = small[0:4, 40 + c:41 + c]
                link(V.tensor_tensor_scan(RMU[:, t], RG[:, t], RG[:, t], mp, ALU.max, ALU.max))
                V.tensor_scalar(RSI[:, t], RMU[:, t], mp, -1.0, ALU.subtract, ALU.mult)
                ins = V.tensor_tensor(REM[:, t], REM[:, t], RMU[:, t], ALU.add)
                if c < NT - 1:
                    link(ins)
                    link(V.tensor_copy(small[0:4, 41 + c:42 + c], REM[:, (c + 1) * P - 1:(c + 1) * P]))
            ins.then_inc(m_rowd, 1)
            first, n = pairs["mqk"]
            for k in range(8):
                j = first + k // 2
                dve.wait_ge(evacuated[j % 2], j // 2 + 1)
                link(V.tensor_scalar(S3[:, k, :], S2[:, k, :], par("conv_qk_2", 24 + k), None, ALU.mult))
                for j in (2, 1, 0):
                    d = 3 - j
                    ins = V.scalar_tensor_tensor(out=S3[:, k, d:T], in0=S2[:, k, 0:T - d],
                                                 scalar=par("conv_qk_2", 8 * j + k), in1=S3[:, k, d:T],
                                                 op0=ALU.mult, op1=ALU.add)
                    if j:
                        link(ins)
                ins.then_inc(m_conv, 1)
            evac_tm("mv", MVT, BMV[:])
            for k in range(4, 8):
                dve.wait_ge(m_silu, k - 3)
                ins = V.tensor_scalar(S3[:, k, :], S3[:, k, :], P ** -0.5, None, ALU.mult)
            ins.then_inc(m_kscaled, 1)
            dve.wait_ge(m_kscaled, 1)

            def between(n):
                if 2 <= n < len(BETWEEN):
                    name, i = BETWEEN[n]
                    if name == "nq":
                        evac("nq", lambda e, b: V.tensor_scalar(NQT[:, e, :], b, par("b_nq", e), HD ** -0.5,
                                                                ALU.add, ALU.mult), i)
                    elif name == "vsw":
                        evac_tm("vsw", VSW, BVS)
                    elif name == "kvc":
                        evac("kvc", lambda e, b: V.tensor_scalar(KVC[:, e, :], b, par("b_nkv", e), None, ALU.add))
                    else:
                        evac("ksw", lambda e, b: V.tensor_scalar((KS, KW)[e], b, par("b_nkv", 2 + 2 * e), None,
                                                                 ALU.add))

            for h in range(4):
                dve.wait_ge(m_b, h + 1)
                V.tensor_tensor(c4(T1[:]), c4(bank[4][:]), mat(LATE_POS).unsqueeze(1).broadcast_to([P, 4, P]),
                                ALU.add).then_inc(m_bd, 1)
                V.tensor_tensor(QS[:], S3[:, h, :], bank[6][:], ALU.mult)
                V.tensor_copy(DC[:], c4(bank[6][:])[:, :, P - 1])
                dve.wait_ge(m_e, h + 1)
                dve.wait_ge(m_kt, h + 1)
                V.tensor_tensor(PM[:], T1[:], bank[5][:], ALU.mult)
                for c in range(NT):
                    t = slice(c * P, (c + 1) * P)
                    ins = V.tensor_scalar(KWT[:, t], bank[7][:, t], T1[:, (c + 1) * P - 1:(c + 1) * P], None, ALU.mult)
                ins.then_inc(m_pd, 1)
                for c in range(NT - 1):
                    dve.wait_ge(m_cn, 3 * h + c + 1)
                    if c == 0:
                        ins = V.tensor_copy(CN[:, 1, :], bank[5][:, 0:256])
                    else:
                        ins = V.scalar_tensor_tensor(out=CN[:, c + 1, :], in0=CN[:, c, :], scalar=DC[:, c:c + 1],
                                                     in1=bank[5 - c % 2][:, 0:256], op0=ALU.mult, op1=ALU.add)
                    ins.then_inc(m_cnd, 1)
                    dve.wait_ge(m_cnd, 3 * h + c + 1)
                between(2 * h)
                dve.wait_ge(m_num, h + 1)
                dve.wait_ge(m_emc, h + 1)
                link(V.scalar_tensor_tensor(out=T3[:], in0=bank[7][:], scalar=-1.0, in1=T3[:],
                                            op0=ALU.mult, op1=ALU.max))
                link(V.tensor_tensor(T3[:], bank[7][:], T3[:], ALU.max))
                link(V.reciprocal(T3[:], T3[:]))
                V.tensor_tensor(T1[:], bank[6][:], T3[:], ALU.mult).then_inc(m_hq1, 1)
                between(2 * h + 1)
                dve.wait_ge(m_rt, h + 1)
                link(V.reciprocal(T2[:], T2[:]))
                link(V.tensor_tensor(T1[:], T1[:], T2[:], ALU.mult))
                V.scalar_tensor_tensor(out=YM[:, h, :], in0=T1[:], scalar=par("g_mlstm_head_2", h), in1=OG[:, h, :],
                                       op0=ALU.mult, op1=ALU.mult).then_inc(m_y, 1)
            for h in range(8):
                dve.wait_ge(z_flip, h + 2)
                V.memset(Z[h][:, 512:896], NEG)
                V.tensor_copy(Z[h][:, 0:512], bank[6 + h % 2][:]).then_inc(z_flipc, 1)
            dve.wait_ge(m_gtc, 1)
            attention(nsa_units, NF, Pn, (2, 3, 4, 5))
            for n in range(2):
                dve.wait_ge(y_hi, n + 1)
                V.tensor_tensor(Y[1][:, 4 * n:4 * n + 4], S6[:, 4 * n:4 * n + 4, :],
                                Y[0][:, 4 * n:4 * n + 4].bitcast(F32), ALU.subtract).then_inc(y_lo, 1)
            for i in range(4):
                for n in range(2):
                    if 2 * i + n < 7:
                        ci = split_range("merge0_0", "merge0_0")[0] + 4 * i + 2 * n + 2
                        hi, lo = weights_split(ci)
                        dve.wait_ge(w_hi, ci + 1)
                        dve.wait_ge(w_lo, ci)
                        V.tensor_tensor(lo, ring[:, chunk_of[ci] % SLOTS], hi.bitcast(F32), ALU.subtract
                                        ).then_inc(w_lo, 1)
                    gates, first_gates = merge_gates(n, i), merge_gates(0, i)
                    pair_wait(dve, f"merge{n}_{i}")
                    j = pairs[f"branch{n}_{i}"][0]
                    dve.wait_ge(chunk_done, ends[j])
                    for half in range(2):
                        b = bank[2 * (j % 2) + half][:]
                        q = gates[half][:]
                        ins = V.tensor_tensor(q, b, q, ALU.mult)
                        if n == 1:
                            link(ins)
                            link(V.tensor_tensor(q, q, first_gates[half][:], ALU.add))
                            ins = rounded(MIXED[0][:, 2 * i + half], MIXED[1][:, 2 * i + half], q)
                    ins.then_inc(evacuated[j % 2], 1)
            residual("w_out")
            norm_split("ffn", [(HHI, HLO, lambda k: par("g_norm_ffn_2", k))])
            for kind, q in mlp_order(FFN_PARTS):
                if kind == "out":
                    residual(f"down{q}")
                    continue
                for i in ffn_part[q]:
                    pair_wait(dve, f"gate_{i}")
                    j = pairs[f"up_{i}"][0]
                    dve.wait_ge(chunk_done, ends[j])
                    for half in range(2):
                        t = 2 * (i - ffn_part[q][0]) + half
                        link(V.tensor_tensor((T3, T4)[half][:], bank[2 * (j % 2) + half][:], (T1, T2)[half][:],
                                             ALU.mult))
                        ins = rounded(HID_HI[q % 2][:, t], HID_LO[q % 2][:, t], (T3, T4)[half][:])
                    ins.then_inc(evacuated[j % 2], 1)
                    dve.wait_ge(evacuated[j % 2], j // 2 + 1)
            norm("final", [(S1, lambda k: par("g_final_2", k))])


NAMES = ["x", "rwkv_norm_g", "rwkv_mu", "rwkv_w_rkv", "rwkv_w0", "rwkv_w1", "rwkv_w2", "rwkv_a0", "rwkv_a1",
         "rwkv_a2", "rwkv_g1", "rwkv_g2", "rwkv_k_k", "rwkv_k_a", "rwkv_r_k", "rwkv_lnx_w", "rwkv_lnx_b",
         "rwkv_w_o", "kv_norm_g", "kv_w", "kv_f_bias", "k_norm_g", "attn_norm_g", "attn_w_q", "q_norm_g",
         "attn_w_o", "mlp_norm_g", "mlp_w_in", "mlp_w_out", "g_norm_mix_2", "w_in_2", "b_in_2", "b_fgate_2",
         "conv_qk_2", "g_mlstm_head_2", "pe_cmp_2", "w_cmp1_2", "w_cmp2_2", "rel_bias_2", "w_branch_2",
         "w_out_2", "g_norm_ffn_2", "w_gate_2", "w_up_2", "w_down_2", "g_final_2"]


def kernel(**inputs):
    import concourse.bacc as bacc
    from concourse.bass_utils import run_bass_kernel_spmd

    nc = bacc.Bacc("TRN2", target_bir_lowering=False, num_devices=1)
    arrays, aps = {}, {}
    given = {n: np.ascontiguousarray(inputs[n]) for n in NAMES}
    given.update(constants())
    for name, v in given.items():
        arrays[f"in_{name}"] = v
        aps[name] = nc.dram_tensor(f"in_{name}", v.shape, mybir.dt.from_np(v.dtype), kind="ExternalInput").ap()
    out = nc.dram_tensor("out_0", (1, T, D), F32, kind="ExternalOutput").ap()
    scratch = nc.dram_tensor("rel_scratch", (8, 1024), F32, kind="Internal").ap()
    build(nc, aps, out, scratch)
    r = run_bass_kernel_spmd(nc, [arrays], core_ids=[0])
    return r.results[0]["out_0"]
```
